# Optimizing a Trainium2 kernel written in Bass

```python
import jax, jax.numpy as jnp
from jax import lax
import numpy as np

D_MODEL = 1024
BATCH = 1
SEQ = 1024
DEPTH = 1

GRID_W = 64
D_CONV = 512
CONV_WIDTH = 31
N_HEADS = 8
HEAD_DIM = 64
D_ATTN = N_HEADS * HEAD_DIM
WIN_H_MAX = 8
WIN_W = 16
N_EXPERTS = 64
TOP_K = 8
N_GROUPS = 8
TOPK_GROUPS = 4
D_EXPERT = 256
D_SHARED = 256
ROUTE_SCALE = 2.5
DISPATCH_BLOCK = 128
EPS = 1e-6
SPLITS = (D_CONV, 2 * D_CONV, 2 * D_CONV + D_ATTN, 2 * D_CONV + 2 * D_ATTN,
          2 * D_CONV + 3 * D_ATTN, 2 * D_CONV + 3 * D_ATTN + D_MODEL)
D_IN = 2 * D_CONV + 3 * D_ATTN + 2 * D_MODEL

kernel_name = 'hybrid_conformer_natten_moe_block'

def rms_norm(x, g):
    xf = x.astype(jnp.float32)
    y = xf * lax.rsqrt(jnp.mean(xf * xf, axis=-1, keepdims=True) + EPS)
    return (y * g.astype(jnp.float32)).astype(x.dtype)

def layer_norm(x, g, b):
    xf = x.astype(jnp.float32)
    mu = jnp.mean(xf, axis=-1, keepdims=True)
    var = jnp.mean(jnp.square(xf - mu), axis=-1, keepdims=True)
    y = (xf - mu) * lax.rsqrt(var + EPS)
    return (y * g.astype(jnp.float32) + b.astype(jnp.float32)).astype(x.dtype)

def conformer_conv(a, gate, w_dw, b_dw, ln_g, ln_b, w_pw):
    u = a * jax.nn.sigmoid(gate)
    pad = CONV_WIDTH // 2
    u = lax.conv_general_dilated(
        u, w_dw.astype(u.dtype), window_strides=(1,), padding=[(pad, pad)],
        dimension_numbers=('NWC', 'WIO', 'NWC'), feature_group_count=D_CONV) + b_dw
    u = jax.nn.silu(layer_norm(u, ln_g, ln_b))
    return u @ w_pw

def neighbourhood_attention(q, k, v, rpb):
    b, s = q.shape[0], q.shape[1]
    rows = s // GRID_W
    win_h = min(WIN_H_MAX, rows)
    grid = (b, rows, GRID_W, N_HEADS, HEAD_DIM)
    q, k, v = q.reshape(grid), k.reshape(grid), v.reshape(grid)
    cols = jnp.arange(GRID_W)
    col_start = jnp.clip(cols - WIN_W // 2, 0, GRID_W - WIN_W)
    col_idx = col_start[:, None] + jnp.arange(WIN_W)
    col_bias_idx = col_idx - cols[:, None] + (WIN_W - 1)
    scale = HEAD_DIM ** -0.5

    def one_row(r):
        rs = jnp.clip(r - win_h // 2, 0, rows - win_h)
        q_r = lax.dynamic_index_in_dim(q, r, axis=1, keepdims=False)
        k_slab = lax.dynamic_slice_in_dim(k, rs, win_h, axis=1)
        v_slab = lax.dynamic_slice_in_dim(v, rs, win_h, axis=1)
        k_win = k_slab[:, :, col_idx]
        v_win = v_slab[:, :, col_idx]
        row_bias_idx = rs + jnp.arange(win_h) - r + (WIN_H_MAX - 1)
        bias = rpb[:, row_bias_idx[None, :, None], col_bias_idx[:, None, :]]
        sc = jnp.einsum('bqhd,biqjhd->bhqij', q_r, k_win).astype(jnp.float32) * scale
        sc = sc + bias.astype(jnp.float32)[None]
        p = jax.nn.softmax(sc.reshape(b, N_HEADS, GRID_W, win_h * WIN_W), axis=-1)
        p = p.reshape(b, N_HEADS, GRID_W, win_h, WIN_W).astype(v.dtype)
        return jnp.einsum('bhqij,biqjhd->bqhd', p, v_win)

    out = lax.map(one_row, jnp.arange(rows))
    return out.transpose(1, 0, 2, 3, 4).reshape(b, s, D_ATTN)

def moe_ffn(h, w_router, router_bias, w_gate, w_up, w_down, w_sh_gate, w_sh_up, w_sh_down):
    b, s, d = h.shape
    n = b * s
    hf = h.reshape(n, d)
    scores = jax.nn.sigmoid((hf @ w_router).astype(jnp.float32))
    biased = scores + router_bias.astype(jnp.float32)
    per_group = N_EXPERTS // N_GROUPS
    grp_score = lax.top_k(biased.reshape(n, N_GROUPS, per_group), 2)[0].sum(-1)
    _, grp_idx = lax.top_k(grp_score, TOPK_GROUPS)
    grp_mask = jnp.any(grp_idx[..., None] == jnp.arange(N_GROUPS), axis=1)
    masked = jnp.where(jnp.repeat(grp_mask, per_group, axis=1), biased, -jnp.inf)
    _, idx = lax.top_k(masked, TOP_K)
    wts = jnp.take_along_axis(scores, idx, axis=1)
    wts = wts / jnp.sum(wts, axis=-1, keepdims=True) * ROUTE_SCALE
    nk = n * TOP_K
    n_blocks = (nk + N_EXPERTS * (DISPATCH_BLOCK - 1) + DISPATCH_BLOCK - 1) // DISPATCH_BLOCK
    flat_e = idx.reshape(nk)
    order = jnp.argsort(flat_e)
    sorted_e = flat_e[order]
    counts = jnp.bincount(flat_e, length=N_EXPERTS)
    padded = (counts + DISPATCH_BLOCK - 1) // DISPATCH_BLOCK * DISPATCH_BLOCK
    start = jnp.cumsum(counts) - counts
    pad_end = jnp.cumsum(padded)
    pad_start = pad_end - padded
    dest = pad_start[sorted_e] + jnp.arange(nk) - start[sorted_e]
    n_slots = n_blocks * DISPATCH_BLOCK
    slot_tok = jnp.full((n_slots,), n, jnp.int32).at[dest].set((order // TOP_K).astype(jnp.int32))
    slot_w = jnp.zeros((n_slots,), jnp.float32).at[dest].set(wts.reshape(nk)[order])
    block_expert = jnp.clip(jnp.searchsorted(pad_end, jnp.arange(n_blocks) * DISPATCH_BLOCK, side='right'),
                            0, N_EXPERTS - 1)
    h_pad = jnp.concatenate([hf, jnp.zeros((1, d), hf.dtype)], axis=0)

    def expert_block(args):
        tok, w, e = args
        xb = h_pad[tok]
        y = (jax.nn.silu(xb @ w_gate[e]) * (xb @ w_up[e])) @ w_down[e]
        return y * w[:, None].astype(y.dtype)

    yb = lax.map(expert_block, (slot_tok.reshape(n_blocks, DISPATCH_BLOCK),
                                slot_w.reshape(n_blocks, DISPATCH_BLOCK), block_expert))
    routed = jax.ops.segment_sum(yb.reshape(n_slots, d), slot_tok, num_segments=n + 1)[:n]
    shared = (jax.nn.silu(hf @ w_sh_gate) * (hf @ w_sh_up)) @ w_sh_down
    return (routed + shared).reshape(b, s, d)

def setup_inputs(seed: int = 0) -> dict:
    key = jax.random.key(seed)
    ks = jax.random.split(key, 24)
    L = DEPTH
    f32 = jnp.float32

    def nrm(k, shape, scale):
        return jax.random.normal(k, shape, f32) * scale

    return {
        'x': nrm(ks[0], (BATCH, SEQ, D_MODEL), 1.0),
        'norm_mix_g': 1.0 + nrm(ks[1], (L, D_MODEL), 0.02),
        'w_in': nrm(ks[2], (L, D_MODEL, D_IN), D_MODEL ** -0.5),
        'q_norm_g': 1.0 + nrm(ks[3], (L, HEAD_DIM), 0.02),
        'k_norm_g': 1.0 + nrm(ks[4], (L, HEAD_DIM), 0.02),
        'rpb': nrm(ks[5], (L, N_HEADS, 2 * WIN_H_MAX - 1, 2 * WIN_W - 1), 0.5),
        'conv_dw_w': nrm(ks[6], (L, CONV_WIDTH, 1, D_CONV), CONV_WIDTH ** -0.5),
        'conv_dw_b': nrm(ks[7], (L, D_CONV), 0.02),
        'conv_ln_g': 1.0 + nrm(ks[8], (L, D_CONV), 0.02),
        'conv_ln_b': nrm(ks[9], (L, D_CONV), 0.02),
        'w_conv_out': nrm(ks[10], (L, D_CONV, D_MODEL), D_CONV ** -0.5),
        'w_attn_out': nrm(ks[11], (L, D_ATTN, D_MODEL), D_ATTN ** -0.5),
        'w_o': nrm(ks[12], (L, D_MODEL, D_MODEL), D_MODEL ** -0.5),
        'norm_ffn_g': 1.0 + nrm(ks[13], (L, D_MODEL), 0.02),
        'w_router': nrm(ks[14], (L, D_MODEL, N_EXPERTS), D_MODEL ** -0.5),
        'router_bias': nrm(ks[15], (L, N_EXPERTS), 0.01),
        'w_exp_gate': nrm(ks[16], (L, N_EXPERTS, D_MODEL, D_EXPERT), D_MODEL ** -0.5),
        'w_exp_up': nrm(ks[17], (L, N_EXPERTS, D_MODEL, D_EXPERT), D_MODEL ** -0.5),
        'w_exp_down': nrm(ks[18], (L, N_EXPERTS, D_EXPERT, D_MODEL), D_EXPERT ** -0.5),
        'w_sh_gate': nrm(ks[19], (L, D_MODEL, D_SHARED), D_MODEL ** -0.5),
        'w_sh_up': nrm(ks[20], (L, D_MODEL, D_SHARED), D_MODEL ** -0.5),
        'w_sh_down': nrm(ks[21], (L, D_SHARED, D_MODEL), D_SHARED ** -0.5),
    }

def reference(x, norm_mix_g, w_in, q_norm_g, k_norm_g, rpb, conv_dw_w, conv_dw_b, conv_ln_g,
              conv_ln_b, w_conv_out, w_attn_out, w_o, norm_ffn_g, w_router, router_bias,
              w_exp_gate, w_exp_up, w_exp_down, w_sh_gate, w_sh_up, w_sh_down):
    b, s, _ = x.shape
    for l in range(DEPTH):
        h = rms_norm(x, norm_mix_g[l])
        proj = h @ w_in[l]
        a, glu_gate, q, k, v, g_a, g_b = jnp.split(proj, SPLITS, axis=-1)
        y_conv = conformer_conv(a, glu_gate, conv_dw_w[l], conv_dw_b[l], conv_ln_g[l],
                                conv_ln_b[l], w_conv_out[l])
        heads = (b, s, N_HEADS, HEAD_DIM)
        q = rms_norm(q.reshape(heads), q_norm_g[l])
        k = rms_norm(k.reshape(heads), k_norm_g[l])
        v = v.reshape(heads)
        y_attn = neighbourhood_attention(q, k, v, rpb[l]) @ w_attn_out[l]
        merged = jax.nn.sigmoid(g_a) * y_conv + jax.nn.sigmoid(g_b) * y_attn
        x = x + merged @ w_o[l]
        x = x + moe_ffn(rms_norm(x, norm_ffn_g[l]), w_router[l], router_bias[l], w_exp_gate[l],
                        w_exp_up[l], w_exp_down[l], w_sh_gate[l], w_sh_up[l], w_sh_down[l])
    return x


_drawn_inputs = setup_inputs


def setup_inputs(seed=0):
    import zlib

    import numpy as np

    out = dict(_drawn_inputs(seed))
    spreads = {}
    factors = {'q_norm_g': 2.783, 'k_norm_g': 2.877}
    for name, (base, spread) in spreads.items():
        noise = np.random.default_rng([zlib.crc32(name.encode()), seed]).standard_normal(out[name].shape)
        drawn = base * np.exp(spread * noise) if base else spread * noise
        out[name] = __import__('jax').numpy.asarray(drawn.astype(out[name].dtype))
    for name, factor in factors.items():
        out[name] = (out[name] * factor).astype(out[name].dtype)
    return out
```

```python
from contextlib import ExitStack, nullcontext

import numpy as np

import concourse.bass as bass
from concourse import mybir

P = 128
T = 1024
D = 1024
NT = T // P
KD = D // P
D_CONV = 512
NC = D_CONV // P
TAPS = 31
PAD = TAPS // 2
CPAD = T + 2 * PAD
HEADS = 8
HD = 64
D_ATTN = HEADS * HD
PAIRS = HEADS // 2
GRID_W = 64
ROWS = T // GRID_W
WIN_H = 8
WIN_W = 16
WKEYS = WIN_H * GRID_W
RELH = 2 * WIN_H - 1
RELW = 2 * WIN_W - 1
RPB_PAD = 64
EXP = 64
GROUPS = 8
PER_GROUP = EXP // GROUPS
TOP_K = 8
F = 256
KF = F // P
WEXP = (2 * KD * F) + KF * D
MAXBLK = T * TOP_K // P + EXP
NBUF = 4
ROUTE_SCALE = 2.5
EPS = 1e-6
BIG = 65536.0
NEG = -1e30

ALU = mybir.AluOpType
ACT = mybir.ActivationFunctionType
F32 = mybir.dt.float32
I32 = mybir.dt.int32
BF16 = mybir.dt.bfloat16
SLOTC = 6
AX = mybir.AxisListType.X

C_ID, C_TRI, C_ONE, C_IOTA, C_MASK, C_ROW, C_EPS, C_PID, C_EMPTY, C_BASE = 0, 128, 256, 384, 512, 576, 584, 585, 586, 587
C_END = C_BASE + MAXBLK + 4
S_DW, S_DB, S_LG, S_LB, S_QG, S_KG, S_END = 0, NC * TAPS, NC * TAPS + 4, NC * TAPS + 8, NC * TAPS + 12, NC * TAPS + 13, NC * TAPS + 14


def build(nc, x, w_in, w_conv_out, w_attn_out, w_o, w_router, w_gate, w_up, w_down,
          w_sh_gate, w_sh_up, w_sh_down, mix_g, ffn_g, router_bias, rpb_rev, small, consts, out):
    with ExitStack() as ctx:
        def sb(name, cols, dt=F32):
            return ctx.enter_context(nc.sbuf_tensor(name, [P, cols], dt))

        def sem(name):
            return ctx.enter_context(nc.semaphore(name))

        h2_rows = nc.dram_tensor("h2_rows", [T, D], F32).ap()

        arena = sb("arena", 24704)
        qT = arena[:, 0:4096].rearrange("p (a t) -> p a t", a=PAIRS)
        kT = arena[:, 4096:8192].rearrange("p (a t) -> p a t", a=PAIRS)
        merged = arena[:, 0:8192].rearrange("p (m t) -> p m t", m=KD)
        v_rows = arena[:, 8192:16384].rearrange("p (s n) -> p s n", n=D_ATTN)
        wo_sb = arena[:, 8192:16384].rearrange("p (k n) -> p k n", k=KD)
        conv_in = arena[:, 16384:16384 + NC * CPAD].rearrange("p (c t) -> p c t", c=NC)
        attnT = arena[:, 16384:16384 + 4096].rearrange("p (a t) -> p a t", a=PAIRS)
        conv_u = arena[:, 20608:24704].rearrange("p (c t) -> p c t", c=NC)
        rpb_raw = arena[:, 20608:20608 + PAIRS * RELH * GRID_W]
        h2T = arena[:, 16384:24576].rearrange("p (k t) -> p k t", k=KD)

        hx = sb("hx", 8192)
        hT = hx[:, :].rearrange("p (k t) -> p k t", k=KD)
        x2 = hx[:, :].rearrange("p (t d) -> p t d", t=NT)

        bias_t = sb("bias_t", PAIRS * RELH * GRID_W)
        biasT = bias_t[:, :].rearrange("p (a r c) -> p a r c", a=PAIRS, r=RELH)
        slot_key = bias_t[:, 0:512]
        weight = bias_t[:, 1024:1536]
        hs2 = [bias_t[:, 1536 + F * i:1536 + F * (i + 1)] for i in range(2)]
        hsT2 = [bias_t[:, 2048 + F * i:2048 + F * (i + 1)] for i in range(2)]
        silu2 = [bias_t[:, 2560 + F * i:2560 + F * (i + 1)] for i in range(2)]
        rt = bias_t[:, 3072:3840]

        wring = sb("wring", 8192)
        wchunk = [wring[:, 4096 * i:4096 * (i + 1)] for i in range(2)]
        onehot = [wring[:, 512 * i:512 * (i + 1)].bitcast(BF16).rearrange("p (t j) -> p t j", t=NT) for i in range(2)]
        slot_tab = wring[:, 4096:4096 + NT * EXP * SLOTC // 2].bitcast(BF16)
        y_sb = [wring[:, 2048 + 1024 * i:2048 + 1024 * (i + 1)] for i in range(2)]
        wr_sb = wring[:, 4096 + 2048:4096 + 2048 + 512].rearrange("p (k e) -> p k e", k=KD)
        wshd_sb = wring[:, 4096:4096 + 2048].rearrange("p (k n) -> p k n", k=KF)
        wshgu_sb = wring[:, 0:4096].rearrange("p (g k f) -> p g k f", g=2, k=KD)

        xr_t = sb("xr_t", 2048)
        hr_t = sb("hr_t", 2048)
        xr = [xr_t[:, D * i:D * (i + 1)] for i in range(2)]
        hr = [hr_t[:, D * i:D * (i + 1)] for i in range(2)]
        half = [xr_t[:, 512 * i:512 * (i + 1)] for i in range(4)] + [hr_t[:, 512 * i:512 * (i + 1)] for i in range(4)]
        gate_row = sb("gate_row", D)
        rb_row = sb("rb_row", EXP)
        cst = sb("cst", C_END)
        sml = sb("sml", S_END)
        ident = cst[:, C_ID:C_ID + P]
        tri = cst[:, C_TRI:C_TRI + P]
        ones = cst[:, C_ONE:C_ONE + P]
        iota = cst[:, C_IOTA:C_IOTA + P]
        wmask = cst[:, C_MASK:C_MASK + GRID_W]
        row_less_big = cst[:, C_ROW:C_ROW + NT]
        eps = cst[:, C_EPS:C_EPS + 1]
        st = sb("st", 160)
        qblk = [sb(f"qblk{i}", P) for i in range(2)]
        osb = [sb(f"osb{i}", P) for i in range(2)]
        blk_i = sb("blk_i", MAXBLK + 8, I32)
        end_i = sb("end_i", EXP, I32)
        idx_i = sb("idx_i", 16, I32)
        nb_i = sb("nb_i", EXP, I32)
        slot_w2 = sb("slot_w2", 8)[:, :].rearrange("p (a u) -> p a u", a=2)

        ps = [ctx.enter_context(nc.psum_tensor(f"ps{i}", [P, 512], F32)) for i in range(8)]

        s = {n: sem(n) for n in """const_in small_in row_in rpb_in x_in0 x_in1 w_in0 w_in1 wo_in vo_in misc_in
            ssq_ready rms_ready rstd_ready h_ready h_T hT_evA hT_evD
            ag_done sig_ready u_ready padded conv_step bias_ready bias_step bias_m
            qk_done sq_ready ss_ready qg_ready qrms_ready qrstd_ready qn_ready qk_T qk_ev v_done v_ev
            qz_ready qblk_ready s_done s_biased negmax_ready p_ready rowinv_ready pT_done pT_ev o_done o_ev oT_done oT_ev
            mu_done cen_ready csq_ready var_done sd_ready lrstd_ready un_ready uT_ready
            m_done gates_ready prod_ready merged_ready
            xo_done x2_ready h2_out h2_T h2T_evA h2T_evD r_done scores_ready
            sh_done shs_ready shh_ready shT_done shT_ev shd_done acc_ready
            rt_step sel_ready cum_done blk_done tab_ready
            oh_step oh_ready idx_done idx_step xg_in0 xg_in1 xT_done xT_evA xT_evD gu_done silu_ready hs_ready
            hsT_done hsT_ev y_done y_evA y_evD y_out wl0 wl1 w_ready acc_out row_parts weight_ready weight_parts""".split()}

        def gchunk(m, part):
            c = wchunk[m % 2]
            if part == "ga":
                return c[:, 0:1024].rearrange("p (k n) -> p k n", k=KD)
            if part == "gb":
                return c[:, 1024:2048].rearrange("p (k n) -> p k n", k=KD)
            if part == "co":
                return c[:, 2048:2560].rearrange("p (k n) -> p k n", k=NC)
            return c[:, 2560:3072].rearrange("p (k n) -> p k n", k=NC)

        w_in_k = w_in.rearrange("(k p) n -> p k n", p=P)
        co_k = w_conv_out.rearrange("(k p) n -> p k n", p=P)
        ao_k = w_attn_out.rearrange("(k p) n -> p k n", p=P)
        x_t = x.rearrange("(t p) d -> t p d", p=P)
        out_t = out.rearrange("(t p) d -> t p d", p=P)
        h2_t = h2_rows.rearrange("(t p) d -> t p d", p=P)
        Q0, K0, V0, GA0, GB0 = 1024, 1536, 2048, 2560, 3584

        plain = [[(0, 256), (512, 256)], [(256, 256), (768, 256)], [(Q0, 512)], [(K0, 512)], [(V0, 512)]]
        NPLAIN = len(plain)
        wload = [0, 0]
        chunk_at = []
        for i in range(NPLAIN + KD):
            n = len(plain[i]) if i < NPLAIN else 4
            slot = i % 2 if i < NPLAIN else (NPLAIN + i - NPLAIN) % 2
            wload[slot] += 16 * n
            chunk_at.append((slot, wload[slot]))

        def chunk_used(eng, i):
            if i < NPLAIN:
                name, n = (("ag_done", NC), ("ag_done", 2 * NC), ("qk_done", NT), ("qk_done", 2 * NT), ("v_done", NT))[i]
            else:
                name, n = "m_done", 2 * (i - NPLAIN + 1)
            eng.wait_ge(s[name], n)

        def chunk_here(eng, i):
            eng.wait_ge(s[f"w_in{chunk_at[i][0]}"], chunk_at[i][1])

        def arena_w(e4, part):
            base = e4 * WEXP
            if part == "gu":
                return arena[:, bass.ds(base, 2 * KD * F)].rearrange("p (g k f) -> p g k f", g=2, k=KD)
            return arena[:, bass.ds(base + 2 * KD * F, KF * D)].rearrange("p (k n) -> p k n", k=KF)

        scores = xr_t[:, 0:512]
        biased = xr_t[:, 512:1024]
        masked = xr_t[:, 1024:1536]
        sel = xr_t[:, 1536:2048]
        ringfree = wring[:, 6656:8192]
        r_top = ringfree[:, 0:EXP]
        r_gs = ringfree[:, 64:76]
        r_go = ringfree[:, 80:92]
        r_rep = ringfree[:, 96:104]
        r_t8 = ringfree[:, 104:112]
        r_gm = ringfree[:, 112:120]
        r_gn = ringfree[:, 120:128]
        r_mo = ringfree[:, 128:192]
        r_sum = ringfree[:, 192:193]
        r_inv = ringfree[:, 193:194]
        r_eb = ringfree[:, 194:195]
        r_nb = ringfree[:, 256:320]
        r_end = ringfree[:, 320:384]
        r_nb_i = nb_i[:, :]
        r_start = ringfree[:, 384:448]
        r_le = ringfree[:, 448:512]
        r_key = ringfree[:, 512:1024]
        gcol = [st[:, 104 + 8 * i:112 + 8 * i] for i in range(2)]

        def load_plain(sp, i):
            slot = chunk_at[i][0]
            c = wchunk[slot].rearrange("p (k n) -> p k n", k=KD)
            at = 0
            for c0, n in plain[i]:
                sp.dma_start(c[:, :, at:at + n], w_in_k[:, :, c0:c0 + n]).then_inc(s[f"w_in{slot}"], 16)
                at += n

        def load_gates(sp, m):
            i = NPLAIN + m
            chunk_used(sp, i - 2)
            slot = chunk_at[i][0]
            for part, src in (("ga", w_in_k[:, :, GA0 + m * P:GA0 + (m + 1) * P]), ("gb", w_in_k[:, :, GB0 + m * P:GB0 + (m + 1) * P]),
                              ("co", co_k[:, :, m * P:(m + 1) * P]), ("ao", ao_k[:, :, m * P:(m + 1) * P])):
                sp.dma_start(gchunk(slot, part), src).then_inc(s[f"w_in{slot}"], 16)

        def load_expert(sp, e, buf, par):
            gu = arena_w(buf, "gu")
            for g, w in ((0, w_gate), (1, w_up)):
                sp.dma_start(gu[:, g].rearrange("p k f -> p (k f)"), w[bass.ds(e, 1)].rearrange("e (p k) f -> p (e k f)", k=KD)
                             ).then_inc(s[f"wl{par}"], 16)
            sp.dma_start(arena_w(buf, "dn").rearrange("p k n -> p (k n)"), w_down[bass.ds(e, 1)].rearrange("e (p k) n -> p (e k n)", k=KF)
                         ).then_inc(s[f"wl{par}"], 16)

        def expert_here(sp, e, par):
            if isinstance(e, int):
                v = 48 * (e // 2 + 1)
            else:
                v = 24 * e + (48 if par == 0 else 24)
            sp.wait_ge(s[f"wl{par}"], v)
            sp.sem_inc(s["w_ready"], 1)

        def query_block(pool, r, a):
            for hh in range(2):
                pr = slice(64 * hh, 64 * hh + 64)
                pool.tensor_copy(qblk[a % 2][pr, 64 * hh:64 * hh + 64], qT[pr, a, bass.ds(r * GRID_W, GRID_W)]
                                 ).then_inc(s["qblk_ready"], 1)

        def gather(pool, b, u, last_token):
            if isinstance(b, int):
                pool.wait_ge(s["idx_step"], 3 * b + 3)
                if b >= 2:
                    pool.wait_ge(s["xT_done"], b - 1)
            else:
                steps, turned = pool.to_reg(3 * b + 3), pool.to_reg(b - 1)
                pool.wait_ge(s["h2_out"], 16 * NT)
                pool.wait_ge(s["idx_step"], steps)
                pool.wait_ge(s["xT_done"], turned)
            pool.indirect_dma_start(hr[u % 2], None, h2_rows, bass.IndirectOffsetOnAxis(ap=idx_i[:, u:u + 1], axis=0),
                                    bounds_check=last_token, oob_is_err=False).then_inc(s[f"xg_in{u % 2}"], 16)

        def expert_of(eng, b):
            return eng.value_load(blk_i[0:1, bass.ds(b, 1)], min_val=0, max_val=EXP - 1)

        def window(r):
            if isinstance(r, int):
                return min(max(r - WIN_H // 2, 0), ROWS - WIN_H)
            first = (r > WIN_H // 2) * (r - WIN_H // 2) - (r > ROWS - WIN_H // 2) * (r - (ROWS - WIN_H // 2))
            return first.with_bounds(min_val=0, max_val=ROWS - WIN_H)

        def value_tile(r0):
            return (r0 % 2) * NT + r0 // 2

        def score(pe, it, a, k0):
            pe.wait_ge(s["qblk_ready"], 2 * it + 2)
            mm = pe.matmul(ps[a][:, :], qblk[a % 2][:, :], kT[:, a, bass.ds(k0, WKEYS)], start=True, stop=True)
            mm.then_inc(s["s_done"], 1)

        def turn_p(pe, it, a):
            pe.wait_ge(s["p_ready"], it + 3)
            pe.wait_ge(s["pT_ev"], it + 1)
            for j in range(4):
                mm = pe.transpose(ps[4 + a % 2][:, P * j:P * j + P], half[4 + a % 2][:, P * j:P * j + P], ident)
            mm.then_inc(s["pT_done"], 1)

        def values(pe, it, a, v0):
            pe.wait_ge(s["pT_ev"], it + 3)
            pe.wait_ge(s["o_ev"], it + 4)
            for j in range(4):
                mm = pe.matmul(ps[6][:, 0:P], half[6 + a % 2][:, P * j:P * j + P],
                               arena[:, bass.ds(v0 + (8192 + j * D_ATTN + a * P), P)], start=(j == 0), stop=(j == 3))
            mm.then_inc(s["o_done"], 1)

        def turn_o(pe, it, a):
            pe.wait_ge(s["o_ev"], it + 5)
            pe.wait_ge(s["oT_ev"], 2 * it + 2)
            pe.transpose(ps[7][:, 0:P], osb[a % 2][:, :], ident).then_inc(s["oT_done"], 1)

        def slots(pe, b, par, e):
            pe.wait_ge(s["oh_ready"], b + 1)
            if not (isinstance(b, int) and b == 0):
                pe.wait_ge(s["idx_step"], 3 * b)
            for t in range(NT):
                mm = pe.matmul(ps[7][:, 256:256 + SLOTC], onehot[par][:, t, :], slot_tab[:, bass.ds(SLOTC * e + SLOTC * EXP * t, SLOTC)],
                               start=(t == 0), stop=(t == NT - 1))
            mm.then_inc(s["idx_done"], 1)

        def turn_x(pe, b, par):
            pe.wait_ge(s[f"xg_in{par}"], 8 * b + (16 if par == 0 else 8))
            if not (isinstance(b, int) and b == 0):
                pe.wait_ge(s["xT_evA"], b)
                pe.wait_ge(s["xT_evD"], b)
            for k in range(KD):
                mm = pe.transpose(ps[k // 4][:, P * (k % 4):P * (k % 4) + P], hr[par][:, k * P:(k + 1) * P], ident)
            mm.then_inc(s["xT_done"], 1)

        def gate_up(pe, b, par, e):
            pe.wait_ge(s["w_ready"], e + 1)
            pe.wait_ge(s["xT_evA"], b + 1)
            pe.wait_ge(s["xT_evD"], b + 1)
            if not (isinstance(b, int) and b == 0):
                pe.wait_ge(s["hs_ready"], b)
            for k in range(KD):
                mm = pe.matmul(ps[2 + par][:, :], xr[par][:, k * P:(k + 1) * P], gu_cols(e, k), start=(k == 0), stop=(k == KD - 1))
            mm.then_inc(s["gu_done"], 1)

        def turn_h(pe, b, par):
            pe.wait_ge(s["hs_ready"], b + 2)
            pe.wait_ge(s["hsT_ev"], b + 1)
            for k in range(KF):
                mm = pe.transpose(ps[6][:, P * k:P * k + P], hs2[par][:, P * k:P * k + P], ident)
            mm.then_inc(s["hsT_done"], 1)

        def down(pe, b, par, e):
            pe.wait_ge(s["hsT_ev"], b + 2)
            pe.wait_ge(s["y_evA"], b + 1)
            pe.wait_ge(s["y_evD"], b + 1)
            for n in range(2):
                for k in range(KF):
                    mm = pe.matmul(ps[4 + n][:, :], hsT2[par][:, P * k:P * k + P], dn_cols(e, k, n), start=(k == 0), stop=(k == KF - 1))
            mm.then_inc(s["y_done"], 1)

        def gu_cols(e, k):
            buf = (e % NBUF) * WEXP
            return arena[:, bass.ds(buf + k * F, KD * F + F)].rearrange("p (a f) -> p a f", f=F)[:, ::KD, :]

        def dn_cols(e, k, n):
            return arena[:, bass.ds((e % NBUF) * WEXP + (2 * KD * F + k * D + 512 * n), 512)]

        def rms_act(act, count, t, src):
            act.activation(hr[t % 2], src, ACT.Square, accum_out=st[:, t:t + 1]).then_inc(s["ssq_ready"], 1)
            act.wait_ge(s["ssq_ready"], count + 1)
            act.activation(st[:, 8 + t:9 + t], st[:, t:t + 1], ACT.Sqrt, bias=eps, scale=1.0 / D).then_inc(s["rms_ready"], 1)

        def hT_act(act, t):
            act.wait_ge(s["h_T"], t + 1)
            act.activation(hT[:, 0:4, P * t:P * t + P], ps[2 * (t % 2)][:, :].rearrange("p (k t) -> p k t", k=4), ACT.Copy).then_inc(s["hT_evA"], 1)

        def copy_pT(act, it, a):
            act.wait_ge(s["pT_done"], it + 3)
            act.wait_ge(s["o_done"], it + 1)
            act.activation(half[6 + a % 2], ps[4 + a % 2][:, :], ACT.Copy).then_inc(s["pT_ev"], 1)

        def copy_xT_act(act, b, par):
            act.wait_ge(s["xT_done"], b + 1)
            if not (isinstance(b, int) and b == 0):
                act.wait_ge(s["gu_done"], b)
            act.activation(xr[par][:, 0:512], ps[0][:, :], ACT.Copy).then_inc(s["xT_evA"], 1)

        def copy_hT(act, b, par):
            act.wait_ge(s["hsT_done"], b + 2)
            act.activation(hsT2[par], ps[6][:, 0:F], ACT.Copy).then_inc(s["hsT_ev"], 1)

        def store_acc(act, j):
            act.wait_ge(s["acc_ready"], 2 * (j + 1))
            act.dma_start(out_t[j], x2[:, j, :]).then_inc(s["acc_out"], 16)

        def all_blocks(eng, nblk, body):
            for u in range(4):
                body(u, u)
            with eng.Fori(1, MAXBLK // 4) as q:
                for u in (0, 2):
                    with eng.If(nblk > q * 4 + u):
                        body(q * 4 + u, u)
                        body(q * 4 + (u + 1), u + 1)

        def silu_act(act, b, par):
            act.wait_ge(s["gu_done"], b + 2)
            if not (isinstance(b, int) and b == 0):
                act.wait_ge(s["hs_ready"], b)
            act.activation(silu2[par], ps[2 + par][:, 0:F], ACT.Silu).then_inc(s["silu_ready"], 1)

        def norm_rows(dve, count, t, src, free, dst):
            dve.wait_ge(s["rms_ready"], count + 1)
            dve.reciprocal(st[:, 16 + t:17 + t], st[:, 8 + t:9 + t]).then_inc(s["rstd_ready"], 1)
            dve.wait_ge(s["rstd_ready"], count + 1)
            dve.wait_ge(s["row_in"], 16 * (count // NT + 1))
            if free:
                dve.wait_ge(s[free[0]], free[1])
            dve.scalar_tensor_tensor(out=dst, in0=src, scalar=st[:, 16 + t:17 + t], in1=gate_row[:, :], op0=ALU.mult, op1=ALU.mult
                                     ).then_inc(s["h_ready"], 1)

        def tap(dve, n):
            c, j = divmod(n, TAPS)
            w = sml[:, S_DW + c * TAPS + j:S_DW + c * TAPS + j + 1]
            src = conv_in[:, c, j:j + T]
            if j == 0:
                dve.tensor_scalar(conv_u[:, c, :], src, w, sml[:, S_DB + c:S_DB + c + 1], ALU.mult, ALU.add).then_inc(s["conv_step"], 1)
            else:
                dve.wait_ge(s["conv_step"], n)
                dve.scalar_tensor_tensor(out=conv_u[:, c, :], in0=src, scalar=w, in1=conv_u[:, c, :], op0=ALU.mult, op1=ALU.add).then_inc(s["conv_step"], 1)

        def bias_max(dve, it, a, d0):
            dve.wait_ge(s["s_done"], it + 1)
            dve.tensor_tensor(half[a].rearrange("p (r c) -> p r c", r=WIN_H), ps[a][:, :].rearrange("p (r c) -> p r c", r=WIN_H),
                              biasT[:, a, bass.ds(d0, WIN_H), :], ALU.add).then_inc(s["s_biased"], 1)
            dve.wait_ge(s["s_biased"], it + 1)
            dve.tensor_reduce(st[:, 80 + a:81 + a], half[a], AX, ALU.max, negate=True).then_inc(s["negmax_ready"], 1)

        def out_rows(dve, it, a):
            dve.wait_ge(s["p_ready"], it + 3)
            dve.reciprocal(st[:, 96 + a:97 + a], st[:, 88 + a:89 + a]).then_inc(s["rowinv_ready"], 1)
            dve.wait_ge(s["rowinv_ready"], it + 1)
            dve.wait_ge(s["o_done"], it + 3)
            dve.wait_ge(s["oT_done"], it + 1)
            dve.tensor_scalar(osb[a % 2][:, :], ps[6][:, 0:P], st[:, 96 + a:97 + a], None, ALU.mult).then_inc(s["o_ev"], 1)

        def out_cols(dve, it, a, r):
            dve.wait_ge(s["oT_done"], it + 3)
            for hh in range(2):
                pr = slice(64 * hh, 64 * hh + 64)
                dve.tensor_copy(attnT[pr, a, bass.ds(r * GRID_W, GRID_W)], ps[7][pr, 64 * hh:64 * hh + 64]
                                ).then_inc(s["oT_ev"], 1)

        def route(dve, step, t):
            sc, bi, ma, se = (v[:, EXP * t:EXP * t + EXP] for v in (scores, biased, masked, sel))
            step(dve.tensor_tensor(bi, sc, rb_row[:, :], ALU.add))
            for g in range(GROUPS):
                m = dve.max(r_top[:, 8 * g:8 * g + 8], bi[:, PER_GROUP * g:PER_GROUP * (g + 1)])
                step(m)
            top = r_top.rearrange("p (g j) -> p g j", g=GROUPS)
            step(dve.tensor_tensor(r_gs[:, 0:GROUPS], top[:, :, 0], top[:, :, 1], ALU.add))
            step(dve.max(r_t8, r_gs[:, 0:GROUPS]))
            step(dve.tensor_copy(r_rep[:, 0:4], r_t8[:, 0:4]))
            step(dve.match_replace(r_go, r_rep, r_gs, 3.0 * NEG))
            step(dve.tensor_tensor(r_gm, r_go[:, 0:GROUPS], r_gs[:, 0:GROUPS], ALU.is_lt))
            step(dve.tensor_scalar(r_gn, r_gm, 1.0, -NEG, ALU.subtract, ALU.mult))
            ma3 = ma.rearrange("p (g j) -> p g j", g=GROUPS)
            step(dve.tensor_tensor(ma3, bi.rearrange("p (g j) -> p g j", g=GROUPS), r_gm.unsqueeze(2).to_broadcast([P, GROUPS, PER_GROUP]), ALU.mult))
            step(dve.tensor_tensor(ma3, ma3, r_gn.unsqueeze(2).to_broadcast([P, GROUPS, PER_GROUP]), ALU.add))
            step(dve.max(r_t8, ma))
            step(dve.match_replace(r_mo, r_t8, ma, 3.0 * NEG))
            dve.tensor_tensor(se, r_mo, ma, ALU.is_lt).then_inc(s["sel_ready"], 1)
            dve.wait_ge(s["sel_ready"], t + 1)
            step(dve.tensor_tensor(r_mo, sc, se, ALU.mult))
            step(dve.tensor_reduce(r_sum, r_mo, AX, ALU.add))
            step(dve.reciprocal(r_inv, r_sum))
            dve.tensor_scalar(weight[:, EXP * t:EXP * t + EXP], r_mo, r_inv, ROUTE_SCALE, ALU.mult, ALU.mult).then_inc(s["weight_ready"], 1)

        def one_hot(dve, b, par):
            e = 0 if isinstance(b, int) and b == 0 else expert_of(dve, b)
            keys = slot_key.rearrange("p (t e) -> p e t", t=NT)[:, bass.ds(e, 1), :].rearrange("p e t -> p (e t)")
            dve.tensor_scalar(gcol[par], keys, cst[:, bass.ds(C_BASE + b, 1)], None, ALU.subtract).then_inc(s["oh_step"], 1)
            dve.wait_ge(s["oh_step"], b + 1)
            if not (isinstance(b, int) and b < 2):
                dve.wait_ge(s["idx_done"], b - 1)
            dve.tensor_tensor(onehot[par], gcol[par].unsqueeze(2).to_broadcast([P, NT, P]), iota.unsqueeze(1).to_broadcast([P, NT, P]), ALU.is_equal
                              ).then_inc(s["oh_ready"], 1)

        def slot_rows(dve, b, u):
            dve.wait_ge(s["idx_done"], b + 1)
            if not (isinstance(b, int) and b < 4):
                dve.wait_ge(s["y_out"], 16 * b - 48)
            dve.tensor_reduce(slot_w2[:, :, u], ps[7][:, 256:256 + SLOTC].rearrange("p (a c) -> p a c", a=2), AX, ALU.add).then_inc(s["idx_step"], 1)
            dve.wait_ge(s["idx_step"], 3 * b + 1)
            dve.tensor_scalar(idx_i[:, u:u + 1], slot_w2[:, 0, u:u + 1], BIG, None, ALU.add).then_inc(s["idx_step"], 1)
            dve.tensor_scalar(idx_i[:, 8 + u:9 + u], slot_w2[:, 0, u:u + 1], BIG, cst[:, C_EMPTY:C_EMPTY + 1], ALU.add, ALU.min
                              ).then_inc(s["idx_step"], 1)

        def copy_xT_dve(dve, b, par):
            dve.wait_ge(s["xT_done"], b + 1)
            if not (isinstance(b, int) and b == 0):
                dve.wait_ge(s["gu_done"], b)
            dve.tensor_copy(xr[par][:, 512:1024], ps[1][:, :]).then_inc(s["xT_evD"], 1)

        def weigh(dve, b, u):
            par = u % 2
            dve.wait_ge(s["silu_ready"], b + 1)
            dve.wait_ge(s["idx_step"], 3 * b + 3)
            if not (isinstance(b, int) and b == 0):
                dve.wait_ge(s["hsT_done"], b)
            dve.scalar_tensor_tensor(out=hs2[par].rearrange("p (k q) -> p q k", k=KF), in0=silu2[par].rearrange("p (q k) -> p q k", k=KF),
                                     scalar=slot_w2[:, 1, u:u + 1], in1=ps[2 + par][:, F:2 * F].rearrange("p (q k) -> p q k", k=KF),
                                     op0=ALU.mult, op1=ALU.mult).then_inc(s["hs_ready"], 1)

        block = ctx.enter_context(nc.Block())

        @block.sync
        def _(sp):
            sp.dma_start(cst[:, :], consts).then_inc(s["const_in"], 16)
            sp.dma_start(sml[:, :], small).then_inc(s["small_in"], 16)
            sp.dma_start(gate_row[:, :], mix_g.partition_broadcast(P)).then_inc(s["row_in"], 16)
            for t in range(NT):
                if t >= 2:
                    sp.wait_ge(s["h_ready"], t - 1)
                sp.dma_start(xr[t % 2], x_t[t]).then_inc(s[f"x_in{t % 2}"], 16)
                if t < 2:
                    load_plain(sp, t)
            sp.dma_start(rb_row[:, :], router_bias.partition_broadcast(P)).then_inc(s["misc_in"], 16)
            for i in range(2, NPLAIN):
                chunk_used(sp, i - 2)
                load_plain(sp, i)
            load_gates(sp, 0)
            sp.wait_ge(s["v_ev"], NT)
            sp.dma_start(v_rows[0:64, NT:2 * NT - 1, :], v_rows[64:128, 0:NT - 1, :]).then_inc(s["vo_in"], 16)
            sp.dma_start(v_rows[64:128, NT:2 * NT - 1, :], v_rows[0:64, 1:NT, :]).then_inc(s["vo_in"], 16)
            load_gates(sp, 1)
            sp.wait_ge(s["oT_done"], ROWS * PAIRS + 2)
            sp.dma_start(wo_sb, w_o.rearrange("(k p) n -> p k n", p=P)).then_inc(s["wo_in"], 16)
            sp.dma_start(gate_row[:, :], ffn_g.partition_broadcast(P)).then_inc(s["row_in"], 16)
            for m in range(2, KD):
                load_gates(sp, m)
            sp.wait_ge(s["merged_ready"], 2 * KD)
            for t in range(NT):
                if t >= 2:
                    sp.wait_ge(s["x2_ready"], 2 * (t - 1))
                sp.dma_start(xr[t % 2], x_t[t]).then_inc(s[f"x_in{t % 2}"], 16)
                if t == 0:
                    chunk_used(sp, NPLAIN + KD - 1)
                    sp.dma_start(wr_sb, w_router.rearrange("(p k) e -> p k e", k=KD)).then_inc(s["misc_in"], 16)
                    sp.dma_start(wshgu_sb[:, 0], w_sh_gate.rearrange("(p k) f -> p k f", k=KD)).then_inc(s["misc_in"], 16)
                    sp.dma_start(wshgu_sb[:, 1], w_sh_up.rearrange("(p k) f -> p k f", k=KD)).then_inc(s["misc_in"], 16)
                    sp.dma_start(wshd_sb, w_sh_down.rearrange("(p k) n -> p k n", k=KF)).then_inc(s["misc_in"], 16)
            sp.wait_ge(s["xo_done"], 2 * NT)
            for e in range(NBUF):
                if e == 2:
                    sp.wait_ge(s["sh_done"], NT)
                load_expert(sp, e, e, e % 2)
                if e:
                    expert_here(sp, e - 1, (e - 1) % 2)
            sp.wait_ge(s["tab_ready"], 3)
            with sp.Fori(0, EXP // NBUF - 1) as q:
                for j in range(NBUF):
                    last = sp.value_load(end_i[0:1, bass.ds(q * NBUF + j, 1)], min_val=0, max_val=MAXBLK)
                    sp.wait_ge(s["y_done"], last)
                    load_expert(sp, q * NBUF + (NBUF + j), j, j % 2)
                    expert_here(sp, q * NBUF + (NBUF + j - 1), (j - 1) % 2)
            expert_here(sp, EXP - 1, 1)

        @block.gpsimd
        def _(pool):
            for c in range(NC):
                pool.memset(conv_in[:, c, 0:PAD], 0.0).then_inc(s["padded"], 1)
                pool.memset(conv_in[:, c, PAD + T:CPAD], 0.0).then_inc(s["padded"], 1)
            for b in range(2):
                pool.memset(qblk[b][:, :], 0.0).then_inc(s["qz_ready"], 1)
            for h in range(HEADS):
                src = bass.AP(rpb_rev.tensor, RPB_PAD + h * RELH * RELW - (GRID_W - WIN_W),
                              [[1, GRID_W], [RELW, RELH], [1, GRID_W]])
                a = (h // 2) * RELH * GRID_W
                pool.dma_start(rpb_raw[64 * (h % 2):64 * (h % 2) + 64, a:a + RELH * GRID_W].rearrange("p (r c) -> p r c", r=RELH),
                               src).then_inc(s["rpb_in"], 16)
            pool.wait_ge(s["rpb_in"], 16 * HEADS)
            pool.wait_ge(s["const_in"], 16)
            mb = wmask.unsqueeze(1).to_broadcast([P, PAIRS * RELH, GRID_W])
            raw = rpb_raw.rearrange("p (r c) -> p r c", c=GRID_W)
            tab = bias_t[:, :].rearrange("p (r c) -> p r c", c=GRID_W)
            pool.tensor_tensor(tab, raw[:, :, ::-1], mb, ALU.mult).then_inc(s["bias_step"], 1)
            pool.tensor_scalar(osb[0][:, 0:GRID_W], wmask, 1.0, -NEG, ALU.subtract, ALU.mult).then_inc(s["bias_m"], 1)
            pool.wait_ge(s["bias_step"], 1)
            pool.wait_ge(s["bias_m"], 1)
            pool.tensor_tensor(tab, tab, osb[0][:, 0:GRID_W].unsqueeze(1).to_broadcast([P, PAIRS * RELH, GRID_W]), ALU.add
                               ).then_inc(s["bias_ready"], 1)
            pool.wait_ge(s["qz_ready"], 2)
            pool.wait_ge(s["qk_ev"], 2 * NT)
            for a in range(2):
                query_block(pool, 0, a)
            with pool.Fori(0, ROWS - 1) as r:
                for a in range(PAIRS):
                    pool.wait_ge(s["s_done"], r * PAIRS + a + 1)
                    query_block(pool, r if a < 2 else r + 1, (a + 2) % PAIRS)
            for a in range(2):
                pool.wait_ge(s["s_done"], (ROWS - 1) * PAIRS + a + 1)
                query_block(pool, ROWS - 1, a + 2)
            tab = slot_tab.rearrange("p (t e c) -> p t e c", t=NT, c=SLOTC)
            pool.wait_ge(s["shd_done"], 2 * NT)
            count = 0
            for i in range(3):
                pool.tensor_copy(tab[:, :, :, i], row_less_big.unsqueeze(2).to_broadcast([P, NT, EXP])).then_inc(s["row_parts"], 1)
                count += 1
                if i < 2:
                    pool.wait_ge(s["row_parts"], count)
                    pool.tensor_tensor(row_less_big, row_less_big, tab[:, :, 0, i], ALU.subtract).then_inc(s["row_parts"], 1)
                    count += 1
                    pool.wait_ge(s["row_parts"], count)
            w3 = weight.rearrange("p (t e) -> p t e", t=NT)
            pool.wait_ge(s["weight_ready"], NT)
            count = 0
            for i in range(3):
                pool.tensor_copy(tab[:, :, :, 3 + i], w3).then_inc(s["weight_parts"], 1)
                count += 1
                if i < 2:
                    pool.wait_ge(s["weight_parts"], count)
                    pool.tensor_tensor(w3, w3, tab[:, :, :, 3 + i], ALU.subtract).then_inc(s["weight_parts"], 1)
                    count += 1
                    pool.wait_ge(s["weight_parts"], count)
            last_token, last_row = pool.to_reg(T - 1), pool.to_reg(T + P - 1)
            pool.wait_ge(s["h2_T"], NT)
            pool.wait_ge(s["h2_out"], 16 * NT)
            for b in range(3):
                gather(pool, b, b, last_token)
            pool.wait_ge(s["tab_ready"], 3)
            nblk = pool.value_load(end_i[0:1, EXP - 1:EXP], min_val=0, max_val=MAXBLK)

            def body(b, u):
                gather(pool, b + 3, (u + 3) % 4, last_token)
                copied, before = pool.to_reg(b + 2), pool.to_reg(16 * b)
                pool.wait_ge(s["acc_out"], 16 * (NT + 1))
                if not (isinstance(b, int) and b == 0):
                    pool.wait_ge(s["y_out"], before)
                pool.wait_ge(s["y_evA"], copied)
                pool.wait_ge(s["y_evD"], copied)
                pool.indirect_dma_start(out, bass.IndirectOffsetOnAxis(ap=idx_i[:, 8 + u:9 + u], axis=0),
                                        y_sb[u % 2], None, bounds_check=last_row, oob_is_err=True, compute_op=ALU.add
                                        ).then_inc(s["y_out"], 16)

            all_blocks(pool, nblk, body)
            pool.wait_ge(s["y_out"], ((nblk + 1) // 2) * 32)

        @block.tensor
        def _(pe):
            pe.wait_ge(s["const_in"], 16)
            for t in range(NT):
                pe.wait_ge(s["h_ready"], t + 1)
                if t >= 2:
                    pe.wait_ge(s["hT_evA"], t - 1)
                    pe.wait_ge(s["hT_evD"], t - 1)
                for k in range(KD):
                    mm = pe.transpose(ps[2 * (t % 2) + k // 4][:, P * (k % 4):P * (k % 4) + P], hr[t % 2][:, k * P:(k + 1) * P], ident)
                mm.then_inc(s["h_T"], 1)
            for c in range(NC):
                if c % 2 == 0:
                    chunk_here(pe, c // 2)
                w = wchunk[c // 2].rearrange("p (k n) -> p k n", k=KD)
                for n in range(2):
                    it = 2 * c + n
                    if c == 0:
                        pe.wait_ge(s["hT_evA"], 4 * (n + 1))
                        pe.wait_ge(s["hT_evD"], 4 * (n + 1))
                    if it >= 2:
                        pe.wait_ge(s["u_ready"], it - 1)
                    for g in range(2):
                        for k in range(KD):
                            mm = pe.matmul(ps[4 + 2 * (it % 2) + g][:, :], w[:, k, 256 * g + P * (c % 2):256 * g + P * (c % 2) + P],
                                           hT[:, k, 512 * n:512 * n + 512], start=(k == 0), stop=(k == KD - 1))
                    mm.then_inc(s["ag_done"], 1)
            for i in range(2 * NT + 1):
                if i < 2 * NT:
                    if i % NT == 0:
                        chunk_here(pe, 2 + i // NT)
                    w = wchunk[(2 + i // NT) % 2].rearrange("p (k n) -> p k n", k=KD)
                    if i == 0:
                        pe.wait_ge(s["hT_evA"], NT)
                    if i >= 2:
                        pe.wait_ge(s["qn_ready"], i - 1)
                    for k in range(KD):
                        mm = pe.matmul(ps[i % 2][:, :], hT[:, k, P * (i % NT):P * (i % NT) + P], w[:, k, :],
                                       start=(k == 0), stop=(k == KD - 1))
                    mm.then_inc(s["qk_done"], 1)
                if i >= 1:
                    j = i - 1
                    pe.wait_ge(s["qn_ready"], j + 1)
                    if j >= 2:
                        pe.wait_ge(s["qk_ev"], j - 1)
                    for a in range(PAIRS):
                        mm = pe.transpose(ps[2 + j % 2][:, P * a:P * a + P], half[2 + j % 2][:, P * a:P * a + P], ident)
                    mm.then_inc(s["qk_T"], 1)
            chunk_here(pe, 4)
            w = wchunk[0].rearrange("p (k n) -> p k n", k=KD)
            pe.wait_ge(s["u_ready"], 2 * NC)
            for t in range(NT):
                if t >= 2:
                    pe.wait_ge(s["v_ev"], t - 1)
                for k in range(KD):
                    mm = pe.matmul(ps[4 + t % 2][:, :], hT[:, k, P * t:P * t + P], w[:, k, :], start=(k == 0), stop=(k == KD - 1))
                mm.then_inc(s["v_done"], 1)
            pe.wait_ge(s["qk_ev"], 2 * NT)
            pe.wait_ge(s["v_ev"], NT)
            pe.wait_ge(s["vo_in"], 32)
            for name in ("pT_done", "o_done", "oT_done"):
                pe.sem_inc(s[name], 2)
            for a in range(PAIRS):
                score(pe, a, a, 0)
            with pe.Fori(0, ROWS - 1) as r:
                k0 = pe.snap(window(r + 1) * GRID_W)
                v0 = pe.snap(value_tile(pe.snap(window(r))) * D_ATTN)
                for a in range(PAIRS):
                    it = r * PAIRS + a
                    pe.wait_ge(s["s_biased"], it + 1)
                    score(pe, it + PAIRS, a, k0)
                    turn_p(pe, it, a)
                    if a:
                        values(pe, it - 1, a - 1, v0)
                    if a > 1:
                        turn_o(pe, it - 2, a - 2)
                values(pe, it, 3, v0)
                turn_o(pe, it - 1, 2)
                turn_o(pe, it, 3)
            v0 = value_tile(window(ROWS - 1)) * D_ATTN
            for a in range(PAIRS):
                it = (ROWS - 1) * PAIRS + a
                turn_p(pe, it, a)
                if a:
                    values(pe, it - 1, a - 1, v0)
                if a > 1:
                    turn_o(pe, it - 2, a - 2)
            values(pe, it, 3, v0)
            turn_o(pe, it - 1, 2)
            turn_o(pe, it, 3)
            pe.wait_ge(s["conv_step"], NC * TAPS)
            for n in range(2):
                for c in range(NC):
                    mm = pe.matmul(ps[n][:, :], ones, conv_u[:, c, 512 * n:512 * n + 512], start=(c == 0), stop=(c == NC - 1))
                mm.then_inc(s["mu_done"], 1)
            for n in range(2):
                for c in range(NC):
                    pe.wait_ge(s["csq_ready"], n * NC + c + 1)
                    mm = pe.matmul(ps[2 + n][:, :], ones, half[NC * n + c], start=(c == 0), stop=(c == NC - 1))
                mm.then_inc(s["var_done"], 1)
            pe.wait_ge(s["oT_ev"], 2 * ROWS * PAIRS + 2)
            for m in range(KD):
                chunk_here(pe, NPLAIN + m)
                slot = chunk_at[NPLAIN + m][0]
                for n in range(2):
                    it = 2 * m + n
                    bank = 4 if it % 2 == 0 else 0
                    if it == 1:
                        pe.wait_ge(s["un_ready"], 2 * NC)
                        pe.wait_ge(s["sd_ready"], 2)
                    if it >= 2:
                        pe.wait_ge(s["prod_ready"], 2 * (it - 1))
                    for b, part, kk, src in ((0, "ga", KD, hT), (1, "gb", KD, hT), (3, "ao", NC, attnT), (2, "co", NC, conv_u)):
                        if it == 0 and part == "co":
                            pe.wait_ge(s["uT_ready"], 2 * NC)
                        for k in range(kk):
                            mm = pe.matmul(ps[bank + b][:, :], gchunk(slot, part)[:, k, :], src[:, k, 512 * n:512 * n + 512],
                                           start=(k == 0), stop=(k == kk - 1))
                    mm.then_inc(s["m_done"], 1)
            pe.wait_ge(s["wo_in"], 16)
            pe.wait_ge(s["merged_ready"], 2 * KD)
            for i in range(NT + 2):
                if i < NT:
                    for n in range(2):
                        if i >= 2:
                            pe.wait_ge(s["x2_ready"], 2 * (i - 2) + n + 1)
                        for k in range(KD):
                            mm = pe.matmul(ps[2 * (i % 2) + n][:, :], merged[:, k, P * i:P * i + P], wo_sb[:, k, 512 * n:512 * n + 512],
                                           start=(k == 0), stop=(k == KD - 1))
                        mm.then_inc(s["xo_done"], 1)
                if i >= 2:
                    j = i - 2
                    pe.wait_ge(s["h_ready"], NT + j + 1)
                    if j >= 1:
                        pe.wait_ge(s["h2T_evA"], j)
                        pe.wait_ge(s["h2T_evD"], j)
                    for k in range(KD):
                        mm = pe.transpose(ps[4 + k // 4][:, P * (k % 4):P * (k % 4) + P], hr[j % 2][:, k * P:(k + 1) * P], ident)
                    mm.then_inc(s["h2_T"], 1)
                    if j == 0:
                        pe.wait_ge(s["misc_in"], 80)
                    pe.wait_ge(s["h2T_evA"], j + 1)
                    pe.wait_ge(s["h2T_evD"], j + 1)
                    for k in range(KD):
                        mm = pe.matmul(ps[6][:, EXP * j:EXP * j + EXP], h2T[:, k, P * j:P * j + P], wr_sb[:, k, :],
                                       start=(k == 0), stop=(k == KD - 1))
                    mm.then_inc(s["r_done"], 1)
            for i in range(NT + 1):
                if i < NT:
                    if i < 2:
                        pe.wait_ge(s["x2_ready"], 2 * NT)
                    else:
                        pe.wait_ge(s["shh_ready"], i - 1)
                    for k in range(KD):
                        mm = pe.matmul(ps[i % 2][:, :], h2T[:, k, P * i:P * i + P], wshgu_sb[:, :, k, :], start=(k == 0), stop=(k == KD - 1))
                    mm.then_inc(s["sh_done"], 1)
                if i >= 1:
                    j = i - 1
                    pe.wait_ge(s["shh_ready"], j + 1)
                    if j >= 1:
                        pe.wait_ge(s["shT_ev"], j)
                    for k in range(KF):
                        mm = pe.transpose(ps[7][:, P * k:P * k + P], hs2[j % 2][:, P * k:P * k + P], ident)
                    mm.then_inc(s["shT_done"], 1)
                    pe.wait_ge(s["shT_ev"], j + 1)
                    for n in range(2):
                        if j >= 1:
                            pe.wait_ge(s["acc_ready"], 2 * (j - 1) + n + 1)
                        else:
                            pe.wait_ge(s["x2_ready"], 2 * NT)
                        for k in range(KF):
                            mm = pe.matmul(ps[2 + n][:, :], hsT2[j % 2][:, P * k:P * k + P], wshd_sb[:, k, 512 * n:512 * n + 512],
                                           start=(k == 0), stop=(k == KF - 1))
                        mm.then_inc(s["shd_done"], 1)
            pe.wait_ge(s["sel_ready"], NT)
            for t in range(NT):
                for j in range(t + 1):
                    pe.matmul(ps[4][:, EXP * t:EXP * t + EXP], tri if j == t else ones, sel[:, EXP * j:EXP * j + EXP],
                              start=(j == 0), stop=(j == t))
            for t in range(NT):
                mm = pe.matmul(ps[5][:, 0:EXP], ones, sel[:, EXP * t:EXP * t + EXP], start=(t == 0), stop=(t == NT - 1))
            mm.then_inc(s["cum_done"], 1)
            pe.wait_ge(s["tab_ready"], 1)
            pe.transpose(ps[5][0:1, P:2 * P], r_eb, ident).then_inc(s["blk_done"], 1)
            pe.sem_inc(s["gu_done"], 1)
            pe.sem_inc(s["hsT_done"], 1)
            pe.wait_ge(s["row_parts"], 5)
            pe.wait_ge(s["weight_parts"], 5)
            slots(pe, 0, 0, 0)
            pe.wait_ge(s["tab_ready"], 3)
            nblk = pe.value_load(end_i[0:1, EXP - 1:EXP], min_val=0, max_val=MAXBLK)
            slots(pe, 1, 1, expert_of(pe, 1))
            slots(pe, 2, 0, expert_of(pe, 2))
            turn_x(pe, 0, 0)
            gate_up(pe, 0, 0, 0)
            turn_x(pe, 1, 1)
            turn_h(pe, 0, 0)

            def body(b, u):
                gate_up(pe, b + 1, (u + 1) % 2, expert_of(pe, b + 1))
                slots(pe, b + 3, (u + 1) % 2, expert_of(pe, b + 3))
                turn_x(pe, b + 2, u % 2)
                down(pe, b, u % 2, expert_of(pe, b))
                turn_h(pe, b + 1, (u + 1) % 2)

            all_blocks(pe, nblk, body)

        @block.scalar
        def _(act):
            act.wait_ge(s["const_in"], 16)
            for t in range(NT):
                act.wait_ge(s[f"x_in{t % 2}"], 16 * (t // 2 + 1))
                if t >= 2:
                    act.wait_ge(s["h_T"], t - 1)
                rms_act(act, t, t, xr[t % 2])
                if t >= 1:
                    hT_act(act, t - 1)
            hT_act(act, NT - 1)
            for it in range(2 * NC):
                act.wait_ge(s["ag_done"], it + 1)
                if it >= 2:
                    act.wait_ge(s["u_ready"], it - 1)
                act.activation(half[it % 2], ps[5 + 2 * (it % 2)][:, :], ACT.Sigmoid).then_inc(s["sig_ready"], 1)
            for i in range(2 * NT + 1):
                if i < 2 * NT:
                    act.wait_ge(s["qk_done"], i + 1)
                    if i >= 2:
                        act.wait_ge(s["ss_ready"], i - 1)
                    act.activation(half[4 + i % 2], ps[i % 2][:, :], ACT.Square).then_inc(s["sq_ready"], 1)
                    act.wait_ge(s["ss_ready"], i + 1)
                    if i >= 2:
                        act.wait_ge(s["qrstd_ready"], i - 1)
                    act.activation(st[:, 40 + 8 * (i % 2):48 + 8 * (i % 2)], st[:, 24 + 8 * (i % 2):32 + 8 * (i % 2)], ACT.Sqrt,
                                   bias=eps, scale=1.0 / HD).then_inc(s["qrms_ready"], 1)
                if i >= 1:
                    j = i - 1
                    act.wait_ge(s["qk_T"], j + 1)
                    if j == 0:
                        act.wait_ge(s["qg_ready"], 1)
                        act.wait_ge(s["small_in"], 16)
                    dst, g = (qT, st[:, 72:73]) if j < NT else (kT, sml[:, S_KG:S_KG + 1])
                    act.activation(dst[:, :, P * (j % NT):P * (j % NT) + P], ps[2 + j % 2][:, :].rearrange("p (a t) -> p a t", a=PAIRS),
                                   ACT.Copy, scale=g).then_inc(s["qk_ev"], 1)
            for t in range(NT):
                act.wait_ge(s["v_done"], t + 1)
                act.activation(v_rows[:, t, :], ps[4 + t % 2][:, :], ACT.Copy).then_inc(s["v_ev"], 1)
            act.sem_inc(s["p_ready"], 2)
            act.sem_inc(s["pT_ev"], 2)
            with act.Fori(0, ROWS) as r:
                for a in range(PAIRS):
                    it = r * PAIRS + a
                    act.wait_ge(s["negmax_ready"], it + 1)
                    act.wait_ge(s["pT_done"], it + 1)
                    act.wait_ge(s["o_ev"], it + 1)
                    act.activation(half[4 + a % 2], half[a], ACT.Exp, bias=st[:, 80 + a:81 + a],
                                   accum_out=st[:, 88 + a:89 + a]).then_inc(s["p_ready"], 1)
                    if a:
                        copy_pT(act, it - 1, a - 1)
                copy_pT(act, it, 3)
            for n in range(2):
                for c in range(NC):
                    act.wait_ge(s["cen_ready"], n * NC + c + 1)
                    act.activation(half[NC * n + c], conv_u[:, c, 512 * n:512 * n + 512], ACT.Square).then_inc(s["csq_ready"], 1)
            for n in range(2):
                act.wait_ge(s["var_done"], n + 1)
                act.activation(half[n], ps[2 + n][:, :], ACT.Sqrt, bias=eps, scale=1.0 / D_CONV).then_inc(s["sd_ready"], 1)
            for n in range(2):
                for c in range(NC):
                    act.wait_ge(s["un_ready"], n * NC + c + 1)
                    act.activation(conv_u[:, c, 512 * n:512 * n + 512], conv_u[:, c, 512 * n:512 * n + 512], ACT.Silu,
                                   scale=sml[:, S_LG + c:S_LG + c + 1], bias=sml[:, S_LB + c:S_LB + c + 1]).then_inc(s["uT_ready"], 1)
            for it in range(2 * KD):
                bank = 4 if it % 2 == 0 else 0
                act.wait_ge(s["m_done"], it + 1)
                if it >= 2:
                    act.wait_ge(s["prod_ready"], 2 * (it - 1))
                for g in range(2):
                    act.activation(half[2 * g + it % 2], ps[bank + g][:, :], ACT.Sigmoid).then_inc(s["gates_ready"], 1)
            for t in range(NT + 2):
                if t < NT:
                    act.wait_ge(s["x2_ready"], 2 * (t + 1))
                    if t >= 2:
                        act.wait_ge(s["h2_T"], t - 1)
                        act.wait_ge(s["h2_out"], 16 * (t - 1))
                    rms_act(act, NT + t, t, x2[:, t, :])
                if 1 <= t <= NT:
                    act.wait_ge(s["h_ready"], NT + t)
                    act.dma_start(h2_t[t - 1], hr[(t - 1) % 2]).then_inc(s["h2_out"], 16)
                if t >= 2:
                    j = t - 2
                    act.wait_ge(s["h2_T"], j + 1)
                    act.activation(h2T[:, 0:4, P * j:P * j + P], ps[4][:, :].rearrange("p (k t) -> p k t", k=4), ACT.Copy).then_inc(s["h2T_evA"], 1)
            act.wait_ge(s["r_done"], NT)
            act.activation(scores, ps[6][:, :], ACT.Sigmoid).then_inc(s["scores_ready"], 1)
            for i in range(NT + 1):
                if i < NT:
                    act.wait_ge(s["sh_done"], i + 1)
                    if i >= 2:
                        act.wait_ge(s["shh_ready"], i - 1)
                    act.activation(silu2[i % 2], ps[i % 2][:, 0:F], ACT.Silu).then_inc(s["shs_ready"], 1)
                if i >= 1:
                    j = i - 1
                    act.wait_ge(s["shT_done"], j + 1)
                    if j >= 2:
                        act.wait_ge(s["shd_done"], 2 * (j - 1))
                    act.activation(hsT2[j % 2], ps[7][:, 0:F], ACT.Copy).then_inc(s["shT_ev"], 1)
                if i >= 2:
                    store_acc(act, i - 2)
            store_acc(act, NT - 1)
            act.dma_start(out_t[NT], x2[:, 0, :]).then_inc(s["acc_out"], 16)
            act.wait_ge(s["tab_ready"], 3)
            nblk = act.value_load(end_i[0:1, EXP - 1:EXP], min_val=0, max_val=MAXBLK)
            act.sem_inc(s["hsT_ev"], 1)
            act.sem_inc(s["y_evA"], 1)
            copy_xT_act(act, 0, 0)
            silu_act(act, 0, 0)
            copy_xT_act(act, 1, 1)
            copy_hT(act, 0, 0)

            def body(b, u):
                silu_act(act, b + 1, (u + 1) % 2)
                copy_xT_act(act, b + 2, u % 2)
                act.wait_ge(s["y_done"], b + 1)
                if not (isinstance(b, int) and b < 2):
                    act.wait_ge(s["y_out"], 16 * b - 16)
                act.activation(y_sb[u % 2][:, 0:512], ps[4][:, :], ACT.Copy).then_inc(s["y_evA"], 1)
                copy_hT(act, b + 1, (u + 1) % 2)

            all_blocks(act, nblk, body)

        @block.vector
        def _(dve):
            dve.wait_ge(s["small_in"], 16)
            dve.tensor_scalar(st[:, 72:73], sml[:, S_QG:S_QG + 1], HD ** -0.5, None, ALU.mult).then_inc(s["qg_ready"], 1)
            for t in range(NT + 1):
                if t < NT:
                    norm_rows(dve, t, t, xr[t % 2], t >= 2 and ("h_T", t - 1), hr[t % 2])
                if t >= 1:
                    j = t - 1
                    dve.wait_ge(s["h_T"], j + 1)
                    dve.tensor_copy(hT[:, 4:8, P * j:P * j + P], ps[2 * (j % 2) + 1][:, :].rearrange("p (k t) -> p k t", k=4)).then_inc(s["hT_evD"], 1)
            for it in range(2 * NC):
                dve.wait_ge(s["sig_ready"], it + 1)
                dve.tensor_tensor(conv_in[:, it // 2, PAD + 512 * (it % 2):PAD + 512 * (it % 2) + 512], ps[4 + 2 * (it % 2)][:, :],
                                  half[it % 2], ALU.mult).then_inc(s["u_ready"], 1)
            dve.wait_ge(s["padded"], 2 * NC)
            dve.wait_ge(s["u_ready"], 2 * NC)
            dve.wait_ge(s["bias_ready"], 1)
            steps = 2 * NT + NT
            for i in range(steps):
                if i < 2 * NT:
                    par = i % 2
                    ss, rms, rs = (st[:, o + 8 * par:o + 8 * par + 8] for o in (24, 40, 56))
                    dve.wait_ge(s["sq_ready"], i + 1)
                    dve.tensor_reduce(ss, half[4 + par].rearrange("p (h d) -> p h d", h=HEADS), AX, ALU.add).then_inc(s["ss_ready"], 1)
                for n in range(i * NC * TAPS // steps, (i + 1) * NC * TAPS // steps):
                    tap(dve, n)
                if i < 2 * NT:
                    dve.wait_ge(s["qrms_ready"], i + 1)
                    dve.reciprocal(rs, rms).then_inc(s["qrstd_ready"], 1)
                    dve.wait_ge(s["qrstd_ready"], i + 1)
                    if i >= 2:
                        dve.wait_ge(s["qk_T"], i - 1)
                    dve.tensor_tensor(half[2 + par].rearrange("p (h d) -> p h d", h=HEADS), ps[par][:, :].rearrange("p (h d) -> p h d", h=HEADS),
                                      rs.unsqueeze(2).to_broadcast([P, HEADS, HD]), ALU.mult).then_inc(s["qn_ready"], 1)
            dve.wait_ge(s["conv_step"], NC * TAPS)
            dve.sem_inc(s["o_ev"], 4)
            dve.sem_inc(s["oT_ev"], 2)
            for a in range(PAIRS):
                bias_max(dve, a, a, WIN_H - 1)
            with dve.Fori(0, ROWS - 1) as r:
                d0 = dve.snap((window(r + 1) - r + (WIN_H - 2)).with_bounds(min_val=0, max_val=WIN_H - 1))
                for a in range(PAIRS):
                    it = r * PAIRS + a
                    dve.wait_ge(s["p_ready"], it + 3)
                    bias_max(dve, it + PAIRS, a, d0)
                    out_rows(dve, it, a)
                    if a:
                        out_cols(dve, it - 1, a - 1, r)
                out_cols(dve, it, 3, r)
            for a in range(PAIRS):
                it = (ROWS - 1) * PAIRS + a
                out_rows(dve, it, a)
                if a:
                    out_cols(dve, it - 1, a - 1, ROWS - 1)
            out_cols(dve, it, 3, ROWS - 1)
            for n in range(2):
                dve.wait_ge(s["mu_done"], n + 1)
                for c in range(NC):
                    u = conv_u[:, c, 512 * n:512 * n + 512]
                    dve.scalar_tensor_tensor(out=u, in0=ps[n][:, :], scalar=-1.0 / D_CONV, in1=u, op0=ALU.mult, op1=ALU.add).then_inc(s["cen_ready"], 1)
            for n in range(2):
                dve.wait_ge(s["sd_ready"], n + 1)
                dve.reciprocal(half[2 + n], half[n]).then_inc(s["lrstd_ready"], 1)
                dve.wait_ge(s["lrstd_ready"], n + 1)
                dve.wait_ge(s["cen_ready"], 2 * NC)
                for c in range(NC):
                    u = conv_u[:, c, 512 * n:512 * n + 512]
                    dve.tensor_tensor(u, u, half[2 + n], ALU.mult).then_inc(s["un_ready"], 1)
            for it in range(2 * KD):
                bank = 4 if it % 2 == 0 else 0
                for g in range(2):
                    dve.wait_ge(s["gates_ready"], 2 * it + g + 1)
                    dve.tensor_tensor(half[4 + 2 * g + it % 2], ps[bank + 2 + g][:, :], half[2 * g + it % 2], ALU.mult).then_inc(s["prod_ready"], 1)
                dve.wait_ge(s["prod_ready"], 2 * (it + 1))
                dve.tensor_tensor(merged[:, it // 2, 512 * (it % 2):512 * (it % 2) + 512], half[4 + it % 2], half[6 + it % 2], ALU.add
                                  ).then_inc(s["merged_ready"], 1)
            for i in range(NT + 2):
                if i < NT:
                    dve.wait_ge(s[f"x_in{i % 2}"], 16 * (NT // 2 + i // 2 + 1))
                    for n in range(2):
                        dve.wait_ge(s["xo_done"], 2 * i + n + 1)
                        dve.tensor_tensor(x2[:, i, 512 * n:512 * n + 512], ps[2 * (i % 2) + n][:, :], xr[i % 2][:, 512 * n:512 * n + 512], ALU.add
                                          ).then_inc(s["x2_ready"], 1)
                if 1 <= i <= NT:
                    j = i - 1
                    dve.wait_ge(s["x2_ready"], 2 * (j + 1))
                    norm_rows(dve, NT + j, j, x2[:, j, :], None, hr[j % 2].rearrange("p (k q) -> p q k", k=KD))
                if i >= 2:
                    j = i - 2
                    dve.wait_ge(s["h2_T"], j + 1)
                    dve.tensor_copy(h2T[:, 4:8, P * j:P * j + P], ps[5][:, :].rearrange("p (k t) -> p k t", k=4)).then_inc(s["h2T_evD"], 1)
            dve.memset(blk_i[:, :], 0).then_inc(s["rt_step"], 1)
            dve.memset(r_gs[:, GROUPS:12], NEG).then_inc(s["rt_step"], 1)
            dve.memset(r_rep[:, 4:8], NEG).then_inc(s["rt_step"], 1)
            count = [3]

            def step(ins):
                count[0] += 1
                ins.then_inc(s["rt_step"], 1)
                dve.wait_ge(s["rt_step"], count[0])

            dve.wait_ge(s["rt_step"], 3)
            dve.wait_ge(s["misc_in"], 80)
            dve.wait_ge(s["scores_ready"], 1)
            for t in range(NT + 1):
                if t < NT:
                    dve.wait_ge(s["shs_ready"], t + 1)
                    if t >= 2:
                        dve.wait_ge(s["shT_done"], t - 1)
                    dve.tensor_tensor(hs2[t % 2].rearrange("p (k q) -> p q k", k=KF), ps[t % 2][:, F:2 * F].rearrange("p (q k) -> p q k", k=KF),
                                      silu2[t % 2].rearrange("p (q k) -> p q k", k=KF), ALU.mult).then_inc(s["shh_ready"], 1)
                    route(dve, step, t)
                if t >= 1:
                    j = t - 1
                    for n in range(2):
                        dve.wait_ge(s["shd_done"], 2 * j + n + 1)
                        dve.tensor_tensor(x2[:, j, 512 * n:512 * n + 512], ps[2 + n][:, :], x2[:, j, 512 * n:512 * n + 512], ALU.add
                                          ).then_inc(s["acc_ready"], 1)
            dve.wait_ge(s["cum_done"], 1)
            step(dve.tensor_scalar(r_nb_i, ps[5][:, 0:EXP], float(P - 1), None, ALU.add))
            step(dve.tensor_scalar(r_nb_i, r_nb_i, 7, None, ALU.logical_shift_right))
            step(dve.tensor_scalar(r_nb, r_nb_i, 1.0, None, ALU.max))
            step(dve.tensor_tensor_scan(r_end, ones[:, 0:EXP], r_nb, 0.0, ALU.mult, ALU.add))
            step(dve.tensor_scalar(r_le, r_end, cst[:, C_PID:C_PID + 1], None, ALU.is_le))
            step(dve.tensor_reduce(r_eb, r_le, AX, ALU.add))
            dve.tensor_scalar(r_eb, r_eb, float(EXP - 1), None, ALU.min).then_inc(s["tab_ready"], 1)
            dve.tensor_copy(end_i[:, :], r_end).then_inc(s["tab_ready"], 1)
            step(dve.tensor_tensor(r_start, r_end, r_nb, ALU.subtract))
            step(dve.tensor_scalar(r_start, r_start, float(P), 1.0, ALU.mult, ALU.add))
            key3 = slot_key.rearrange("p (t e) -> p t e", t=NT)
            sel3 = sel.rearrange("p (t e) -> p t e", t=NT)
            step(dve.tensor_tensor(key3, ps[4][:, :].rearrange("p (t e) -> p t e", t=NT), r_start.unsqueeze(1).to_broadcast([P, NT, EXP]), ALU.add))
            step(dve.tensor_tensor(slot_key, slot_key, sel, ALU.mult))
            step(dve.tensor_scalar(slot_key, slot_key, -1.0, None, ALU.add))
            dve.wait_ge(s["blk_done"], 1)
            dve.tensor_copy(blk_i[0:1, 0:MAXBLK], ps[5][0:1, P:P + MAXBLK]).then_inc(s["tab_ready"], 1)
            dve.wait_ge(s["tab_ready"], 3)
            nblk = dve.value_load(end_i[0:1, EXP - 1:EXP], min_val=0, max_val=MAXBLK)
            dve.sem_inc(s["hs_ready"], 1)
            dve.sem_inc(s["y_evD"], 1)
            one_hot(dve, 0, 0)
            one_hot(dve, 1, 1)
            slot_rows(dve, 0, 0)
            one_hot(dve, 2, 0)
            slot_rows(dve, 1, 1)
            one_hot(dve, 3, 1)
            slot_rows(dve, 2, 2)
            copy_xT_dve(dve, 0, 0)
            weigh(dve, 0, 0)
            copy_xT_dve(dve, 1, 1)

            def body(b, u):
                weigh(dve, b + 1, (u + 1) % 4)
                slot_rows(dve, b + 3, (u + 3) % 4)
                copy_xT_dve(dve, b + 2, u % 2)
                one_hot(dve, b + 4, u % 2)
                dve.wait_ge(s["y_done"], b + 1)
                if not (isinstance(b, int) and b < 2):
                    dve.wait_ge(s["y_out"], 16 * b - 16)
                dve.tensor_copy(y_sb[u % 2][:, 512:1024], ps[5][:, :]).then_inc(s["y_evD"], 1)

            all_blocks(dve, nblk, body)


def _constants():
    p = np.arange(P)
    c = np.zeros((P, C_END), np.float32)
    c[:, C_ID:C_ID + P] = np.eye(P)
    c[:, C_TRI:C_TRI + P] = p[:, None] < p[None, :]
    c[:, C_ONE:C_ONE + P] = 1.0
    c[:, C_IOTA:C_IOTA + P] = p[None, :]
    q = p % GRID_W
    start = np.clip(q - WIN_W // 2, 0, GRID_W - WIN_W)
    col = np.arange(GRID_W)[None, :]
    c[:, C_MASK:C_MASK + GRID_W] = (col >= start[:, None]) & (col < start[:, None] + WIN_W)
    t = np.arange(NT)[None, :]
    c[:, C_ROW:C_ROW + NT] = P * t + p[:, None] - BIG
    c[:, C_EMPTY] = T + p
    c[:, C_EPS] = EPS
    c[:, C_PID] = p
    c[:, C_BASE:C_BASE + MAXBLK + 4] = P * np.arange(MAXBLK + 4)[None, :]
    return c


def kernel(x, norm_mix_g, w_in, q_norm_g, k_norm_g, rpb, conv_dw_w, conv_dw_b, conv_ln_g, conv_ln_b, w_conv_out,
           w_attn_out, w_o, norm_ffn_g, w_router, router_bias, w_exp_gate, w_exp_up, w_exp_down, w_sh_gate, w_sh_up, w_sh_down):
    import concourse.bacc as bacc
    from concourse.bass_utils import run_bass_kernel_spmd

    def chan(v):
        return np.asarray(v).reshape(NC, P, -1).transpose(1, 0, 2).reshape(P, -1)

    small = np.concatenate([chan(np.asarray(conv_dw_w)[0, :, 0, :].T), chan(conv_dw_b[0]), chan(conv_ln_g[0]), chan(conv_ln_b[0]),
                            np.tile(np.asarray(q_norm_g)[0], 2)[:, None], np.tile(np.asarray(k_norm_g)[0], 2)[:, None]], axis=1)
    rpb_rev = np.pad(np.asarray(rpb)[0, :, :, ::-1].reshape(-1), RPB_PAD)
    arrays = {
        "x": np.asarray(x)[0], "w_in": np.asarray(w_in)[0], "w_conv_out": np.asarray(w_conv_out)[0],
        "w_attn_out": np.asarray(w_attn_out)[0], "w_o": np.asarray(w_o)[0], "w_router": np.asarray(w_router)[0],
        "w_gate": np.asarray(w_exp_gate)[0], "w_up": np.asarray(w_exp_up)[0], "w_down": np.asarray(w_exp_down)[0],
        "w_sh_gate": np.asarray(w_sh_gate)[0], "w_sh_up": np.asarray(w_sh_up)[0], "w_sh_down": np.asarray(w_sh_down)[0],
        "mix_g": np.asarray(norm_mix_g)[0], "ffn_g": np.asarray(norm_ffn_g)[0], "router_bias": np.asarray(router_bias)[0],
        "rpb_rev": rpb_rev, "small": small, "consts": _constants(),
    }
    arrays = {k: np.ascontiguousarray(v) for k, v in arrays.items()}
    nc = bacc.Bacc("TRN2", target_bir_lowering=False, num_devices=1)
    args = [nc.dram_tensor(k, v.shape, mybir.dt.from_np(v.dtype), kind="ExternalInput").ap() for k, v in arrays.items()]
    out = nc.dram_tensor("out", (T + P, D), F32, kind="ExternalOutput").ap()
    build(nc, *args, out)
    r = run_bass_kernel_spmd(nc, [arrays], core_ids=[0])
    return r.results[0]["out"][:T].reshape(1, T, D)
```

```python
from contextlib import ExitStack, nullcontext

import numpy as np

import concourse.bass as bass
from concourse import mybir

P = 128
T = 1024
D = 1024
NT = T // P
KD = D // P
D_CONV = 512
NC = D_CONV // P
TAPS = 31
PAD = TAPS // 2
CPAD = T + 2 * PAD
HEADS = 8
HD = 64
D_ATTN = HEADS * HD
PAIRS = HEADS // 2
GRID_W = 64
ROWS = T // GRID_W
WIN_H = 8
WIN_W = 16
WKEYS = WIN_H * GRID_W
RELH = 2 * WIN_H - 1
RELW = 2 * WIN_W - 1
RPB_PAD = 64
EXP = 64
GROUPS = 8
PER_GROUP = EXP // GROUPS
TOP_K = 8
F = 256
KF = F // P
WEXP = (2 * KD * F) + KF * D
MAXBLK = T * TOP_K // P + EXP
NBUF = 4
ROUTE_SCALE = 2.5
EPS = 1e-6
BIG = 65536.0
NEG = -1e30

ALU = mybir.AluOpType
ACT = mybir.ActivationFunctionType
F32 = mybir.dt.float32
I32 = mybir.dt.int32
BF16 = mybir.dt.bfloat16
SLOTC = 6
AX = mybir.AxisListType.X

C_ID, C_TRI, C_ONE, C_IOTA, C_MASK, C_ROW, C_EPS, C_PID, C_EMPTY, C_BASE = 0, 128, 256, 384, 512, 576, 584, 585, 586, 587
C_END = C_BASE + MAXBLK + 4
S_DW, S_DB, S_LG, S_LB, S_QG, S_KG, S_END = 0, NC * TAPS, NC * TAPS + 4, NC * TAPS + 8, NC * TAPS + 12, NC * TAPS + 13, NC * TAPS + 14


def build(nc, x, w_in, w_conv_out, w_attn_out, w_o, w_router, w_gate, w_up, w_down,
          w_sh_gate, w_sh_up, w_sh_down, mix_g, ffn_g, router_bias, rpb_rev, small, consts, out):
    with ExitStack() as ctx:
        def sb(name, cols, dt=F32):
            return ctx.enter_context(nc.sbuf_tensor(name, [P, cols], dt))

        def sem(name):
            return ctx.enter_context(nc.semaphore(name))

        h2_rows = nc.dram_tensor("h2_rows", [T, D], F32).ap()

        arena = sb("arena", 24704)
        qT = arena[:, 0:4096].rearrange("p (a t) -> p a t", a=PAIRS)
        kT = arena[:, 4096:8192].rearrange("p (a t) -> p a t", a=PAIRS)
        x_first = arena[:, 0:8192].rearrange("p (t d) -> p t d", t=NT)
        attnT = arena[:, 0:4096].rearrange("p (a t) -> p a t", a=PAIRS)
        merged = arena[:, 8192:16384].rearrange("p (m t) -> p m t", m=KD)
        v_rows = arena[:, 8192:16384].rearrange("p (s n) -> p s n", n=D_ATTN)
        wo_sb = arena[:, 0:8192].rearrange("p (k n) -> p k n", k=KD)
        conv_in = arena[:, 16384:16384 + NC * CPAD].rearrange("p (c t) -> p c t", c=NC)
        conv_u = arena[:, 20608:24704].rearrange("p (c t) -> p c t", c=NC)
        rpb_raw = arena[:, 20608:20608 + PAIRS * RELH * GRID_W]
        h2T = arena[:, 16384:24576].rearrange("p (k t) -> p k t", k=KD)

        hx = sb("hx", 8192)
        hT = hx[:, :].rearrange("p (k t) -> p k t", k=KD)
        x2 = hx[:, :].rearrange("p (t d) -> p t d", t=NT)

        bias_t = sb("bias_t", PAIRS * RELH * GRID_W)
        biasT = bias_t[:, :].rearrange("p (a r c) -> p a r c", a=PAIRS, r=RELH)
        slot_key = bias_t[:, 0:512]
        weight = bias_t[:, 1024:1536]
        hs2 = [bias_t[:, 1536 + F * i:1536 + F * (i + 1)] for i in range(2)]
        hsT2 = [bias_t[:, 2048 + F * i:2048 + F * (i + 1)] for i in range(2)]
        silu2 = [bias_t[:, 2560 + F * i:2560 + F * (i + 1)] for i in range(2)]
        rt = bias_t[:, 3072:3840]

        wring = sb("wring", 8192)
        wchunk = [wring[:, 4096 * i:4096 * (i + 1)] for i in range(2)]
        onehot = [wring[:, 512 * i:512 * (i + 1)].bitcast(BF16).rearrange("p (t j) -> p t j", t=NT) for i in range(2)]
        slot_tab = wring[:, 4096:4096 + NT * EXP * SLOTC // 2].bitcast(BF16)
        y_sb = [wring[:, 2048 + 1024 * i:2048 + 1024 * (i + 1)] for i in range(2)]
        wr_sb = wring[:, 4096 + 2048:4096 + 2048 + 512].rearrange("p (k e) -> p k e", k=KD)
        wshd_sb = wring[:, 4096:4096 + 2048].rearrange("p (k n) -> p k n", k=KF)
        wshgu_sb = wring[:, 0:4096].rearrange("p (g k f) -> p g k f", g=2, k=KD)

        xr_t = sb("xr_t", 2048)
        hr_t = sb("hr_t", 2048)
        xr = [xr_t[:, D * i:D * (i + 1)] for i in range(2)]
        hr = [hr_t[:, D * i:D * (i + 1)] for i in range(2)]
        half = [xr_t[:, 512 * i:512 * (i + 1)] for i in range(4)] + [hr_t[:, 512 * i:512 * (i + 1)] for i in range(4)]
        gate_row = sb("gate_row", D)
        rb_row = sb("rb_row", EXP)
        cst = sb("cst", C_END)
        sml = sb("sml", S_END)
        ident = cst[:, C_ID:C_ID + P]
        tri = cst[:, C_TRI:C_TRI + P]
        ones = cst[:, C_ONE:C_ONE + P]
        iota = cst[:, C_IOTA:C_IOTA + P]
        wmask = cst[:, C_MASK:C_MASK + GRID_W]
        row_less_big = cst[:, C_ROW:C_ROW + NT]
        eps = cst[:, C_EPS:C_EPS + 1]
        st = sb("st", 160)
        qblk = [sb(f"qblk{i}", P) for i in range(2)]
        osb = [sb(f"osb{i}", P) for i in range(2)]
        blk_i = sb("blk_i", MAXBLK + 8, I32)
        end_i = sb("end_i", EXP, I32)
        idx_i = sb("idx_i", 16, I32)
        to_i = sb("to_i", 8, I32)
        nb_i = sb("nb_i", EXP, I32)
        slot_w2 = sb("slot_w2", 8)[:, :].rearrange("p (a u) -> p a u", a=2)

        ps = [ctx.enter_context(nc.psum_tensor(f"ps{i}", [P, 512], F32)) for i in range(8)]

        s = {n: sem(n) for n in """const_in small_in row_in rpb_in x_in0 x_in1 x0_in x1_in x2_in x3_in x4_in x5_in x6_in x7_in w_in0 w_in1 wo_in vo_in misc_in
            ssq_ready rms_ready rstd_ready h_ready h_T hT_evA hT_evD
            ag_done sig_ready u_ready padded conv_step bias_ready bias_step bias_m
            qk_done sq_ready ss_ready qg_ready qrms_ready qrstd_ready qn_ready qk_T qk_ev v_done v_ev
            qz_ready qblk_ready s_done s_biased negmax_ready p_ready rowinv_ready pT_done pT_ev o_done o_ev oT_done oT_ev
            mu_done cen_ready csq_ready var_done sd_ready lrstd_ready un_ready uT_ready
            m_done gates_ready prod_ready merged_ready
            xo_done x2_ready h2_out h2_T h2T_evA h2T_evD r_done scores_ready
            sh_done shs_ready shh_ready shT_done shT_ev shd_done acc_ready
            rt_step sel_ready cum_done blk_done tab_ready
            oh_step oh_ready idx_done idx_step xg_in0 xg_in1 xT_done xT_evA xT_evD gu_done silu_ready hs_ready
            hsT_done hsT_ev y_done y_evA y_evD y_out to_ready wl0 wl1 w_ready acc_out row_parts weight_ready weight_parts""".split()}

        def gchunk(slot, part, m):
            c = wchunk[slot]
            c = c[:, 0:2 * KD * P].rearrange("p (k n) -> p k n", k=KD) if part == "gate" else c[:, 2 * KD * P:2 * (KD + NC) * P].rearrange("p (k n) -> p k n", k=NC)
            return c[:, :, P * (m % 2):P * (m % 2) + P]

        w_in_k = w_in.rearrange("(k p) n -> p k n", p=P)
        co_k = w_conv_out.rearrange("(k p) n -> p k n", p=P)
        ao_k = w_attn_out.rearrange("(k p) n -> p k n", p=P)
        x_t = x.rearrange("(t p) d -> t p d", p=P)
        out_t = out.rearrange("(t p) d -> t p d", p=P)
        h2_t = h2_rows.rearrange("(t p) d -> t p d", p=P)
        Q0, K0, V0, GA0, GB0 = 1024, 1536, 2048, 2560, 3584

        plain = [[(0, 256), (512, 256)], [(256, 256), (768, 256)], [(Q0, 512)], [(K0, 512)], [(V0, 512)]]
        NPLAIN = len(plain)
        wload = [0, 0]
        chunk_at = []
        for i in range(NPLAIN + KD):
            n = len(plain[i]) if i < NPLAIN else 2
            slot = i % 2
            wload[slot] += 16 * n
            chunk_at.append((slot, wload[slot]))

        def chunk_used(eng, i):
            if i < NPLAIN:
                name, n = (("ag_done", NC), ("ag_done", 2 * NC), ("qk_done", NT), ("qk_done", 2 * NT), ("v_done", NT))[i]
            else:
                name, n = "m_done", 4 * (i - NPLAIN + 1)
            eng.wait_ge(s[name], n)

        def chunk_here(eng, i):
            eng.wait_ge(s[f"w_in{chunk_at[i][0]}"], chunk_at[i][1])

        def arena_w(e4, part):
            base = e4 * WEXP
            if part == "gu":
                return arena[:, bass.ds(base, 2 * KD * F)].rearrange("p (g k f) -> p g k f", g=2, k=KD)
            return arena[:, bass.ds(base + 2 * KD * F, KF * D)].rearrange("p (k n) -> p k n", k=KF)

        AG_STEPS = [(0, 0), (1, 0), (0, 1), (1, 1), (2, 0), (2, 1), (3, 0), (3, 1)]

        LN_STEP = 10

        scores = xr_t[:, 0:512]
        biased = xr_t[:, 512:1024]
        masked = xr_t[:, 1024:1536]
        sel = xr_t[:, 1536:2048]
        ringfree = wring[:, 6656:8192]
        r_top = ringfree[:, 0:EXP]
        r_gs = ringfree[:, 64:76]
        r_go = ringfree[:, 80:92]
        r_rep = ringfree[:, 96:104]
        r_t8 = ringfree[:, 104:112]
        r_gm = ringfree[:, 112:120]
        r_gn = ringfree[:, 120:128]
        r_mo = ringfree[:, 128:192]
        r_sum = ringfree[:, 192:193]
        r_inv = ringfree[:, 193:194]
        r_eb = ringfree[:, 194:195]
        r_nb = ringfree[:, 256:320]
        r_end = ringfree[:, 320:384]
        r_nb_i = nb_i[:, :]
        r_start = ringfree[:, 384:448]
        r_le = ringfree[:, 448:512]
        r_key = ringfree[:, 512:1024]
        gcol = [st[:, 104 + 8 * i:112 + 8 * i] for i in range(2)]

        def load_plain(sp, i):
            slot = chunk_at[i][0]
            c = wchunk[slot].rearrange("p (k n) -> p k n", k=KD)
            at = 0
            for c0, n in plain[i]:
                sp.dma_start(c[:, :, at:at + n], w_in_k[:, :, c0:c0 + n]).then_inc(s[f"w_in{slot}"], 16)
                at += n

        def load_gates(sp, g):
            i = NPLAIN + g
            chunk_used(sp, i - 2)
            slot = chunk_at[i][0]
            c = wchunk[slot]
            c0 = 2 * P * (g % 4)
            gate0, w_k = ((GB0, ao_k), (GA0, co_k))[g // 4]
            sp.dma_start(c[:, 0:2 * KD * P].rearrange("p (k n) -> p k n", k=KD), w_in_k[:, :, gate0 + c0:gate0 + c0 + 2 * P]).then_inc(s[f"w_in{slot}"], 16)
            sp.dma_start(c[:, 2 * KD * P:2 * (KD + NC) * P].rearrange("p (k n) -> p k n", k=NC), w_k[:, :, c0:c0 + 2 * P]).then_inc(s[f"w_in{slot}"], 16)

        def load_expert(sp, e, buf, par):
            gu = arena_w(buf, "gu")
            for g, w in ((0, w_gate), (1, w_up)):
                sp.dma_start(gu[:, g].rearrange("p k f -> p (k f)"), w[bass.ds(e, 1)].rearrange("e (p k) f -> p (e k f)", k=KD)
                             ).then_inc(s[f"wl{par}"], 16)
            sp.dma_start(arena_w(buf, "dn").rearrange("p k n -> p (k n)"), w_down[bass.ds(e, 1)].rearrange("e (p k) n -> p (e k n)", k=KF)
                         ).then_inc(s[f"wl{par}"], 16)

        def expert_here(sp, e, par):
            if isinstance(e, int):
                v = 48 * (e // 2 + 1)
            else:
                v = 24 * e + (48 if par == 0 else 24)
            sp.wait_ge(s[f"wl{par}"], v)
            sp.sem_inc(s["w_ready"], 1)

        def query_block(pool, r, a):
            for hh in range(2):
                pr = slice(64 * hh, 64 * hh + 64)
                pool.tensor_copy(qblk[a % 2][pr, 64 * hh:64 * hh + 64], qT[pr, a, bass.ds(r * GRID_W, GRID_W)]
                                 ).then_inc(s["qblk_ready"], 1)

        def gather(pool, b, u, last_token):
            if isinstance(b, int):
                pool.wait_ge(s["idx_step"], 3 * b + 3)
                if b >= 2:
                    pool.wait_ge(s["xT_done"], b - 1)
            else:
                steps, turned = pool.to_reg(3 * b + 3), pool.to_reg(b - 1)
                pool.wait_ge(s["h2_out"], 16 * NT)
                pool.wait_ge(s["idx_step"], steps)
                pool.wait_ge(s["xT_done"], turned)
            pool.indirect_dma_start(hr[u % 2], None, h2_rows, bass.IndirectOffsetOnAxis(ap=idx_i[:, u:u + 1], axis=0),
                                    bounds_check=last_token, oob_is_err=False).then_inc(s[f"xg_in{u % 2}"], 16)

        def expert_of(eng, b):
            return eng.value_load(blk_i[0:1, bass.ds(b, 1)], min_val=0, max_val=EXP - 1)

        def window(r):
            if isinstance(r, int):
                return min(max(r - WIN_H // 2, 0), ROWS - WIN_H)
            first = (r > WIN_H // 2) * (r - WIN_H // 2) - (r > ROWS - WIN_H // 2) * (r - (ROWS - WIN_H // 2))
            return first.with_bounds(min_val=0, max_val=ROWS - WIN_H)

        def value_tile(r0):
            return (r0 % 2) * NT + r0 // 2

        def key_start(pe, r):
            return window(r) * GRID_W if isinstance(r, int) else pe.snap(window(r) * GRID_W)

        def value_start(pe, r):
            if isinstance(r, int):
                return value_tile(window(r)) * D_ATTN
            return pe.snap(value_tile(pe.snap(window(r))) * D_ATTN)

        def all_rows(eng, row):
            row(0, first=True)
            with eng.Fori(0, (ROWS - 2) // 2) as q:
                row(q * 2 + 1)
                row(q * 2 + 2)
            row(ROWS - 1, last=True)

        def score(pe, it, a, k0):
            pe.wait_ge(s["qblk_ready"], 2 * it + 2)
            mm = pe.matmul(ps[a][:, :], qblk[a % 2][:, :], kT[:, a, bass.ds(k0, WKEYS)], start=True, stop=True)
            mm.then_inc(s["s_done"], 1)

        def turn_p(pe, it, a):
            pe.wait_ge(s["p_ready"], it + 3)
            pe.wait_ge(s["pT_ev"], it + 1)
            for j in range(4):
                mm = pe.transpose(ps[4 + a % 2][:, P * j:P * j + P], half[4 + a % 2][:, P * j:P * j + P], ident)
            mm.then_inc(s["pT_done"], 1)

        def values(pe, it, a, v0):
            pe.wait_ge(s["pT_ev"], it + 3)
            pe.wait_ge(s["o_ev"], it + 4)
            for j in range(4):
                mm = pe.matmul(ps[6][:, 0:P], half[6 + a % 2][:, P * j:P * j + P],
                               arena[:, bass.ds(v0 + (8192 + j * D_ATTN + a * P), P)], start=(j == 0), stop=(j == 3))
            mm.then_inc(s["o_done"], 1)

        def turn_o(pe, it, a):
            pe.wait_ge(s["o_ev"], it + 5)
            pe.wait_ge(s["oT_ev"], 2 * it + 2)
            pe.transpose(ps[7][:, 0:P], osb[a % 2][:, :], ident).then_inc(s["oT_done"], 1)

        def slots(pe, b, par, e):
            pe.wait_ge(s["oh_ready"], b + 1)
            if not (isinstance(b, int) and b == 0):
                pe.wait_ge(s["idx_step"], 3 * b)
            for t in range(NT):
                mm = pe.matmul(ps[7][:, 256:256 + SLOTC], onehot[par][:, t, :], slot_tab[:, bass.ds(SLOTC * e + SLOTC * EXP * t, SLOTC)],
                               start=(t == 0), stop=(t == NT - 1))
            mm.then_inc(s["idx_done"], 1)

        def turn_x(pe, b, par):
            pe.wait_ge(s[f"xg_in{par}"], 8 * b + (16 if par == 0 else 8))
            if not (isinstance(b, int) and b == 0):
                pe.wait_ge(s["xT_evA"], b)
                pe.wait_ge(s["xT_evD"], b)
            for k in range(KD):
                mm = pe.transpose(ps[k // 4][:, P * (k % 4):P * (k % 4) + P], hr[par][:, k * P:(k + 1) * P], ident)
            mm.then_inc(s["xT_done"], 1)

        def gate_up(pe, b, par, e):
            pe.wait_ge(s["w_ready"], e + 1)
            pe.wait_ge(s["xT_evA"], b + 1)
            pe.wait_ge(s["xT_evD"], b + 1)
            if not (isinstance(b, int) and b == 0):
                pe.wait_ge(s["hs_ready"], b)
            for k in range(KD):
                mm = pe.matmul(ps[2 + par][:, :], xr[par][:, k * P:(k + 1) * P], gu_cols(e, k), start=(k == 0), stop=(k == KD - 1))
            mm.then_inc(s["gu_done"], 1)

        def turn_h(pe, b, par):
            pe.wait_ge(s["hs_ready"], b + 2)
            pe.wait_ge(s["hsT_ev"], b + 1)
            for k in range(KF):
                mm = pe.transpose(ps[6][:, P * k:P * k + P], hs2[par][:, P * k:P * k + P], ident)
            mm.then_inc(s["hsT_done"], 1)

        def down(pe, b, par, e):
            pe.wait_ge(s["hsT_ev"], b + 2)
            pe.wait_ge(s["y_evA"], b + 1)
            pe.wait_ge(s["y_evD"], b + 1)
            for n in range(2):
                for k in range(KF):
                    mm = pe.matmul(ps[4 + n][:, :], hsT2[par][:, P * k:P * k + P], dn_cols(e, k, n), start=(k == 0), stop=(k == KF - 1))
            mm.then_inc(s["y_done"], 1)

        def gu_cols(e, k):
            buf = (e % NBUF) * WEXP
            return arena[:, bass.ds(buf + k * F, KD * F + F)].rearrange("p (a f) -> p a f", f=F)[:, ::KD, :]

        def dn_cols(e, k, n):
            return arena[:, bass.ds((e % NBUF) * WEXP + (2 * KD * F + k * D + 512 * n), 512)]

        def rms_act(act, count, t, src):
            act.activation(hr[t % 2], src, ACT.Square, accum_out=st[:, t:t + 1]).then_inc(s["ssq_ready"], 1)
            act.wait_ge(s["ssq_ready"], count + 1)
            act.activation(st[:, 8 + t:9 + t], st[:, t:t + 1], ACT.Sqrt, bias=eps, scale=1.0 / D).then_inc(s["rms_ready"], 1)

        def hT_act(act, t):
            act.wait_ge(s["h_T"], t + 1)
            act.activation(hT[:, 0:4, P * t:P * t + P], ps[2 * (t % 2)][:, :].rearrange("p (k t) -> p k t", k=4), ACT.Copy).then_inc(s["hT_evA"], 1)

        def copy_pT(act, it, a):
            act.wait_ge(s["pT_done"], it + 3)
            act.wait_ge(s["o_done"], it + 1)
            act.activation(half[6 + a % 2], ps[4 + a % 2][:, :], ACT.Copy).then_inc(s["pT_ev"], 1)

        def copy_xT_act(act, b, par):
            act.wait_ge(s["xT_done"], b + 1)
            if not (isinstance(b, int) and b == 0):
                act.wait_ge(s["gu_done"], b)
            act.activation(xr[par][:, 0:512], ps[0][:, :], ACT.Copy).then_inc(s["xT_evA"], 1)

        def copy_hT(act, b, par):
            act.wait_ge(s["hsT_done"], b + 2)
            act.activation(hsT2[par], ps[6][:, 0:F], ACT.Copy).then_inc(s["hsT_ev"], 1)

        def store_acc(act, j):
            act.wait_ge(s["acc_ready"], 2 * (j + 1))
            act.dma_start(out_t[j], x2[:, j, :]).then_inc(s["acc_out"], 16)

        def all_blocks(eng, nblk, body):
            for u in range(4):
                body(u, u)
            with eng.Fori(1, MAXBLK // 4) as q:
                with eng.If(nblk > q * 4):
                    for u in range(4):
                        body(q * 4 + u, u)

        def silu_act(act, b, par):
            act.wait_ge(s["gu_done"], b + 2)
            if not (isinstance(b, int) and b == 0):
                act.wait_ge(s["hs_ready"], b)
            act.activation(silu2[par], ps[2 + par][:, 0:F], ACT.Silu).then_inc(s["silu_ready"], 1)

        def norm_rows(dve, count, t, src, free, dst):
            dve.wait_ge(s["rms_ready"], count + 1)
            dve.reciprocal(st[:, 16 + t:17 + t], st[:, 8 + t:9 + t]).then_inc(s["rstd_ready"], 1)
            dve.wait_ge(s["rstd_ready"], count + 1)
            dve.wait_ge(s["row_in"], 16 * (count // NT + 1))
            if free:
                dve.wait_ge(s[free[0]], free[1])
            dve.scalar_tensor_tensor(out=dst, in0=src, scalar=st[:, 16 + t:17 + t], in1=gate_row[:, :], op0=ALU.mult, op1=ALU.mult
                                     ).then_inc(s["h_ready"], 1)

        def tap(dve, n):
            c, j = divmod(n, TAPS)
            w = sml[:, S_DW + c * TAPS + j:S_DW + c * TAPS + j + 1]
            src = conv_in[:, c, j:j + T]
            if j == 0:
                dve.tensor_scalar(conv_u[:, c, :], src, w, sml[:, S_DB + c:S_DB + c + 1], ALU.mult, ALU.add).then_inc(s["conv_step"], 1)
            else:
                dve.wait_ge(s["conv_step"], n)
                dve.scalar_tensor_tensor(out=conv_u[:, c, :], in0=src, scalar=w, in1=conv_u[:, c, :], op0=ALU.mult, op1=ALU.add).then_inc(s["conv_step"], 1)

        def tap_start(i):
            return min(3 * min(i, 2 * NT) + 5 * min(max(i - 2 * NT, 0), NT) + 4 * max(i - 3 * NT, 0), NC * TAPS)

        def bias_max(dve, it, a, d0):
            dve.wait_ge(s["s_done"], it + 1)
            dve.tensor_tensor(half[a].rearrange("p (r c) -> p r c", r=WIN_H), ps[a][:, :].rearrange("p (r c) -> p r c", r=WIN_H),
                              biasT[:, a, bass.ds(d0, WIN_H), :], ALU.add).then_inc(s["s_biased"], 1)
            dve.wait_ge(s["s_biased"], it + 1)
            dve.tensor_reduce(st[:, 80 + a:81 + a], half[a], AX, ALU.max, negate=True).then_inc(s["negmax_ready"], 1)

        def out_rows(dve, it, a):
            dve.wait_ge(s["p_ready"], it + 3)
            dve.reciprocal(st[:, 96 + a:97 + a], st[:, 88 + a:89 + a]).then_inc(s["rowinv_ready"], 1)
            dve.wait_ge(s["rowinv_ready"], it + 1)
            dve.wait_ge(s["o_done"], it + 3)
            dve.wait_ge(s["oT_done"], it + 1)
            dve.tensor_scalar(osb[a % 2][:, :], ps[6][:, 0:P], st[:, 96 + a:97 + a], None, ALU.mult).then_inc(s["o_ev"], 1)

        def out_cols(dve, it, a, r):
            dve.wait_ge(s["oT_done"], it + 3)
            for hh in range(2):
                pr = slice(64 * hh, 64 * hh + 64)
                dve.tensor_copy(attnT[pr, a, bass.ds(r * GRID_W, GRID_W)], ps[7][pr, 64 * hh:64 * hh + 64]
                                ).then_inc(s["oT_ev"], 1)

        def route(dve, step, t):
            sc, bi, ma, se = (v[:, EXP * t:EXP * t + EXP] for v in (scores, biased, masked, sel))
            step(dve.tensor_tensor(bi, sc, rb_row[:, :], ALU.add))
            for g in range(GROUPS):
                m = dve.max(r_top[:, 8 * g:8 * g + 8], bi[:, PER_GROUP * g:PER_GROUP * (g + 1)])
                step(m)
            top = r_top.rearrange("p (g j) -> p g j", g=GROUPS)
            step(dve.tensor_tensor(r_gs[:, 0:GROUPS], top[:, :, 0], top[:, :, 1], ALU.add))
            step(dve.max(r_t8, r_gs[:, 0:GROUPS]))
            step(dve.tensor_copy(r_rep[:, 0:4], r_t8[:, 0:4]))
            step(dve.match_replace(r_go, r_rep, r_gs, 3.0 * NEG))
            step(dve.tensor_tensor(r_gm, r_go[:, 0:GROUPS], r_gs[:, 0:GROUPS], ALU.is_lt))
            step(dve.tensor_scalar(r_gn, r_gm, 1.0, -NEG, ALU.subtract, ALU.mult))
            ma3 = ma.rearrange("p (g j) -> p g j", g=GROUPS)
            step(dve.tensor_tensor(ma3, bi.rearrange("p (g j) -> p g j", g=GROUPS), r_gm.unsqueeze(2).to_broadcast([P, GROUPS, PER_GROUP]), ALU.mult))
            step(dve.tensor_tensor(ma3, ma3, r_gn.unsqueeze(2).to_broadcast([P, GROUPS, PER_GROUP]), ALU.add))
            step(dve.max(r_t8, ma))
            step(dve.match_replace(r_mo, r_t8, ma, 3.0 * NEG))
            dve.tensor_tensor(se, r_mo, ma, ALU.is_lt).then_inc(s["sel_ready"], 1)
            dve.wait_ge(s["sel_ready"], t + 1)
            step(dve.tensor_tensor(r_mo, sc, se, ALU.mult))
            step(dve.tensor_reduce(r_sum, r_mo, AX, ALU.add))
            step(dve.reciprocal(r_inv, r_sum))
            dve.tensor_scalar(weight[:, EXP * t:EXP * t + EXP], r_mo, r_inv, ROUTE_SCALE, ALU.mult, ALU.mult).then_inc(s["weight_ready"], 1)

        def one_hot(dve, b, par):
            e = 0 if isinstance(b, int) and b == 0 else expert_of(dve, b)
            keys = slot_key.rearrange("p (t e) -> p e t", t=NT)[:, bass.ds(e, 1), :].rearrange("p e t -> p (e t)")
            dve.tensor_scalar(gcol[par], keys, cst[:, bass.ds(C_BASE + b, 1)], None, ALU.subtract).then_inc(s["oh_step"], 1)
            dve.wait_ge(s["oh_step"], b + 1)
            if not (isinstance(b, int) and b < 2):
                dve.wait_ge(s["idx_done"], b - 1)
            dve.tensor_tensor(onehot[par], gcol[par].unsqueeze(2).to_broadcast([P, NT, P]), iota.unsqueeze(1).to_broadcast([P, NT, P]), ALU.is_equal
                              ).then_inc(s["oh_ready"], 1)

        def slot_rows(dve, b, u):
            dve.wait_ge(s["idx_done"], b + 1)
            if not (isinstance(b, int) and b < 4):
                dve.wait_ge(s["to_ready"], b - 3)
            dve.tensor_reduce(slot_w2[:, :, u], ps[7][:, 256:256 + SLOTC].rearrange("p (a c) -> p a c", a=2), AX, ALU.add).then_inc(s["idx_step"], 1)
            dve.wait_ge(s["idx_step"], 3 * b + 1)
            dve.tensor_scalar(idx_i[:, u:u + 1], slot_w2[:, 0, u:u + 1], BIG, None, ALU.add).then_inc(s["idx_step"], 1)
            dve.tensor_scalar(idx_i[:, 8 + u:9 + u], slot_w2[:, 0, u:u + 1], BIG, cst[:, C_EMPTY:C_EMPTY + 1], ALU.add, ALU.min
                              ).then_inc(s["idx_step"], 1)

        def copy_xT_dve(dve, b, par):
            dve.wait_ge(s["xT_done"], b + 1)
            if not (isinstance(b, int) and b == 0):
                dve.wait_ge(s["gu_done"], b)
            dve.tensor_copy(xr[par][:, 512:1024], ps[1][:, :]).then_inc(s["xT_evD"], 1)

        def weigh(dve, b, u):
            par = u % 2
            dve.wait_ge(s["silu_ready"], b + 1)
            dve.wait_ge(s["idx_step"], 3 * b + 3)
            if not (isinstance(b, int) and b == 0):
                dve.wait_ge(s["hsT_done"], b)
            dve.scalar_tensor_tensor(out=hs2[par].rearrange("p (k q) -> p q k", k=KF), in0=silu2[par].rearrange("p (q k) -> p q k", k=KF),
                                     scalar=slot_w2[:, 1, u:u + 1], in1=ps[2 + par][:, F:2 * F].rearrange("p (q k) -> p q k", k=KF),
                                     op0=ALU.mult, op1=ALU.mult).then_inc(s["hs_ready"], 1)

        block = ctx.enter_context(nc.Block())

        @block.sync
        def _(sp):
            sp.dma_start(x_first[:, 0, :], x_t[0]).then_inc(s["x0_in"], 16)
            sp.dma_start(cst[:, :], consts).then_inc(s["const_in"], 16)
            sp.dma_start(gate_row[:, :], mix_g.partition_broadcast(P)).then_inc(s["row_in"], 16)
            for t in range(1, NT):
                sp.dma_start(x_first[:, t, :], x_t[t]).then_inc(s[f"x{t}_in"], 16)
                if t == 3:
                    load_plain(sp, 0)
            sp.dma_start(sml[:, :], small).then_inc(s["small_in"], 16)
            load_plain(sp, 1)
            sp.dma_start(rb_row[:, :], router_bias.partition_broadcast(P)).then_inc(s["misc_in"], 16)
            for i in range(2, NPLAIN):
                chunk_used(sp, i - 2)
                load_plain(sp, i)
            load_gates(sp, 0)
            sp.wait_ge(s["v_ev"], NT)
            sp.dma_start(v_rows[0:64, NT:2 * NT - 1, :], v_rows[64:128, 0:NT - 1, :]).then_inc(s["vo_in"], 16)
            sp.dma_start(v_rows[64:128, NT:2 * NT - 1, :], v_rows[0:64, 1:NT, :]).then_inc(s["vo_in"], 16)
            load_gates(sp, 1)
            for g in range(2, 6):
                load_gates(sp, g)
            sp.wait_ge(s["m_done"], 2 * KD)
            sp.dma_start(wo_sb, w_o.rearrange("(k p) n -> p k n", p=P)).then_inc(s["wo_in"], 16)
            sp.dma_start(gate_row[:, :], ffn_g.partition_broadcast(P)).then_inc(s["row_in"], 16)
            for g in range(6, 8):
                load_gates(sp, g)
            sp.wait_ge(s["merged_ready"], 2 * KD)
            for t in range(NT):
                if t >= 2:
                    sp.wait_ge(s["x2_ready"], 2 * (t - 1))
                sp.dma_start(xr[t % 2], x_t[t]).then_inc(s[f"x_in{t % 2}"], 16)
                if t == 0:
                    chunk_used(sp, NPLAIN + 7)
                    sp.dma_start(wr_sb, w_router.rearrange("(p k) e -> p k e", k=KD)).then_inc(s["misc_in"], 16)
                    sp.dma_start(wshgu_sb[:, 0], w_sh_gate.rearrange("(p k) f -> p k f", k=KD)).then_inc(s["misc_in"], 16)
                    sp.dma_start(wshgu_sb[:, 1], w_sh_up.rearrange("(p k) f -> p k f", k=KD)).then_inc(s["misc_in"], 16)
                    sp.dma_start(wshd_sb, w_sh_down.rearrange("(p k) n -> p k n", k=KF)).then_inc(s["misc_in"], 16)
            sp.wait_ge(s["xo_done"], 2 * NT)
            for e in range(NBUF):
                if e == 2:
                    sp.wait_ge(s["sh_done"], NT)
                load_expert(sp, e, e, e % 2)
                if e:
                    expert_here(sp, e - 1, (e - 1) % 2)
            sp.wait_ge(s["tab_ready"], 3)
            with sp.Fori(0, EXP // NBUF - 1) as q:
                for j in range(NBUF):
                    last = sp.value_load(end_i[0:1, bass.ds(q * NBUF + j, 1)], min_val=0, max_val=MAXBLK)
                    sp.wait_ge(s["y_done"], last)
                    load_expert(sp, q * NBUF + (NBUF + j), j, j % 2)
                    expert_here(sp, q * NBUF + (NBUF + j - 1), (j - 1) % 2)
            expert_here(sp, EXP - 1, 1)

        @block.gpsimd
        def _(pool):
            for c in range(NC):
                pool.memset(conv_in[:, c, 0:PAD], 0.0).then_inc(s["padded"], 1)
                pool.memset(conv_in[:, c, PAD + T:CPAD], 0.0).then_inc(s["padded"], 1)
            for b in range(2):
                pool.memset(qblk[b][:, :], 0.0).then_inc(s["qz_ready"], 1)
            for h in range(HEADS):
                src = bass.AP(rpb_rev.tensor, RPB_PAD + h * RELH * RELW - (GRID_W - WIN_W),
                              [[1, GRID_W], [RELW, RELH], [1, GRID_W]])
                a = (h // 2) * RELH * GRID_W
                pool.dma_start(rpb_raw[64 * (h % 2):64 * (h % 2) + 64, a:a + RELH * GRID_W].rearrange("p (r c) -> p r c", r=RELH),
                               src).then_inc(s["rpb_in"], 16)
            pool.wait_ge(s["rpb_in"], 16 * HEADS)
            pool.wait_ge(s["const_in"], 16)
            mb = wmask.unsqueeze(1).to_broadcast([P, PAIRS * RELH, GRID_W])
            raw = rpb_raw.rearrange("p (r c) -> p r c", c=GRID_W)
            tab = bias_t[:, :].rearrange("p (r c) -> p r c", c=GRID_W)
            pool.tensor_tensor(tab, raw[:, :, ::-1], mb, ALU.mult).then_inc(s["bias_step"], 1)
            pool.tensor_scalar(osb[0][:, 0:GRID_W], wmask, 1.0, -NEG, ALU.subtract, ALU.mult).then_inc(s["bias_m"], 1)
            pool.wait_ge(s["bias_step"], 1)
            pool.wait_ge(s["bias_m"], 1)
            pool.tensor_tensor(tab, tab, osb[0][:, 0:GRID_W].unsqueeze(1).to_broadcast([P, PAIRS * RELH, GRID_W]), ALU.add
                               ).then_inc(s["bias_ready"], 1)
            pool.wait_ge(s["qz_ready"], 2)
            pool.wait_ge(s["qk_ev"], 2 * NT)
            for a in range(2):
                query_block(pool, 0, a)
            with pool.Fori(0, ROWS - 1) as r:
                for a in range(PAIRS):
                    pool.wait_ge(s["s_done"], r * PAIRS + a + 1)
                    query_block(pool, r if a < 2 else r + 1, (a + 2) % PAIRS)
            for a in range(2):
                pool.wait_ge(s["s_done"], (ROWS - 1) * PAIRS + a + 1)
                query_block(pool, ROWS - 1, a + 2)
            tab = slot_tab.rearrange("p (t e c) -> p t e c", t=NT, c=SLOTC)
            pool.wait_ge(s["shd_done"], 2 * NT)
            count = 0
            for i in range(3):
                pool.tensor_copy(tab[:, :, :, i], row_less_big.unsqueeze(2).to_broadcast([P, NT, EXP])).then_inc(s["row_parts"], 1)
                count += 1
                if i < 2:
                    pool.wait_ge(s["row_parts"], count)
                    pool.tensor_tensor(row_less_big, row_less_big, tab[:, :, 0, i], ALU.subtract).then_inc(s["row_parts"], 1)
                    count += 1
                    pool.wait_ge(s["row_parts"], count)
            w3 = weight.rearrange("p (t e) -> p t e", t=NT)
            pool.wait_ge(s["weight_ready"], NT)
            count = 0
            for i in range(3):
                pool.tensor_copy(tab[:, :, :, 3 + i], w3).then_inc(s["weight_parts"], 1)
                count += 1
                if i < 2:
                    pool.wait_ge(s["weight_parts"], count)
                    pool.tensor_tensor(w3, w3, tab[:, :, :, 3 + i], ALU.subtract).then_inc(s["weight_parts"], 1)
                    count += 1
                    pool.wait_ge(s["weight_parts"], count)
            last_token, last_row = pool.to_reg(T - 1), pool.to_reg(T + P - 1)
            pool.wait_ge(s["h2_T"], NT)
            pool.wait_ge(s["h2_out"], 16 * NT)
            for b in range(3):
                gather(pool, b, b, last_token)
            pool.wait_ge(s["tab_ready"], 3)
            nblk = pool.value_load(end_i[0:1, EXP - 1:EXP], min_val=0, max_val=MAXBLK)

            def body(b, u):
                gather(pool, b + 3, (u + 3) % 4, last_token)
                copied, before, named = pool.to_reg(b + 2), pool.to_reg(16 * b), pool.to_reg(b + 1)
                pool.wait_ge(s["acc_out"], 16 * (NT + 1))
                if not (isinstance(b, int) and b == 0):
                    pool.wait_ge(s["y_out"], before)
                pool.tensor_copy(to_i[:, 0:1], idx_i[:, 8 + u:9 + u]).then_inc(s["to_ready"], 1)
                pool.wait_ge(s["acc_out"], 16 * (NT + 1))
                pool.wait_ge(s["to_ready"], named)
                pool.wait_ge(s["y_evA"], copied)
                pool.wait_ge(s["y_evD"], copied)
                pool.indirect_dma_start(out, bass.IndirectOffsetOnAxis(ap=to_i[:, 0:1], axis=0),
                                        y_sb[u % 2], None, bounds_check=last_row, oob_is_err=True, compute_op=ALU.add
                                        ).then_inc(s["y_out"], 16)

            all_blocks(pool, nblk, body)
            pool.wait_ge(s["y_out"], ((nblk + 3) // 4) * 64)

        @block.tensor
        def _(pe):
            pe.wait_ge(s["const_in"], 16)
            def turn_h1(t):
                pe.wait_ge(s["h_ready"], t + 1)
                if t >= 2:
                    pe.wait_ge(s["hT_evA"], t - 1)
                    pe.wait_ge(s["hT_evD"], t - 1)
                for k in range(KD):
                    mm = pe.transpose(ps[2 * (t % 2) + k // 4][:, P * (k % 4):P * (k % 4) + P], hr[t % 2][:, k * P:(k + 1) * P], ident)
                mm.then_inc(s["h_T"], 1)

            for t in range(4):
                turn_h1(t)
            for it, (c, n) in enumerate(AG_STEPS):
                if it in (0, 4):
                    chunk_here(pe, it // 4)
                w = wchunk[c // 2].rearrange("p (k n) -> p k n", k=KD)
                if it in (0, 2):
                    pe.wait_ge(s["hT_evA"], 4 * (n + 1))
                    pe.wait_ge(s["hT_evD"], 4 * (n + 1))
                if it >= 2:
                    pe.wait_ge(s["u_ready"], it - 1)
                for g in range(2):
                    for k in range(KD):
                        mm = pe.matmul(ps[4 + 2 * (it % 2) + g][:, :], w[:, k, 256 * g + P * (c % 2):256 * g + P * (c % 2) + P],
                                       hT[:, k, 512 * n:512 * n + 512], start=(k == 0), stop=(k == KD - 1))
                mm.then_inc(s["ag_done"], 1)
                if it < 2:
                    turn_h1(4 + 2 * it)
                    turn_h1(5 + 2 * it)
            for i in range(2 * NT + 1):
                if i < 2 * NT:
                    if i % NT == 0:
                        chunk_here(pe, 2 + i // NT)
                    w = wchunk[(2 + i // NT) % 2].rearrange("p (k n) -> p k n", k=KD)
                    if i == 0:
                        pe.wait_ge(s["hT_evA"], NT)
                    if i >= 2:
                        pe.wait_ge(s["qn_ready"], i - 1)
                    for k in range(KD):
                        mm = pe.matmul(ps[i % 2][:, :], hT[:, k, P * (i % NT):P * (i % NT) + P], w[:, k, :],
                                       start=(k == 0), stop=(k == KD - 1))
                    mm.then_inc(s["qk_done"], 1)
                if i >= 1:
                    j = i - 1
                    pe.wait_ge(s["qn_ready"], j + 1)
                    if j >= 2:
                        pe.wait_ge(s["qk_ev"], j - 1)
                    for a in range(PAIRS):
                        mm = pe.transpose(ps[2 + j % 2][:, P * a:P * a + P], half[2 + j % 2][:, P * a:P * a + P], ident)
                    mm.then_inc(s["qk_T"], 1)
            chunk_here(pe, 4)
            w = wchunk[0].rearrange("p (k n) -> p k n", k=KD)
            pe.wait_ge(s["u_ready"], 2 * NC)
            for t in range(NT):
                if t >= 2:
                    pe.wait_ge(s["v_ev"], t - 1)
                for k in range(KD):
                    mm = pe.matmul(ps[4 + t % 2][:, :], hT[:, k, P * t:P * t + P], w[:, k, :], start=(k == 0), stop=(k == KD - 1))
                mm.then_inc(s["v_done"], 1)
            pe.wait_ge(s["qk_ev"], 2 * NT)
            pe.wait_ge(s["v_ev"], NT)
            pe.wait_ge(s["vo_in"], 32)
            for name in ("pT_done", "o_done", "oT_done"):
                pe.sem_inc(s[name], 2)
            for a in range(PAIRS):
                score(pe, a, a, 0)
            def row(r, first=False, last=False):
                k0 = None if last else key_start(pe, r + 1)
                v0 = value_start(pe, r)
                v0_before = None if first else value_start(pe, r - 1)
                for a in range(PAIRS):
                    it = r * PAIRS + a
                    pe.wait_ge(s["s_biased"], it + 1)
                    if not last:
                        score(pe, it + PAIRS, a, k0)
                    turn_p(pe, it, a)
                    if a or not first:
                        values(pe, it - 1, (a - 1) % PAIRS, v0 if a else v0_before)
                    if a > 1 or not first:
                        turn_o(pe, it - 2, (a - 2) % PAIRS)

            all_rows(pe, row)
            it = ROWS * PAIRS - 1
            values(pe, it, 3, value_start(pe, ROWS - 1))
            turn_o(pe, it - 1, 2)
            turn_o(pe, it, 3)
            pe.wait_ge(s["oT_ev"], 2 * ROWS * PAIRS + 2)
            for it in range(4 * KD):
                m, n = it // 2 % KD, it % 2
                if it % 4 == 0:
                    chunk_here(pe, NPLAIN + it // 4)
                slot = chunk_at[NPLAIN + it // 4][0]
                if it == LN_STEP:
                    pe.wait_ge(s["conv_step"], NC * TAPS)
                    for h in range(2):
                        for c in range(NC):
                            mm = pe.matmul(ps[4 + h][:, :], ones, conv_u[:, c, 512 * h:512 * h + 512], start=(c == 0), stop=(c == NC - 1))
                        mm.then_inc(s["mu_done"], 1)
                if it >= 2:
                    pe.wait_ge(s["prod_ready"], it - 1)
                if it == 2 * KD:
                    pe.wait_ge(s["uT_ready"], 2 * NC)
                for b, kk, part, src in ((0, KD, "gate", hT), (1, NC, "out", attnT if it < 2 * KD else conv_u)):
                    for k in range(kk):
                        mm = pe.matmul(ps[2 * (it % 2) + b][:, :], gchunk(slot, part, m)[:, k, :], src[:, k, 512 * n:512 * n + 512],
                                       start=(k == 0), stop=(k == kk - 1))
                mm.then_inc(s["m_done"], 1)
                if it in (LN_STEP, LN_STEP + 1):
                    h = it - LN_STEP
                    for c in range(NC):
                        pe.wait_ge(s["csq_ready"], h * NC + c + 1)
                        mm = pe.matmul(ps[6 + h][:, :], ones, half[2 + c], start=(c == 0), stop=(c == NC - 1))
                    mm.then_inc(s["var_done"], 1)
            pe.wait_ge(s["wo_in"], 16)
            pe.wait_ge(s["merged_ready"], 2 * KD)
            for i in range(NT + 2):
                if i < NT:
                    for n in range(2):
                        if i >= 2:
                            pe.wait_ge(s["x2_ready"], 2 * (i - 2) + n + 1)
                        for k in range(KD):
                            mm = pe.matmul(ps[2 * (i % 2) + n][:, :], merged[:, k, P * i:P * i + P], wo_sb[:, k, 512 * n:512 * n + 512],
                                           start=(k == 0), stop=(k == KD - 1))
                        mm.then_inc(s["xo_done"], 1)
                if i >= 2:
                    j = i - 2
                    pe.wait_ge(s["h_ready"], NT + j + 1)
                    if j >= 1:
                        pe.wait_ge(s["h2T_evA"], j)
                        pe.wait_ge(s["h2T_evD"], j)
                    for k in range(KD):
                        mm = pe.transpose(ps[4 + k // 4][:, P * (k % 4):P * (k % 4) + P], hr[j % 2][:, k * P:(k + 1) * P], ident)
                    mm.then_inc(s["h2_T"], 1)
                    if j == 0:
                        pe.wait_ge(s["misc_in"], 80)
                    pe.wait_ge(s["h2T_evA"], j + 1)
                    pe.wait_ge(s["h2T_evD"], j + 1)
                    for k in range(KD):
                        mm = pe.matmul(ps[6][:, EXP * j:EXP * j + EXP], h2T[:, k, P * j:P * j + P], wr_sb[:, k, :],
                                       start=(k == 0), stop=(k == KD - 1))
                    mm.then_inc(s["r_done"], 1)
            for i in range(NT + 1):
                if i < NT:
                    if i < 2:
                        pe.wait_ge(s["x2_ready"], 2 * NT)
                    else:
                        pe.wait_ge(s["shh_ready"], i - 1)
                    for k in range(KD):
                        mm = pe.matmul(ps[i % 2][:, :], h2T[:, k, P * i:P * i + P], wshgu_sb[:, :, k, :], start=(k == 0), stop=(k == KD - 1))
                    mm.then_inc(s["sh_done"], 1)
                if i >= 1:
                    j = i - 1
                    pe.wait_ge(s["shh_ready"], j + 1)
                    if j >= 1:
                        pe.wait_ge(s["shT_ev"], j)
                    for k in range(KF):
                        mm = pe.transpose(ps[7][:, P * k:P * k + P], hs2[j % 2][:, P * k:P * k + P], ident)
                    mm.then_inc(s["shT_done"], 1)
                    pe.wait_ge(s["shT_ev"], j + 1)
                    for n in range(2):
                        if j >= 1:
                            pe.wait_ge(s["acc_ready"], 2 * (j - 1) + n + 1)
                        else:
                            pe.wait_ge(s["x2_ready"], 2 * NT)
                        for k in range(KF):
                            mm = pe.matmul(ps[2 + n][:, :], hsT2[j % 2][:, P * k:P * k + P], wshd_sb[:, k, 512 * n:512 * n + 512],
                                           start=(k == 0), stop=(k == KF - 1))
                        mm.then_inc(s["shd_done"], 1)
            pe.wait_ge(s["sel_ready"], NT)
            for t in range(NT):
                for j in range(t + 1):
                    pe.matmul(ps[4][:, EXP * t:EXP * t + EXP], tri if j == t else ones, sel[:, EXP * j:EXP * j + EXP],
                              start=(j == 0), stop=(j == t))
            for t in range(NT):
                mm = pe.matmul(ps[5][:, 0:EXP], ones, sel[:, EXP * t:EXP * t + EXP], start=(t == 0), stop=(t == NT - 1))
            mm.then_inc(s["cum_done"], 1)
            pe.wait_ge(s["tab_ready"], 1)
            pe.transpose(ps[5][0:1, P:2 * P], r_eb, ident).then_inc(s["blk_done"], 1)
            pe.sem_inc(s["gu_done"], 1)
            pe.sem_inc(s["hsT_done"], 1)
            pe.wait_ge(s["row_parts"], 5)
            pe.wait_ge(s["weight_parts"], 5)
            slots(pe, 0, 0, 0)
            pe.wait_ge(s["tab_ready"], 3)
            nblk = pe.value_load(end_i[0:1, EXP - 1:EXP], min_val=0, max_val=MAXBLK)
            slots(pe, 1, 1, expert_of(pe, 1))
            slots(pe, 2, 0, expert_of(pe, 2))
            turn_x(pe, 0, 0)
            gate_up(pe, 0, 0, 0)
            turn_x(pe, 1, 1)
            turn_h(pe, 0, 0)
            gate_up(pe, 1, 1, expert_of(pe, 1))

            def body(b, u):
                slots(pe, b + 3, (u + 1) % 2, expert_of(pe, b + 3))
                turn_x(pe, b + 2, u % 2)
                down(pe, b, u % 2, expert_of(pe, b))
                turn_h(pe, b + 1, (u + 1) % 2)
                gate_up(pe, b + 2, u % 2, expert_of(pe, b + 2))

            all_blocks(pe, nblk, body)

        @block.scalar
        def _(act):
            act.wait_ge(s["const_in"], 16)
            def rms(t):
                act.wait_ge(s[f"x{t}_in"], 16)
                if t >= 2:
                    act.wait_ge(s["h_T"], t - 1)
                rms_act(act, t, t, x_first[:, t, :])

            def sigmoid(it):
                act.wait_ge(s["ag_done"], it + 1)
                if it >= 2:
                    act.wait_ge(s["u_ready"], it - 1)
                act.activation(half[it % 2], ps[5 + 2 * (it % 2)][:, :], ACT.Sigmoid).then_inc(s["sig_ready"], 1)

            rms(0)
            for t in range(1, 6):
                rms(t)
                if t <= 4:
                    hT_act(act, t - 1)
            sigmoid(0)
            for t in (6, 7):
                hT_act(act, t - 2)
                rms(t)
            sigmoid(1)
            hT_act(act, 6)
            hT_act(act, 7)
            for it in range(2, 2 * NC):
                sigmoid(it)
            for i in range(2 * NT + 1):
                if i < 2 * NT:
                    act.wait_ge(s["qk_done"], i + 1)
                    if i >= 2:
                        act.wait_ge(s["ss_ready"], i - 1)
                    act.activation(half[4 + i % 2], ps[i % 2][:, :], ACT.Square).then_inc(s["sq_ready"], 1)
                    act.wait_ge(s["ss_ready"], i + 1)
                    if i >= 2:
                        act.wait_ge(s["qrstd_ready"], i - 1)
                    act.activation(st[:, 40 + 8 * (i % 2):48 + 8 * (i % 2)], st[:, 24 + 8 * (i % 2):32 + 8 * (i % 2)], ACT.Sqrt,
                                   bias=eps, scale=1.0 / HD).then_inc(s["qrms_ready"], 1)
                if i >= 1:
                    j = i - 1
                    act.wait_ge(s["qk_T"], j + 1)
                    if j == 0:
                        act.wait_ge(s["qg_ready"], 1)
                        act.wait_ge(s["small_in"], 16)
                    dst, g = (qT, st[:, 72:73]) if j < NT else (kT, sml[:, S_KG:S_KG + 1])
                    act.activation(dst[:, :, P * (j % NT):P * (j % NT) + P], ps[2 + j % 2][:, :].rearrange("p (a t) -> p a t", a=PAIRS),
                                   ACT.Copy, scale=g).then_inc(s["qk_ev"], 1)
            for t in range(NT):
                act.wait_ge(s["v_done"], t + 1)
                act.activation(v_rows[:, t, :], ps[4 + t % 2][:, :], ACT.Copy).then_inc(s["v_ev"], 1)
            act.sem_inc(s["p_ready"], 2)
            act.sem_inc(s["pT_ev"], 2)
            def row(r, first=False, last=False):
                for a in range(PAIRS):
                    it = r * PAIRS + a
                    act.wait_ge(s["negmax_ready"], it + 1)
                    act.wait_ge(s["pT_done"], it + 1)
                    act.wait_ge(s["o_ev"], it + 1)
                    act.activation(half[4 + a % 2], half[a], ACT.Exp, bias=st[:, 80 + a:81 + a],
                                   accum_out=st[:, 88 + a:89 + a]).then_inc(s["p_ready"], 1)
                    if a or not first:
                        copy_pT(act, it - 1, (a - 1) % PAIRS)

            all_rows(act, row)
            copy_pT(act, ROWS * PAIRS - 1, 3)
            def squares(n):
                if n:
                    act.wait_ge(s["var_done"], 1)
                for c in range(NC):
                    act.wait_ge(s["cen_ready"], n * NC + c + 1)
                    act.activation(half[2 + c], conv_u[:, c, 512 * n:512 * n + 512], ACT.Square).then_inc(s["csq_ready"], 1)

            def deviation(n):
                act.wait_ge(s["var_done"], n + 1)
                if n:
                    act.wait_ge(s["lrstd_ready"], 1)
                act.activation(half[6], ps[6 + n][:, :], ACT.Sqrt, bias=eps, scale=1.0 / D_CONV).then_inc(s["sd_ready"], 1)

            def conv_silu(n):
                for c in range(NC):
                    act.wait_ge(s["un_ready"], n * NC + c + 1)
                    act.activation(conv_u[:, c, 512 * n:512 * n + 512], conv_u[:, c, 512 * n:512 * n + 512], ACT.Silu,
                                   scale=sml[:, S_LG + c:S_LG + c + 1], bias=sml[:, S_LB + c:S_LB + c + 1]).then_inc(s["uT_ready"], 1)

            for it in range(4 * KD):
                if it == LN_STEP:
                    squares(0)
                if it == LN_STEP + 1:
                    deviation(0)
                    squares(1)
                if it == LN_STEP + 2:
                    deviation(1)
                if it in (LN_STEP + 3, LN_STEP + 4):
                    conv_silu(it - LN_STEP - 3)
                act.wait_ge(s["m_done"], it + 1)
                if it >= 2:
                    act.wait_ge(s["prod_ready"], it - 1)
                act.activation(half[it % 2], ps[2 * (it % 2)][:, :], ACT.Sigmoid).then_inc(s["gates_ready"], 1)
            for t in range(NT + 2):
                if t < NT:
                    act.wait_ge(s["x2_ready"], 2 * (t + 1))
                    if t >= 2:
                        act.wait_ge(s["h2_T"], t - 1)
                        act.wait_ge(s["h2_out"], 16 * (t - 1))
                    rms_act(act, NT + t, t, x2[:, t, :])
                if 1 <= t <= NT:
                    act.wait_ge(s["h_ready"], NT + t)
                    act.dma_start(h2_t[t - 1], hr[(t - 1) % 2]).then_inc(s["h2_out"], 16)
                if t >= 2:
                    j = t - 2
                    act.wait_ge(s["h2_T"], j + 1)
                    act.activation(h2T[:, 0:4, P * j:P * j + P], ps[4][:, :].rearrange("p (k t) -> p k t", k=4), ACT.Copy).then_inc(s["h2T_evA"], 1)
            act.wait_ge(s["r_done"], NT)
            act.activation(scores, ps[6][:, :], ACT.Sigmoid).then_inc(s["scores_ready"], 1)
            for i in range(NT + 1):
                if i < NT:
                    act.wait_ge(s["sh_done"], i + 1)
                    if i >= 2:
                        act.wait_ge(s["shh_ready"], i - 1)
                    act.activation(silu2[i % 2], ps[i % 2][:, 0:F], ACT.Silu).then_inc(s["shs_ready"], 1)
                if i >= 1:
                    j = i - 1
                    act.wait_ge(s["shT_done"], j + 1)
                    if j >= 2:
                        act.wait_ge(s["shd_done"], 2 * (j - 1))
                    act.activation(hsT2[j % 2], ps[7][:, 0:F], ACT.Copy).then_inc(s["shT_ev"], 1)
                if i >= 2:
                    store_acc(act, i - 2)
            store_acc(act, NT - 1)
            act.dma_start(out_t[NT], x2[:, 0, :]).then_inc(s["acc_out"], 16)
            act.wait_ge(s["tab_ready"], 3)
            nblk = act.value_load(end_i[0:1, EXP - 1:EXP], min_val=0, max_val=MAXBLK)
            act.sem_inc(s["hsT_ev"], 1)
            act.sem_inc(s["y_evA"], 1)
            copy_xT_act(act, 0, 0)
            silu_act(act, 0, 0)
            copy_xT_act(act, 1, 1)
            copy_hT(act, 0, 0)

            def body(b, u):
                silu_act(act, b + 1, (u + 1) % 2)
                copy_xT_act(act, b + 2, u % 2)
                act.wait_ge(s["y_done"], b + 1)
                if not (isinstance(b, int) and b < 2):
                    act.wait_ge(s["y_out"], 16 * b - 16)
                act.activation(y_sb[u % 2][:, 0:512], ps[4][:, :], ACT.Copy).then_inc(s["y_evA"], 1)
                copy_hT(act, b + 1, (u + 1) % 2)

            all_blocks(act, nblk, body)

        @block.vector
        def _(dve):
            def norm(t):
                norm_rows(dve, t, t, x_first[:, t, :], t >= 2 and ("h_T", t - 1), hr[t % 2])

            def copy_hT_dve(j):
                dve.wait_ge(s["h_T"], j + 1)
                dve.tensor_copy(hT[:, 4:8, P * j:P * j + P], ps[2 * (j % 2) + 1][:, :].rearrange("p (k t) -> p k t", k=4)).then_inc(s["hT_evD"], 1)

            def glu(it):
                c, n = AG_STEPS[it]
                dve.wait_ge(s["sig_ready"], it + 1)
                dve.tensor_tensor(conv_in[:, c, PAD + 512 * n:PAD + 512 * n + 512], ps[4 + 2 * (it % 2)][:, :],
                                  half[it % 2], ALU.mult).then_inc(s["u_ready"], 1)

            norm(0)
            for t in range(1, 6):
                norm(t)
                if t <= 4:
                    copy_hT_dve(t - 1)
            glu(0)
            for t in (6, 7):
                copy_hT_dve(t - 2)
                norm(t)
            glu(1)
            copy_hT_dve(6)
            copy_hT_dve(7)
            for it in range(2, 2 * NC):
                glu(it)
            dve.wait_ge(s["small_in"], 16)
            dve.tensor_scalar(st[:, 72:73], sml[:, S_QG:S_QG + 1], HD ** -0.5, None, ALU.mult).then_inc(s["qg_ready"], 1)
            dve.wait_ge(s["padded"], 2 * NC)
            dve.wait_ge(s["u_ready"], 2 * NC)
            dve.wait_ge(s["bias_ready"], 1)
            for i in range(3 * NT):
                if i < 2 * NT:
                    par = i % 2
                    ss, rms, rs = (st[:, o + 8 * par:o + 8 * par + 8] for o in (24, 40, 56))
                    dve.wait_ge(s["sq_ready"], i + 1)
                    dve.tensor_reduce(ss, half[4 + par].rearrange("p (h d) -> p h d", h=HEADS), AX, ALU.add).then_inc(s["ss_ready"], 1)
                for n in range(tap_start(i), tap_start(i + 1)):
                    tap(dve, n)
                if i < 2 * NT:
                    dve.wait_ge(s["qrms_ready"], i + 1)
                    dve.reciprocal(rs, rms).then_inc(s["qrstd_ready"], 1)
                    dve.wait_ge(s["qrstd_ready"], i + 1)
                    if i >= 2:
                        dve.wait_ge(s["qk_T"], i - 1)
                    dve.tensor_tensor(half[2 + par].rearrange("p (h d) -> p h d", h=HEADS), ps[par][:, :].rearrange("p (h d) -> p h d", h=HEADS),
                                      rs.unsqueeze(2).to_broadcast([P, HEADS, HD]), ALU.mult).then_inc(s["qn_ready"], 1)
            dve.sem_inc(s["o_ev"], 4)
            dve.sem_inc(s["oT_ev"], 2)
            for a in range(PAIRS):
                bias_max(dve, a, a, WIN_H - 1)
            def row(r, first=False, last=False):
                if isinstance(r, int):
                    d0 = None if last else window(r + 1) - r + (WIN_H - 2)
                else:
                    d0 = dve.snap((window(r + 1) - r + (WIN_H - 2)).with_bounds(min_val=0, max_val=WIN_H - 1))
                for a in range(PAIRS):
                    it = r * PAIRS + a
                    if not last:
                        dve.wait_ge(s["p_ready"], it + 3)
                        bias_max(dve, it + PAIRS, a, d0)
                    out_rows(dve, it, a)
                    if a or not first:
                        out_cols(dve, it - 1, (a - 1) % PAIRS, r if a else r - 1)

            all_rows(dve, row)
            out_cols(dve, ROWS * PAIRS - 1, 3, ROWS - 1)
            def center(n):
                dve.wait_ge(s["mu_done"], n + 1)
                for c in range(NC):
                    u = conv_u[:, c, 512 * n:512 * n + 512]
                    dve.scalar_tensor_tensor(out=u, in0=ps[4 + n][:, :], scalar=-1.0 / D_CONV, in1=u, op0=ALU.mult, op1=ALU.add).then_inc(s["cen_ready"], 1)

            def divide(n):
                dve.wait_ge(s["sd_ready"], n + 1)
                if n:
                    dve.wait_ge(s["un_ready"], NC)
                dve.reciprocal(half[7], half[6]).then_inc(s["lrstd_ready"], 1)
                dve.wait_ge(s["lrstd_ready"], n + 1)
                dve.wait_ge(s["cen_ready"], 2 * NC)
                for c in range(NC):
                    u = conv_u[:, c, 512 * n:512 * n + 512]
                    dve.tensor_tensor(u, u, half[7], ALU.mult).then_inc(s["un_ready"], 1)

            for it in range(4 * KD):
                m, n = it // 2 % KD, it % 2
                dst = merged[:, m, 512 * n:512 * n + 512]
                if it == LN_STEP:
                    center(0)
                    center(1)
                dve.wait_ge(s["gates_ready"], it + 1)
                if it < 2 * KD:
                    dve.tensor_tensor(dst, ps[2 * (it % 2) + 1][:, :], half[it % 2], ALU.mult).then_inc(s["prod_ready"], 1)
                    for j in range(tap_start(3 * NT + it), tap_start(3 * NT + it + 1)):
                        tap(dve, j)
                    if it in (LN_STEP, LN_STEP + 1):
                        divide(it - LN_STEP)
                else:
                    dve.tensor_tensor(half[4 + it % 2], ps[2 * (it % 2) + 1][:, :], half[it % 2], ALU.mult).then_inc(s["prod_ready"], 1)
                    dve.wait_ge(s["prod_ready"], it + 1)
                    dve.tensor_tensor(dst, dst, half[4 + it % 2], ALU.add).then_inc(s["merged_ready"], 1)
            for i in range(NT + 2):
                if i < NT:
                    dve.wait_ge(s[f"x_in{i % 2}"], 16 * (i // 2 + 1))
                    for n in range(2):
                        dve.wait_ge(s["xo_done"], 2 * i + n + 1)
                        dve.tensor_tensor(x2[:, i, 512 * n:512 * n + 512], ps[2 * (i % 2) + n][:, :], xr[i % 2][:, 512 * n:512 * n + 512], ALU.add
                                          ).then_inc(s["x2_ready"], 1)
                if 1 <= i <= NT:
                    j = i - 1
                    dve.wait_ge(s["x2_ready"], 2 * (j + 1))
                    norm_rows(dve, NT + j, j, x2[:, j, :], None, hr[j % 2].rearrange("p (k q) -> p q k", k=KD))
                if i >= 2:
                    j = i - 2
                    dve.wait_ge(s["h2_T"], j + 1)
                    dve.tensor_copy(h2T[:, 4:8, P * j:P * j + P], ps[5][:, :].rearrange("p (k t) -> p k t", k=4)).then_inc(s["h2T_evD"], 1)
            dve.memset(blk_i[:, :], 0).then_inc(s["rt_step"], 1)
            dve.memset(r_gs[:, GROUPS:12], NEG).then_inc(s["rt_step"], 1)
            dve.memset(r_rep[:, 4:8], NEG).then_inc(s["rt_step"], 1)
            count = [3]

            def step(ins):
                count[0] += 1
                ins.then_inc(s["rt_step"], 1)
                dve.wait_ge(s["rt_step"], count[0])

            dve.wait_ge(s["rt_step"], 3)
            dve.wait_ge(s["misc_in"], 80)
            dve.wait_ge(s["scores_ready"], 1)
            for t in range(NT + 1):
                if t < NT:
                    dve.wait_ge(s["shs_ready"], t + 1)
                    if t >= 2:
                        dve.wait_ge(s["shT_done"], t - 1)
                    dve.tensor_tensor(hs2[t % 2].rearrange("p (k q) -> p q k", k=KF), ps[t % 2][:, F:2 * F].rearrange("p (q k) -> p q k", k=KF),
                                      silu2[t % 2].rearrange("p (q k) -> p q k", k=KF), ALU.mult).then_inc(s["shh_ready"], 1)
                    route(dve, step, t)
                if t >= 1:
                    j = t - 1
                    for n in range(2):
                        dve.wait_ge(s["shd_done"], 2 * j + n + 1)
                        dve.tensor_tensor(x2[:, j, 512 * n:512 * n + 512], ps[2 + n][:, :], x2[:, j, 512 * n:512 * n + 512], ALU.add
                                          ).then_inc(s["acc_ready"], 1)
            dve.wait_ge(s["cum_done"], 1)
            step(dve.tensor_scalar(r_nb_i, ps[5][:, 0:EXP], float(P - 1), None, ALU.add))
            step(dve.tensor_scalar(r_nb_i, r_nb_i, 7, None, ALU.logical_shift_right))
            step(dve.tensor_scalar(r_nb, r_nb_i, 1.0, None, ALU.max))
            step(dve.tensor_tensor_scan(r_end, ones[:, 0:EXP], r_nb, 0.0, ALU.mult, ALU.add))
            step(dve.tensor_scalar(r_le, r_end, cst[:, C_PID:C_PID + 1], None, ALU.is_le))
            step(dve.tensor_reduce(r_eb, r_le, AX, ALU.add))
            dve.tensor_scalar(r_eb, r_eb, float(EXP - 1), None, ALU.min).then_inc(s["tab_ready"], 1)
            dve.tensor_copy(end_i[:, :], r_end).then_inc(s["tab_ready"], 1)
            step(dve.tensor_tensor(r_start, r_end, r_nb, ALU.subtract))
            step(dve.tensor_scalar(r_start, r_start, float(P), 1.0, ALU.mult, ALU.add))
            key3 = slot_key.rearrange("p (t e) -> p t e", t=NT)
            sel3 = sel.rearrange("p (t e) -> p t e", t=NT)
            step(dve.tensor_tensor(key3, ps[4][:, :].rearrange("p (t e) -> p t e", t=NT), r_start.unsqueeze(1).to_broadcast([P, NT, EXP]), ALU.add))
            step(dve.tensor_tensor(slot_key, slot_key, sel, ALU.mult))
            step(dve.tensor_scalar(slot_key, slot_key, -1.0, None, ALU.add))
            dve.wait_ge(s["blk_done"], 1)
            dve.tensor_copy(blk_i[0:1, 0:MAXBLK], ps[5][0:1, P:P + MAXBLK]).then_inc(s["tab_ready"], 1)
            dve.wait_ge(s["tab_ready"], 3)
            nblk = dve.value_load(end_i[0:1, EXP - 1:EXP], min_val=0, max_val=MAXBLK)
            dve.sem_inc(s["hs_ready"], 1)
            dve.sem_inc(s["y_evD"], 1)
            one_hot(dve, 0, 0)
            one_hot(dve, 1, 1)
            slot_rows(dve, 0, 0)
            one_hot(dve, 2, 0)
            slot_rows(dve, 1, 1)
            one_hot(dve, 3, 1)
            slot_rows(dve, 2, 2)
            copy_xT_dve(dve, 0, 0)
            weigh(dve, 0, 0)
            copy_xT_dve(dve, 1, 1)

            def body(b, u):
                weigh(dve, b + 1, (u + 1) % 4)
                slot_rows(dve, b + 3, (u + 3) % 4)
                copy_xT_dve(dve, b + 2, u % 2)
                one_hot(dve, b + 4, u % 2)
                dve.wait_ge(s["y_done"], b + 1)
                if not (isinstance(b, int) and b < 2):
                    dve.wait_ge(s["y_out"], 16 * b - 16)
                dve.tensor_copy(y_sb[u % 2][:, 512:1024], ps[5][:, :]).then_inc(s["y_evD"], 1)

            all_blocks(dve, nblk, body)


def _constants():
    p = np.arange(P)
    c = np.zeros((P, C_END), np.float32)
    c[:, C_ID:C_ID + P] = np.eye(P)
    c[:, C_TRI:C_TRI + P] = p[:, None] < p[None, :]
    c[:, C_ONE:C_ONE + P] = 1.0
    c[:, C_IOTA:C_IOTA + P] = p[None, :]
    q = p % GRID_W
    start = np.clip(q - WIN_W // 2, 0, GRID_W - WIN_W)
    col = np.arange(GRID_W)[None, :]
    c[:, C_MASK:C_MASK + GRID_W] = (col >= start[:, None]) & (col < start[:, None] + WIN_W)
    t = np.arange(NT)[None, :]
    c[:, C_ROW:C_ROW + NT] = P * t + p[:, None] - BIG
    c[:, C_EMPTY] = T + p
    c[:, C_EPS] = EPS
    c[:, C_PID] = p
    c[:, C_BASE:C_BASE + MAXBLK + 4] = P * np.arange(MAXBLK + 4)[None, :]
    return c


def kernel(x, norm_mix_g, w_in, q_norm_g, k_norm_g, rpb, conv_dw_w, conv_dw_b, conv_ln_g, conv_ln_b, w_conv_out,
           w_attn_out, w_o, norm_ffn_g, w_router, router_bias, w_exp_gate, w_exp_up, w_exp_down, w_sh_gate, w_sh_up, w_sh_down):
    import concourse.bacc as bacc
    from concourse.bass_utils import run_bass_kernel_spmd

    def chan(v):
        return np.asarray(v).reshape(NC, P, -1).transpose(1, 0, 2).reshape(P, -1)

    small = np.concatenate([chan(np.asarray(conv_dw_w)[0, :, 0, :].T), chan(conv_dw_b[0]), chan(conv_ln_g[0]), chan(conv_ln_b[0]),
                            np.tile(np.asarray(q_norm_g)[0], 2)[:, None], np.tile(np.asarray(k_norm_g)[0], 2)[:, None]], axis=1)
    rpb_rev = np.pad(np.asarray(rpb)[0, :, :, ::-1].reshape(-1), RPB_PAD)
    arrays = {
        "x": np.asarray(x)[0], "w_in": np.asarray(w_in)[0], "w_conv_out": np.asarray(w_conv_out)[0],
        "w_attn_out": np.asarray(w_attn_out)[0], "w_o": np.asarray(w_o)[0], "w_router": np.asarray(w_router)[0],
        "w_gate": np.asarray(w_exp_gate)[0], "w_up": np.asarray(w_exp_up)[0], "w_down": np.asarray(w_exp_down)[0],
        "w_sh_gate": np.asarray(w_sh_gate)[0], "w_sh_up": np.asarray(w_sh_up)[0], "w_sh_down": np.asarray(w_sh_down)[0],
        "mix_g": np.asarray(norm_mix_g)[0], "ffn_g": np.asarray(norm_ffn_g)[0], "router_bias": np.asarray(router_bias)[0],
        "rpb_rev": rpb_rev, "small": small, "consts": _constants(),
    }
    arrays = {k: np.ascontiguousarray(v) for k, v in arrays.items()}
    nc = bacc.Bacc("TRN2", target_bir_lowering=False, num_devices=1)
    args = [nc.dram_tensor(k, v.shape, mybir.dt.from_np(v.dtype), kind="ExternalInput").ap() for k, v in arrays.items()]
    out = nc.dram_tensor("out", (T + P, D), F32, kind="ExternalOutput").ap()
    build(nc, *args, out)
    r = run_bass_kernel_spmd(nc, [arrays], core_ids=[0])
    return r.results[0]["out"][:T].reshape(1, T, D)
```

```python
from contextlib import ExitStack

import numpy as np

import concourse.bass as bass
from concourse import mybir

P = 128
T = 1024
D = 1024
NT = T // P
KD = D // P
D_CONV = 512
NC = D_CONV // P
TAPS = 31
PAD = TAPS // 2
CPAD = T + 2 * PAD
HEADS = 8
HD = 64
D_ATTN = HEADS * HD
PAIRS = HEADS // 2
GRID_W = 64
ROWS = T // GRID_W
WIN_H = 8
WIN_W = 16
WKEYS = WIN_H * GRID_W
RELH = 2 * WIN_H - 1
RELW = 2 * WIN_W - 1
RPB_PAD = 64
EXP = 64
ARENA = 24704
GROUPS = 8
PER_GROUP = EXP // GROUPS
TOP_K = 8
F = 256
KF = F // P
GU = 2 * KD * F
DN = KF * D
PIECES = 4
PIECE = GU // PIECES
MAXBLK = T * TOP_K // P + EXP
NGU = 2
NDN = 4
ROUTE_SCALE = 2.5
EPS = 1e-6
BIG = 65536.0
NEG = -1e30

ALU = mybir.AluOpType
ACT = mybir.ActivationFunctionType
F32 = mybir.dt.float32
I32 = mybir.dt.int32
BF16 = mybir.dt.bfloat16
F32R = mybir.dt.float32r
SLOTC = 6
AX = mybir.AxisListType.X

C_ID, C_TRI, C_ONE, C_IOTA, C_MASK, C_ROW, C_EPS, C_PID, C_EMPTY, C_BASE = 0, 128, 256, 384, 512, 576, 584, 585, 586, 587
C_END = C_BASE + MAXBLK + 8
S_DW, S_DB, S_LG, S_LB, S_QG, S_KG, S_END = 0, NC * TAPS, NC * TAPS + 4, NC * TAPS + 8, NC * TAPS + 12, NC * TAPS + 13, NC * TAPS + 14


def build(nc, x, w_in, w_conv_out, w_attn_out, w_o, w_router, w_gate, w_up, w_down,
          w_sh_gate, w_sh_up, w_sh_down, mix_g, ffn_g, router_bias, rpb_rev, small, consts, out):
    with ExitStack() as ctx:
        def sb(name, cols, dt=F32):
            return ctx.enter_context(nc.sbuf_tensor(name, [P, cols], dt))

        def sem(name):
            return ctx.enter_context(nc.semaphore(name))

        h2_rows = nc.dram_tensor("h2_rows", [T, D], F32).ap()

        main_at = -(-nc.sbuf_base // 32) * 32
        main = sb("main", ARENA + 8192 + 2048)
        arena = main[:, 0:ARENA]
        qT = arena[:, 0:4096].rearrange("p (a t) -> p a t", a=PAIRS)
        kT = arena[:, 4096:8192].rearrange("p (a t) -> p a t", a=PAIRS)
        x_first = arena[:, 0:8192].rearrange("p (t d) -> p t d", t=NT)
        attnT = arena[:, 0:4096].rearrange("p (a t) -> p a t", a=PAIRS)
        merged = arena[:, 8192:16384].rearrange("p (m t) -> p m t", m=KD)
        v_rows = arena[:, 8192:16384].rearrange("p (s n) -> p s n", n=D_ATTN)
        wo_sb = arena[:, 0:8192].rearrange("p (k n) -> p k n", k=KD)
        conv_in = arena[:, 16384:16384 + NC * CPAD].rearrange("p (c t) -> p c t", c=NC)
        conv_u = arena[:, 20608:24704].rearrange("p (c t) -> p c t", c=NC)
        rpb_raw = arena[:, 20608:20608 + PAIRS * RELH * GRID_W]
        h2T = arena[:, 16384:24576].rearrange("p (k t) -> p k t", k=KD)

        hx = main[:, ARENA:ARENA + 8192]
        hT = hx.rearrange("p (k t) -> p k t", k=KD)
        x2 = hx.rearrange("p (t d) -> p t d", t=NT)
        xr_t = main[:, ARENA + 8192:ARENA + 8192 + 2048]
        raw_gu = main[:, 0:NGU * GU]
        raw_dn = main[:, NGU * GU:NGU * GU + NDN * DN]
        PARTS = NGU * GU + NDN * DN
        w_lo = nc.alloc_sbuf_tensor_at("w_lo", [P, 2 * GU], F32R, offset=main_at + 4 * PARTS)
        w_hi = nc.alloc_sbuf_tensor_at("w_hi", [P, 2 * GU], F32R, offset=main_at + 4 * (PARTS + 2 * GU))

        bias_t = sb("bias_t", PAIRS * RELH * GRID_W)
        biasT = bias_t[:, :].rearrange("p (a r c) -> p a r c", a=PAIRS, r=RELH)
        slot_key = bias_t[:, 0:512]
        weight = [bias_t[:, 1024 + EXP * i:1024 + EXP * (i + 1)] for i in range(2)]
        rb_row = bias_t[:, 1152:1216]
        blk_i = bias_t[:, 1216:1352].bitcast(I32)
        end_i = bias_t[:, 1352:1416].bitcast(I32)
        nb_i = bias_t[:, 1416:1480].bitcast(I32)
        idx_i = bias_t[:, 1480:1496].bitcast(I32)
        to_i = bias_t[:, 1496:1504].bitcast(I32)
        slot_w2 = bias_t[:, 1504:1512].rearrange("p (a u) -> p a u", a=2)
        hs2 = [bias_t[:, 1536 + F * i:1536 + F * (i + 1)] for i in range(2)]
        hsT2 = [bias_t[:, 2048 + F * i:2048 + F * (i + 1)] for i in range(2)]
        silu2 = [bias_t[:, 2560 + F * i:2560 + F * (i + 1)] for i in range(2)]
        rt = bias_t[:, 3072:3328]

        wring_at = -(-nc.sbuf_base // 32) * 32
        wring = sb("wring", 8192)
        x_hi = nc.alloc_sbuf_tensor_at("x_hi", [P, 2 * D], F32R, offset=wring_at + 4 * 4096)
        x_lo = nc.alloc_sbuf_tensor_at("x_lo", [P, 2 * D], F32R, offset=wring_at + 4 * 6144)
        wchunk = [wring[:, 4096 * i:4096 * (i + 1)] for i in range(2)]
        onehot = [bias_t[:, o:o + NT * P // 2].bitcast(BF16).rearrange("p (t j) -> p t j", t=NT) for o in (512, 3328)]
        y_sb = [wring[:, 2048 + 1024 * i:2048 + 1024 * (i + 1)] for i in range(2)]
        wr_sb = wring[:, 4096 + 2048:4096 + 2048 + 512].rearrange("p (k e) -> p k e", k=KD)
        wshd_sb = wring[:, 4096:4096 + 2048].rearrange("p (k n) -> p k n", k=KF)
        wshgu_sb = wring[:, 0:4096].rearrange("p (g k f) -> p g k f", g=2, k=KD)

        hr_t = sb("hr_t", 2048)
        xr = [xr_t[:, D * i:D * (i + 1)] for i in range(2)]
        hr = [hr_t[:, D * i:D * (i + 1)] for i in range(2)]
        rows_in = hr + [wring[:, D * i:D * (i + 1)] for i in range(2)]
        half = [xr_t[:, 512 * i:512 * (i + 1)] for i in range(4)] + [hr_t[:, 512 * i:512 * (i + 1)] for i in range(4)]
        gate_row = sb("gate_row", D)
        cst = sb("cst", C_END)
        sml = sb("sml", S_END)
        ident = cst[:, C_ID:C_ID + P]
        tri = cst[:, C_TRI:C_TRI + P]
        ones = cst[:, C_ONE:C_ONE + P]
        iota = cst[:, C_IOTA:C_IOTA + P]
        wmask = cst[:, C_MASK:C_MASK + GRID_W]
        row_less_big = cst[:, C_ROW:C_ROW + NT]
        eps = cst[:, C_EPS:C_EPS + 1]
        st = sb("st", 160)
        qblk = [sb(f"qblk{i}", P) for i in range(2)]
        osb = [sb(f"osb{i}", P) for i in range(2)]
        slot_no = sb("slot_no", 16, BF16)
        iota_b = sb("iota_b", P, BF16)
        slot_tab = sb("slot_tab", NT * EXP * SLOTC, BF16)[:, :]

        ps = [ctx.enter_context(nc.psum_tensor(f"ps{i}", [P, 512], F32)) for i in range(8)]

        s = {n: sem(n) for n in """const_in small_in row_in rpb_in x_in0 x_in1 x0_in x1_in x2_in x3_in x4_in x5_in x6_in x7_in w_in0 w_in1 wo_in vo_in misc_in
            ssq_ready rms_ready rstd_ready h_ready h_T hT_evA hT_evD
            ag_done sig_ready u_ready padded conv_step bias_ready bias_step bias_m
            qk_done sq_ready ss_ready qg_ready qrms_ready qrstd_ready qn_ready qk_T qk_ev v_done v_ev
            qz_ready qblk_ready s_done s_biased negmax_ready p_ready rowinv_ready pT_done pT_ev o_done o_ev oT_done oT_ev
            mu_done cen_ready csq_ready var_done sd_ready lrstd_ready un_ready uT_ready
            m_done gates_ready prod_ready merged_ready
            xo_done x2_ready h2_out h2_T h2T_evA h2T_evD r_done scores_ready
            sh_done shs_ready shh_ready shT_done shT_ev shd_done acc_ready
            rt_step sel_ready sum_ready cum_done blk_done tab_ready
            iota_ready oh_step oh_ready idx_done idx_step xg_in0 xg_in1 xg_in2 xg_in3 xT_done xT_hi xT_lo gu_done silu_ready hs_ready
            hsT_done hsT_ev y_done y_evA y_evD y_out to_ready gl0 gl1 dl0 dl1 dl2 dl3 gu_here dn_here w_hi_ready w_lo_ready acc_first acc_out row_parts weight_ready weight_parts""".split()}

        def gchunk(slot, part, m):
            c = wchunk[slot]
            c = c[:, 0:2 * KD * P].rearrange("p (k n) -> p k n", k=KD) if part == "gate" else c[:, 2 * KD * P:2 * (KD + NC) * P].rearrange("p (k n) -> p k n", k=NC)
            return c[:, :, P * (m % 2):P * (m % 2) + P]

        w_in_k = w_in.rearrange("(k p) n -> p k n", p=P)
        co_k = w_conv_out.rearrange("(k p) n -> p k n", p=P)
        ao_k = w_attn_out.rearrange("(k p) n -> p k n", p=P)
        x_t = x.rearrange("(t p) d -> t p d", p=P)
        out_t = out.rearrange("(t p) d -> t p d", p=P)
        h2_t = h2_rows.rearrange("(t p) d -> t p d", p=P)
        Q0, K0, V0, GA0, GB0 = 1024, 1536, 2048, 2560, 3584

        plain = [[(0, 256), (512, 256)], [(256, 256), (768, 256)], [(Q0, 512)], [(K0, 512)], [(V0, 512)]]
        NPLAIN = len(plain)
        wload = [0, 0]
        chunk_at = []
        for i in range(NPLAIN + KD):
            n = len(plain[i]) if i < NPLAIN else 2
            slot = i % 2
            wload[slot] += 16 * n
            chunk_at.append((slot, wload[slot]))

        def chunk_used(eng, i):
            if i < NPLAIN:
                name, n = (("ag_done", NC), ("ag_done", 2 * NC), ("qk_done", NT), ("qk_done", 2 * NT), ("v_done", NT))[i]
            else:
                name, n = "m_done", 4 * (i - NPLAIN + 1)
            eng.wait_ge(s[name], n)

        def chunk_here(eng, i):
            eng.wait_ge(s[f"w_in{chunk_at[i][0]}"], chunk_at[i][1])

        AG_STEPS = [(0, 0), (1, 0), (0, 1), (1, 1), (2, 0), (2, 1), (3, 0), (3, 1)]

        LN_STEP = 10

        scores = [rt[:, EXP * i:EXP * (i + 1)] for i in range(2)]
        biased = rt[:, 2 * EXP:3 * EXP]
        masked = rt[:, 3 * EXP:4 * EXP]
        ringfree = wring[:, 6656:8192]
        r_top = ringfree[:, 0:EXP]
        r_gs = ringfree[:, 64:76]
        r_go = ringfree[:, 80:92]
        r_rep = ringfree[:, 96:104]
        r_t8 = ringfree[:, 104:112]
        r_gm = ringfree[:, 112:120]
        r_gn = ringfree[:, 120:128]
        r_mo = ringfree[:, 128:192]
        r_sum = ringfree[:, 192:193]
        r_inv = ringfree[:, 193:194]
        r_eb = ringfree[:, 194:195]
        r_nb = ringfree[:, 256:320]
        r_end = ringfree[:, 320:384]
        r_nb_i = nb_i[:, :]
        r_start = ringfree[:, 384:448]
        r_le = ringfree[:, 448:512]
        sel = ringfree[:, 512:1024]
        sel_sum = ringfree[:, 1024:1536]
        gcol = [slot_no[:, 8 * i:8 * i + 8] for i in range(2)]

        def load_plain(sp, i):
            slot = chunk_at[i][0]
            c = wchunk[slot].rearrange("p (k n) -> p k n", k=KD)
            at = 0
            for c0, n in plain[i]:
                sp.dma_start(c[:, :, at:at + n], w_in_k[:, :, c0:c0 + n]).then_inc(s[f"w_in{slot}"], 16)
                at += n

        def load_gates(sp, g):
            i = NPLAIN + g
            chunk_used(sp, i - 2)
            slot = chunk_at[i][0]
            c = wchunk[slot]
            c0 = 2 * P * (g % 4)
            gate0, w_k = ((GB0, ao_k), (GA0, co_k))[g // 4]
            sp.dma_start(c[:, 0:2 * KD * P].rearrange("p (k n) -> p k n", k=KD), w_in_k[:, :, gate0 + c0:gate0 + c0 + 2 * P]).then_inc(s[f"w_in{slot}"], 16)
            sp.dma_start(c[:, 2 * KD * P:2 * (KD + NC) * P].rearrange("p (k n) -> p k n", k=NC), w_k[:, :, c0:c0 + 2 * P]).then_inc(s[f"w_in{slot}"], 16)

        def load_gu(sp, e, par):
            gu = raw_gu[:, GU * par:GU * (par + 1)].rearrange("p (g k f) -> p g k f", g=2, k=KD)
            for g, w in ((0, w_gate), (1, w_up)):
                sp.dma_start(gu[:, g].rearrange("p k f -> p (k f)"), w[bass.ds(e, 1)].rearrange("e (p k) f -> p (e k f)", k=KD)
                             ).then_inc(s[f"gl{par}"], 16)

        def load_dn(sp, e, j):
            sp.dma_start(raw_dn[:, DN * j:DN * (j + 1)], w_down[bass.ds(e, 1)].rearrange("e (p k) n -> p (e k n)", k=KF)
                         ).then_inc(s[f"dl{j}"], 16)

        def gu_in(sp, e, par):
            sp.wait_ge(s[f"gl{par}"], 32 * (e // 2 + 1) if isinstance(e, int) else 16 * e + (32 if par == 0 else 16))
            sp.sem_inc(s["gu_here"], 1)

        def dn_in(sp, turns, j):
            sp.wait_ge(s[f"dl{j}"], 16 * turns)
            sp.sem_inc(s["dn_here"], 1)

        def query_block(pool, r, a):
            for hh in range(2):
                pr = slice(64 * hh, 64 * hh + 64)
                pool.tensor_copy(qblk[a % 2][pr, 64 * hh:64 * hh + 64], qT[pr, a, bass.ds(r * GRID_W, GRID_W)]
                                 ).then_inc(s["qblk_ready"], 1)

        def gather(pool, b, u, last_token):
            if isinstance(b, int):
                pool.wait_ge(s["idx_step"], 3 * b + 3)
                if b >= 4:
                    pool.wait_ge(s["xT_done"], b - 3)
            else:
                steps, turned = pool.to_reg(3 * b + 3), pool.to_reg(b - 3)
                pool.wait_ge(s["h2_out"], 16 * NT)
                pool.wait_ge(s["idx_step"], steps)
                pool.wait_ge(s["xT_done"], turned)
            pool.indirect_dma_start(rows_in[u], None, h2_rows, bass.IndirectOffsetOnAxis(ap=idx_i[:, u:u + 1], axis=0),
                                    bounds_check=last_token, oob_is_err=False).then_inc(s[f"xg_in{u}"], 16)

        def expert_of(eng, b):
            return eng.value_load(blk_i[0:1, bass.ds(b, 1)], min_val=0, max_val=EXP - 1)

        def window(r):
            if isinstance(r, int):
                return min(max(r - WIN_H // 2, 0), ROWS - WIN_H)
            first = (r > WIN_H // 2) * (r - WIN_H // 2) - (r > ROWS - WIN_H // 2) * (r - (ROWS - WIN_H // 2))
            return first.with_bounds(min_val=0, max_val=ROWS - WIN_H)

        def value_tile(r0):
            return (r0 % 2) * NT + r0 // 2

        def key_start(pe, r):
            return window(r) * GRID_W if isinstance(r, int) else pe.snap(window(r) * GRID_W)

        def value_start(pe, r):
            if isinstance(r, int):
                return value_tile(window(r)) * D_ATTN
            return pe.snap(value_tile(pe.snap(window(r))) * D_ATTN)

        def all_rows(eng, row):
            row(0, first=True)
            with eng.Fori(0, (ROWS - 2) // 2) as q:
                row(q * 2 + 1)
                row(q * 2 + 2)
            row(ROWS - 1, last=True)

        def score(pe, it, a, k0):
            pe.wait_ge(s["qblk_ready"], 2 * it + 2)
            mm = pe.matmul(ps[a][:, :], qblk[a % 2][:, :], kT[:, a, bass.ds(k0, WKEYS)], start=True, stop=True)
            mm.then_inc(s["s_done"], 1)

        def turn_p(pe, it, a):
            pe.wait_ge(s["p_ready"], it + 3)
            pe.wait_ge(s["pT_ev"], it + 1)
            for j in range(4):
                mm = pe.transpose(ps[4 + a % 2][:, P * j:P * j + P], half[4 + a % 2][:, P * j:P * j + P], ident)
            mm.then_inc(s["pT_done"], 1)

        def values(pe, it, a, v0):
            pe.wait_ge(s["pT_ev"], it + 3)
            pe.wait_ge(s["o_ev"], it + 4)
            for j in range(4):
                mm = pe.matmul(ps[6][:, 0:P], half[6 + a % 2][:, P * j:P * j + P],
                               arena[:, bass.ds(v0 + (8192 + j * D_ATTN + a * P), P)], start=(j == 0), stop=(j == 3))
            mm.then_inc(s["o_done"], 1)

        def turn_o(pe, it, a):
            pe.wait_ge(s["o_ev"], it + 5)
            pe.wait_ge(s["oT_ev"], 2 * it + 2)
            pe.transpose(ps[7][:, 0:P], osb[a % 2][:, :], ident).then_inc(s["oT_done"], 1)

        def slots(pe, b, par, e):
            pe.wait_ge(s["oh_ready"], b + 1)
            if not (isinstance(b, int) and b == 0):
                pe.wait_ge(s["idx_step"], 3 * b)
            for t in range(NT):
                mm = pe.matmul(ps[6][:, 256:256 + SLOTC], onehot[par][:, t, :], slot_tab[:, bass.ds(SLOTC * e + SLOTC * EXP * t, SLOTC)],
                               start=(t == 0), stop=(t == NT - 1))
            mm.then_inc(s["idx_done"], 1)

        def turn_x(pe, b, u):
            pe.wait_ge(s[f"xg_in{u}"], 4 * b + (16 - 4 * u))
            if not (isinstance(b, int) and b == 0):
                pe.wait_ge(s["xT_lo"], 2 * b)
            for k in range(KD):
                mm = pe.transpose(ps[k // 4][:, P * (k % 4):P * (k % 4) + P], rows_in[u][:, k * P:(k + 1) * P], ident)
            mm.then_inc(s["xT_done"], 1)

        def gate_up(pe, b, par, e):
            pe.wait_ge(s["w_hi_ready"], PIECES * e + PIECES)
            pe.wait_ge(s["w_lo_ready"], PIECES * e + PIECES)
            pe.wait_ge(s["xT_hi"], 2 * b + 2)
            pe.wait_ge(s["xT_lo"], 2 * b + 2)
            if not (isinstance(b, int) and b == 0):
                pe.wait_ge(s["hs_ready"], b)
            for k in range(KD):
                cols = slice(D * par + P * k, D * par + P * k + P)
                for i, (xp, wp) in enumerate(((x_hi, w_hi), (x_hi, w_lo), (x_lo, w_hi))):
                    mm = pe.matmul(ps[2 + par][:, :], xp[:, cols], gu_cols(wp, e, k), start=(k == 0 and i == 0), stop=(k == KD - 1 and i == 2))
            mm.then_inc(s["gu_done"], 1)

        def turn_h(pe, b, par):
            pe.wait_ge(s["hs_ready"], b + 2)
            pe.wait_ge(s["hsT_ev"], b + 1)
            for k in range(KF):
                mm = pe.transpose(ps[7][:, P * k:P * k + P], hs2[par][:, P * k:P * k + P], ident)
            mm.then_inc(s["hsT_done"], 1)

        def down(pe, b, par, e):
            pe.wait_ge(s["dn_here"], e + 1)
            pe.wait_ge(s["hsT_ev"], b + 2)
            pe.wait_ge(s["y_evA"], b + 1)
            pe.wait_ge(s["y_evD"], b + 1)
            for n in range(2):
                for k in range(KF):
                    mm = pe.matmul(ps[4 + n][:, :], hsT2[par][:, P * k:P * k + P], dn_cols(e, k, n), start=(k == 0), stop=(k == KF - 1))
            mm.then_inc(s["y_done"], 1)

        def gu_cols(w, e, k):
            return w[:, bass.ds((e % 2) * GU + k * F, KD * F + F)].rearrange("p (a f) -> p a f", f=F)[:, ::KD, :]

        def dn_cols(e, k, n):
            return raw_dn[:, bass.ds((e % NDN) * DN + (k * D + 512 * n), 512)]

        def first_block(eng, b, e, e_before, split, pieces):
            if isinstance(b, int) and b == 0:
                split(eng, b, e, pieces)
            else:
                with eng.If(e > e_before):
                    split(eng, b, e, pieces)

        def split_hi(act, b, e, pieces):
            act.wait_ge(s["gu_here"], e + 1)
            if not (isinstance(b, int) and b == 0):
                act.wait_ge(s["gu_done"], b)
            for j in pieces:
                act.activation(w_hi[:, bass.ds((e % 2) * GU + j * PIECE, PIECE)], raw_gu[:, bass.ds((e % NGU) * GU + j * PIECE, PIECE)],
                               ACT.Copy).then_inc(s["w_hi_ready"], 1)

        def split_lo(dve, b, e, pieces):
            for j in pieces:
                dve.wait_ge(s["w_hi_ready"], PIECES * e + (1 + j))
                dve.tensor_tensor(w_lo[:, bass.ds((e % 2) * GU + j * PIECE, PIECE)], raw_gu[:, bass.ds((e % NGU) * GU + j * PIECE, PIECE)],
                                  w_hi[:, bass.ds((e % 2) * GU + j * PIECE, PIECE)], ALU.subtract).then_inc(s["w_lo_ready"], 1)

        def rms_act(act, count, t, src):
            act.activation(hr[t % 2], src, ACT.Square, accum_out=st[:, t:t + 1]).then_inc(s["ssq_ready"], 1)
            act.wait_ge(s["ssq_ready"], count + 1)
            act.activation(st[:, 8 + t:9 + t], st[:, t:t + 1], ACT.Sqrt, bias=eps, scale=1.0 / D).then_inc(s["rms_ready"], 1)

        def hT_act(act, t):
            act.wait_ge(s["h_T"], t + 1)
            act.activation(hT[:, 0:4, P * t:P * t + P], ps[2 * (t % 2)][:, :].rearrange("p (k t) -> p k t", k=4), ACT.Copy).then_inc(s["hT_evA"], 1)

        def copy_pT(act, it, a):
            act.wait_ge(s["pT_done"], it + 3)
            act.wait_ge(s["o_done"], it + 1)
            act.activation(half[6 + a % 2], ps[4 + a % 2][:, :], ACT.Copy).then_inc(s["pT_ev"], 1)

        def copy_xT_act(act, b, par):
            act.wait_ge(s["xT_done"], b + 1)
            if not (isinstance(b, int) and b == 0):
                act.wait_ge(s["gu_done"], b)
            for j in range(2):
                act.activation(x_hi[:, D * par + 512 * j:D * par + 512 * j + 512], ps[j][:, :], ACT.Copy).then_inc(s["xT_hi"], 1)

        def copy_hT(act, b, par):
            act.wait_ge(s["hsT_done"], b + 2)
            act.activation(hsT2[par], ps[7][:, 0:F], ACT.Copy).then_inc(s["hsT_ev"], 1)

        def store_acc(act, j):
            act.wait_ge(s["acc_ready"], 2 * (j + 1))
            act.dma_start(out_t[j], x2[:, j, :]).then_inc(s["acc_first" if j < NT // 2 else "acc_out"], 16)
            if j == 0:
                act.dma_start(out_t[NT], x2[:, 0, :]).then_inc(s["acc_first"], 16)

        def all_blocks(eng, nblk, body):
            for u in range(4):
                body(u, u)
            with eng.Fori(1, MAXBLK // 4) as q:
                with eng.If(nblk > q * 4):
                    for u in range(4):
                        body(q * 4 + u, u)

        def silu_act(act, b, par):
            act.wait_ge(s["gu_done"], b + 2)
            if not (isinstance(b, int) and b == 0):
                act.wait_ge(s["hs_ready"], b)
            act.activation(silu2[par], ps[2 + par][:, 0:F], ACT.Silu).then_inc(s["silu_ready"], 1)

        def norm_rows(dve, count, t, src, free, dst):
            dve.wait_ge(s["rms_ready"], count + 1)
            dve.reciprocal(st[:, 16 + t:17 + t], st[:, 8 + t:9 + t]).then_inc(s["rstd_ready"], 1)
            dve.wait_ge(s["rstd_ready"], count + 1)
            dve.wait_ge(s["row_in"], 16 * (count // NT + 1))
            if free:
                dve.wait_ge(s[free[0]], free[1])
            dve.scalar_tensor_tensor(out=dst, in0=src, scalar=st[:, 16 + t:17 + t], in1=gate_row[:, :], op0=ALU.mult, op1=ALU.mult
                                     ).then_inc(s["h_ready"], 1)

        def tap(dve, n):
            c, j = divmod(n, TAPS)
            w = sml[:, S_DW + c * TAPS + j:S_DW + c * TAPS + j + 1]
            src = conv_in[:, c, j:j + T]
            if j == 0:
                dve.tensor_scalar(conv_u[:, c, :], src, w, sml[:, S_DB + c:S_DB + c + 1], ALU.mult, ALU.add).then_inc(s["conv_step"], 1)
            else:
                dve.wait_ge(s["conv_step"], n)
                dve.scalar_tensor_tensor(out=conv_u[:, c, :], in0=src, scalar=w, in1=conv_u[:, c, :], op0=ALU.mult, op1=ALU.add).then_inc(s["conv_step"], 1)

        def tap_start(i):
            return min(3 * min(i, 2 * NT) + 5 * min(max(i - 2 * NT, 0), NT) + 4 * max(i - 3 * NT, 0), NC * TAPS)

        def bias_max(dve, it, a, d0):
            dve.wait_ge(s["s_done"], it + 1)
            dve.tensor_tensor(half[a].rearrange("p (r c) -> p r c", r=WIN_H), ps[a][:, :].rearrange("p (r c) -> p r c", r=WIN_H),
                              biasT[:, a, bass.ds(d0, WIN_H), :], ALU.add).then_inc(s["s_biased"], 1)
            dve.wait_ge(s["s_biased"], it + 1)
            dve.tensor_reduce(st[:, 80 + a:81 + a], half[a], AX, ALU.max, negate=True).then_inc(s["negmax_ready"], 1)

        def out_rows(dve, it, a):
            dve.wait_ge(s["p_ready"], it + 3)
            dve.reciprocal(st[:, 96 + a:97 + a], st[:, 88 + a:89 + a]).then_inc(s["rowinv_ready"], 1)
            dve.wait_ge(s["rowinv_ready"], it + 1)
            dve.wait_ge(s["o_done"], it + 3)
            dve.wait_ge(s["oT_done"], it + 1)
            dve.tensor_scalar(osb[a % 2][:, :], ps[6][:, 0:P], st[:, 96 + a:97 + a], None, ALU.mult).then_inc(s["o_ev"], 1)

        def out_cols(dve, it, a, r):
            dve.wait_ge(s["oT_done"], it + 3)
            for hh in range(2):
                pr = slice(64 * hh, 64 * hh + 64)
                dve.tensor_copy(attnT[pr, a, bass.ds(r * GRID_W, GRID_W)], ps[7][pr, 64 * hh:64 * hh + 64]
                                ).then_inc(s["oT_ev"], 1)

        def route(dve, step, t):
            sc, bi, ma, se = scores[t % 2], biased, masked, sel[:, EXP * t:EXP * t + EXP]
            dve.wait_ge(s["scores_ready"], t + 1)
            step(dve.tensor_tensor(bi, sc, rb_row[:, :], ALU.add))
            for g in range(GROUPS):
                m = dve.max(r_top[:, 8 * g:8 * g + 8], bi[:, PER_GROUP * g:PER_GROUP * (g + 1)])
                step(m)
            top = r_top.rearrange("p (g j) -> p g j", g=GROUPS)
            step(dve.tensor_tensor(r_gs[:, 0:GROUPS], top[:, :, 0], top[:, :, 1], ALU.add))
            step(dve.max(r_t8, r_gs[:, 0:GROUPS]))
            step(dve.tensor_copy(r_rep[:, 0:4], r_t8[:, 0:4]))
            step(dve.match_replace(r_go, r_rep, r_gs, 3.0 * NEG))
            step(dve.tensor_tensor(r_gm, r_go[:, 0:GROUPS], r_gs[:, 0:GROUPS], ALU.is_lt))
            step(dve.tensor_scalar(r_gn, r_gm, 1.0, -NEG, ALU.subtract, ALU.mult))
            ma3 = ma.rearrange("p (g j) -> p g j", g=GROUPS)
            step(dve.tensor_tensor(ma3, bi.rearrange("p (g j) -> p g j", g=GROUPS), r_gm.unsqueeze(2).to_broadcast([P, GROUPS, PER_GROUP]), ALU.mult))
            step(dve.tensor_tensor(ma3, ma3, r_gn.unsqueeze(2).to_broadcast([P, GROUPS, PER_GROUP]), ALU.add))
            step(dve.max(r_t8, ma))
            step(dve.match_replace(r_mo, r_t8, ma, 3.0 * NEG))
            dve.tensor_tensor(se, r_mo, ma, ALU.is_lt).then_inc(s["sel_ready"], 1)
            dve.wait_ge(s["sel_ready"], t + 1)
            if t == 0:
                dve.tensor_copy(sel_sum[:, 0:EXP], se).then_inc(s["sum_ready"], 1)
            else:
                dve.wait_ge(s["sum_ready"], t)
                dve.tensor_tensor(sel_sum[:, EXP * t:EXP * t + EXP], sel_sum[:, EXP * (t - 1):EXP * t], se, ALU.add).then_inc(s["sum_ready"], 1)
            step(dve.tensor_tensor(r_mo, sc, se, ALU.mult))
            step(dve.tensor_reduce(r_sum, r_mo, AX, ALU.add))
            step(dve.reciprocal(r_inv, r_sum))
            if t >= 2:
                dve.wait_ge(s["weight_parts"], 5 * (t - 1))
            dve.tensor_scalar(weight[t % 2], r_mo, r_inv, ROUTE_SCALE, ALU.mult, ALU.mult).then_inc(s["weight_ready"], 1)

        def one_hot(dve, b, par):
            e = 0 if isinstance(b, int) and b == 0 else expert_of(dve, b)
            keys = slot_key.rearrange("p (t e) -> p e t", t=NT)[:, bass.ds(e, 1), :].rearrange("p e t -> p (e t)")
            dve.tensor_scalar(gcol[par], keys, cst[:, bass.ds(C_BASE + b, 1)], None, ALU.subtract).then_inc(s["oh_step"], 1)
            dve.wait_ge(s["oh_step"], b + 1)
            if not (isinstance(b, int) and b < 2):
                dve.wait_ge(s["idx_done"], b - 1)
            dve.tensor_tensor(onehot[par], gcol[par].unsqueeze(2).to_broadcast([P, NT, P]), iota_b[:, :].unsqueeze(1).to_broadcast([P, NT, P]), ALU.is_equal
                              ).then_inc(s["oh_ready"], 1)

        def slot_rows(dve, b, u):
            dve.wait_ge(s["idx_done"], b + 1)
            if not (isinstance(b, int) and b < 4):
                dve.wait_ge(s["to_ready"], b - 3)
            dve.tensor_reduce(slot_w2[:, :, u], ps[6][:, 256:256 + SLOTC].rearrange("p (a c) -> p a c", a=2), AX, ALU.add).then_inc(s["idx_step"], 1)
            dve.wait_ge(s["idx_step"], 3 * b + 1)
            dve.tensor_scalar(idx_i[:, u:u + 1], slot_w2[:, 0, u:u + 1], BIG, None, ALU.add).then_inc(s["idx_step"], 1)
            dve.tensor_scalar(idx_i[:, 8 + u:9 + u], slot_w2[:, 0, u:u + 1], BIG, cst[:, C_EMPTY:C_EMPTY + 1], ALU.add, ALU.min
                              ).then_inc(s["idx_step"], 1)

        def copy_xT_dve(dve, b, par):
            for j in range(2):
                dve.wait_ge(s["xT_hi"], 2 * b + (1 + j))
                dve.tensor_tensor(x_lo[:, D * par + 512 * j:D * par + 512 * j + 512], ps[j][:, :],
                                  x_hi[:, D * par + 512 * j:D * par + 512 * j + 512], ALU.subtract).then_inc(s["xT_lo"], 1)

        def weigh(dve, b, u):
            par = u % 2
            dve.wait_ge(s["silu_ready"], b + 1)
            dve.wait_ge(s["idx_step"], 3 * b + 3)
            if not (isinstance(b, int) and b == 0):
                dve.wait_ge(s["hsT_done"], b)
            dve.scalar_tensor_tensor(out=hs2[par].rearrange("p (k q) -> p q k", k=KF), in0=silu2[par].rearrange("p (q k) -> p q k", k=KF),
                                     scalar=slot_w2[:, 1, u:u + 1], in1=ps[2 + par][:, F:2 * F].rearrange("p (q k) -> p q k", k=KF),
                                     op0=ALU.mult, op1=ALU.mult).then_inc(s["hs_ready"], 1)

        block = ctx.enter_context(nc.Block())

        @block.sync
        def _(sp):
            sp.dma_start(x_first[:, 0, :], x_t[0]).then_inc(s["x0_in"], 16)
            sp.dma_start(cst[:, :], consts).then_inc(s["const_in"], 16)
            sp.dma_start(gate_row[:, :], mix_g.partition_broadcast(P)).then_inc(s["row_in"], 16)
            for t in range(1, NT):
                sp.dma_start(x_first[:, t, :], x_t[t]).then_inc(s[f"x{t}_in"], 16)
                if t == 3:
                    load_plain(sp, 0)
            sp.dma_start(sml[:, :], small).then_inc(s["small_in"], 16)
            load_plain(sp, 1)
            for i in range(2, NPLAIN):
                chunk_used(sp, i - 2)
                load_plain(sp, i)
            load_gates(sp, 0)
            sp.wait_ge(s["v_ev"], NT)
            sp.dma_start(v_rows[0:64, NT:2 * NT - 1, :], v_rows[64:128, 0:NT - 1, :]).then_inc(s["vo_in"], 16)
            sp.dma_start(v_rows[64:128, NT:2 * NT - 1, :], v_rows[0:64, 1:NT, :]).then_inc(s["vo_in"], 16)
            load_gates(sp, 1)
            for g in range(2, 6):
                load_gates(sp, g)
            sp.wait_ge(s["m_done"], 2 * KD)
            sp.dma_start(wo_sb, w_o.rearrange("(k p) n -> p k n", p=P)).then_inc(s["wo_in"], 16)
            sp.dma_start(gate_row[:, :], ffn_g.partition_broadcast(P)).then_inc(s["row_in"], 16)
            for g in range(6, 8):
                load_gates(sp, g)
            sp.wait_ge(s["merged_ready"], 2 * KD)
            for t in range(NT):
                if t >= 2:
                    sp.wait_ge(s["x2_ready"], 2 * (t - 1))
                sp.dma_start(xr[t % 2], x_t[t]).then_inc(s[f"x_in{t % 2}"], 16)
                if t == 0:
                    chunk_used(sp, NPLAIN + 7)
                    sp.dma_start(rb_row, router_bias.partition_broadcast(P)).then_inc(s["misc_in"], 16)
                    sp.dma_start(wr_sb, w_router.rearrange("(p k) e -> p k e", k=KD)).then_inc(s["misc_in"], 16)
                    sp.dma_start(wshgu_sb[:, 0], w_sh_gate.rearrange("(p k) f -> p k f", k=KD)).then_inc(s["misc_in"], 16)
                    sp.dma_start(wshgu_sb[:, 1], w_sh_up.rearrange("(p k) f -> p k f", k=KD)).then_inc(s["misc_in"], 16)
                    sp.dma_start(wshd_sb, w_sh_down.rearrange("(p k) n -> p k n", k=KF)).then_inc(s["misc_in"], 16)
            sp.wait_ge(s["xo_done"], 2 * NT)
            for e in range(NGU):
                load_gu(sp, e, e)
            for e in range(NDN):
                load_dn(sp, e, e)
            for e in range(NGU):
                gu_in(sp, e, e)
            for e in range(NDN - 1):
                dn_in(sp, 1, e)
            sp.wait_ge(s["tab_ready"], 3)
            for e in range(2, 4):
                sp.wait_ge(s["w_lo_ready"], PIECES * e - PIECES)
                load_gu(sp, e, e % 2)
                gu_in(sp, e, e % 2)
            with sp.Fori(0, EXP // NDN - 1) as q:
                for j in range(NDN):
                    e = q * NDN + (NDN + j)
                    sp.wait_ge(s["w_lo_ready"], PIECES * e - PIECES)
                    load_gu(sp, e, j % 2)
                    last = sp.value_load(end_i[0:1, bass.ds(q * NDN + j, 1)], min_val=0, max_val=MAXBLK)
                    sp.wait_ge(s["y_done"], last)
                    load_dn(sp, e, j)
                    gu_in(sp, e, j % 2)
                    dn_in(sp, q + (2 if j else 1), (j - 1) % NDN)
            dn_in(sp, EXP // NDN, NDN - 1)

        @block.gpsimd
        def _(pool):
            for c in range(NC):
                pool.memset(conv_in[:, c, 0:PAD], 0.0).then_inc(s["padded"], 1)
                pool.memset(conv_in[:, c, PAD + T:CPAD], 0.0).then_inc(s["padded"], 1)
            for b in range(2):
                pool.memset(qblk[b][:, :], 0.0).then_inc(s["qz_ready"], 1)
            pool.wait_ge(s["h_T"], 2)
            for h in range(HEADS):
                src = bass.AP(rpb_rev.tensor, RPB_PAD + h * RELH * RELW - (GRID_W - WIN_W),
                              [[1, GRID_W], [RELW, RELH], [1, GRID_W]])
                a = (h // 2) * RELH * GRID_W
                pool.dma_start(rpb_raw[64 * (h % 2):64 * (h % 2) + 64, a:a + RELH * GRID_W].rearrange("p (r c) -> p r c", r=RELH),
                               src).then_inc(s["rpb_in"], 16)
            pool.wait_ge(s["rpb_in"], 16 * HEADS)
            pool.wait_ge(s["const_in"], 16)
            mb = wmask.unsqueeze(1).to_broadcast([P, PAIRS * RELH, GRID_W])
            raw = rpb_raw.rearrange("p (r c) -> p r c", c=GRID_W)
            tab = bias_t[:, :].rearrange("p (r c) -> p r c", c=GRID_W)
            pool.tensor_tensor(tab, raw[:, :, ::-1], mb, ALU.mult).then_inc(s["bias_step"], 1)
            pool.tensor_scalar(osb[0][:, 0:GRID_W], wmask, 1.0, -NEG, ALU.subtract, ALU.mult).then_inc(s["bias_m"], 1)
            pool.wait_ge(s["bias_step"], 1)
            pool.wait_ge(s["bias_m"], 1)
            pool.tensor_tensor(tab, tab, osb[0][:, 0:GRID_W].unsqueeze(1).to_broadcast([P, PAIRS * RELH, GRID_W]), ALU.add
                               ).then_inc(s["bias_ready"], 1)
            pool.wait_ge(s["qz_ready"], 2)
            pool.wait_ge(s["qk_ev"], 2 * NT)
            for a in range(2):
                query_block(pool, 0, a)
            with pool.Fori(0, ROWS - 1) as r:
                for a in range(PAIRS):
                    pool.wait_ge(s["s_done"], r * PAIRS + a + 1)
                    query_block(pool, r if a < 2 else r + 1, (a + 2) % PAIRS)
            for a in range(2):
                pool.wait_ge(s["s_done"], (ROWS - 1) * PAIRS + a + 1)
                query_block(pool, ROWS - 1, a + 2)
            tab = slot_tab.rearrange("p (t e c) -> p t e c", t=NT, c=SLOTC)
            pool.wait_ge(s["qblk_ready"], 2 * ROWS * PAIRS)
            count = 0
            for i in range(3):
                pool.tensor_copy(tab[:, :, :, i], row_less_big.unsqueeze(2).to_broadcast([P, NT, EXP])).then_inc(s["row_parts"], 1)
                count += 1
                if i < 2:
                    pool.wait_ge(s["row_parts"], count)
                    pool.tensor_tensor(row_less_big, row_less_big, tab[:, :, 0, i], ALU.subtract).then_inc(s["row_parts"], 1)
                    count += 1
                    pool.wait_ge(s["row_parts"], count)
            pool.wait_ge(s["row_parts"], 5)
            count = 0
            for t in range(NT):
                w = weight[t % 2]
                pool.wait_ge(s["weight_ready"], t + 1)
                for i in range(3):
                    pool.tensor_copy(tab[:, t, :, 3 + i], w).then_inc(s["weight_parts"], 1)
                    count += 1
                    pool.wait_ge(s["weight_parts"], count)
                    if i < 2:
                        pool.tensor_tensor(w, w, tab[:, t, :, 3 + i], ALU.subtract).then_inc(s["weight_parts"], 1)
                        count += 1
                        pool.wait_ge(s["weight_parts"], count)
            last_token, last_row = pool.to_reg(T - 1), pool.to_reg(T + P - 1)
            pool.wait_ge(s["h2_T"], NT)
            pool.wait_ge(s["h2_out"], 16 * NT)
            for b in range(4):
                if b == 2:
                    pool.wait_ge(s["sh_done"], NT)
                gather(pool, b, b, last_token)
            pool.wait_ge(s["tab_ready"], 3)
            nblk = pool.value_load(end_i[0:1, EXP - 1:EXP], min_val=0, max_val=MAXBLK)

            def body(b, u):
                named, returns = to_i[:, u % 2:u % 2 + 1], pool.to_reg(b + 1)
                pool.tensor_copy(named, idx_i[:, 8 + u:9 + u]).then_inc(s["to_ready"], 1)
                gather(pool, b + 4, u, last_token)
                copied, before = pool.to_reg(b + 2), pool.to_reg(16 * b)
                pool.wait_ge(s["acc_first"], 16 * (NT // 2 + 1))
                pool.wait_ge(s["acc_out"], 16 * NT // 2)
                pool.wait_ge(s["to_ready"], returns)
                if not (isinstance(b, int) and b == 0):
                    pool.wait_ge(s["y_out"], before)
                pool.wait_ge(s["y_evA"], copied)
                pool.wait_ge(s["y_evD"], copied)
                pool.indirect_dma_start(out, bass.IndirectOffsetOnAxis(ap=named, axis=0),
                                        y_sb[u % 2], None, bounds_check=last_row, oob_is_err=True, compute_op=ALU.add
                                        ).then_inc(s["y_out"], 16)

            all_blocks(pool, nblk, body)
            pool.wait_ge(s["y_out"], ((nblk + 3) // 4) * 64)

        @block.tensor
        def _(pe):
            pe.wait_ge(s["const_in"], 16)
            def turn_h1(t):
                pe.wait_ge(s["h_ready"], t + 1)
                if t >= 2:
                    pe.wait_ge(s["hT_evA"], t - 1)
                    pe.wait_ge(s["hT_evD"], t - 1)
                for k in range(KD):
                    mm = pe.transpose(ps[2 * (t % 2) + k // 4][:, P * (k % 4):P * (k % 4) + P], hr[t % 2][:, k * P:(k + 1) * P], ident)
                mm.then_inc(s["h_T"], 1)

            for t in range(4):
                turn_h1(t)
            for it, (c, n) in enumerate(AG_STEPS):
                if it in (0, 4):
                    chunk_here(pe, it // 4)
                w = wchunk[c // 2].rearrange("p (k n) -> p k n", k=KD)
                if it in (0, 2):
                    pe.wait_ge(s["hT_evA"], 4 * (n + 1))
                    pe.wait_ge(s["hT_evD"], 4 * (n + 1))
                if it >= 2:
                    pe.wait_ge(s["u_ready"], it - 1)
                for g in range(2):
                    for k in range(KD):
                        mm = pe.matmul(ps[4 + 2 * (it % 2) + g][:, :], w[:, k, 256 * g + P * (c % 2):256 * g + P * (c % 2) + P],
                                       hT[:, k, 512 * n:512 * n + 512], start=(k == 0), stop=(k == KD - 1))
                mm.then_inc(s["ag_done"], 1)
                if it < 2:
                    turn_h1(4 + 2 * it)
                    turn_h1(5 + 2 * it)
            def value_rows(t):
                if t >= 2:
                    pe.wait_ge(s["v_ev"], t - 1)
                for k in range(KD):
                    mm = pe.matmul(ps[4 + t % 2][:, :], hT[:, k, P * t:P * t + P], wchunk[0][:, 512 * k:512 * k + 512],
                                   start=(k == 0), stop=(k == KD - 1))
                mm.then_inc(s["v_done"], 1)

            for i in range(2 * NT + 1):
                if i < 2 * NT:
                    if i % NT == 0:
                        chunk_here(pe, 2 + i // NT)
                    w = wchunk[(2 + i // NT) % 2].rearrange("p (k n) -> p k n", k=KD)
                    if i == 0:
                        pe.wait_ge(s["hT_evA"], NT)
                    if i >= 2:
                        pe.wait_ge(s["qn_ready"], i - 1)
                    for k in range(KD):
                        mm = pe.matmul(ps[i % 2][:, :], hT[:, k, P * (i % NT):P * (i % NT) + P], w[:, k, :],
                                       start=(k == 0), stop=(k == KD - 1))
                    mm.then_inc(s["qk_done"], 1)
                else:
                    chunk_here(pe, 4)
                    pe.wait_ge(s["u_ready"], 2 * NC)
                    value_rows(0)
                if i >= 1:
                    j = i - 1
                    pe.wait_ge(s["qn_ready"], j + 1)
                    if j >= 2:
                        pe.wait_ge(s["qk_ev"], j - 1)
                    for a in range(PAIRS):
                        mm = pe.transpose(ps[2 + j % 2][:, P * a:P * a + P], half[2 + j % 2][:, P * a:P * a + P], ident)
                    mm.then_inc(s["qk_T"], 1)
            for t in range(1, NT):
                value_rows(t)
            pe.wait_ge(s["qk_ev"], 2 * NT)
            pe.wait_ge(s["v_ev"], NT)
            for name in ("pT_done", "o_done", "oT_done"):
                pe.sem_inc(s[name], 2)
            for a in range(PAIRS):
                score(pe, a, a, 0)
            def row(r, first=False, last=False):
                k0 = None if last else key_start(pe, r + 1)
                v0 = value_start(pe, r)
                v0_before = None if first else value_start(pe, r - 1)
                if isinstance(r, int) and r == 0:
                    v0 = 0
                else:
                    pe.wait_ge(s["vo_in"], 32)
                for a in range(PAIRS):
                    it = r * PAIRS + a
                    pe.wait_ge(s["s_biased"], it + 1)
                    if not last:
                        score(pe, it + PAIRS, a, k0)
                    turn_p(pe, it, a)
                    if a or not first:
                        values(pe, it - 1, (a - 1) % PAIRS, v0 if a else v0_before)
                    if a > 1 or not first:
                        turn_o(pe, it - 2, (a - 2) % PAIRS)

            all_rows(pe, row)
            it = ROWS * PAIRS - 1
            values(pe, it, 3, value_start(pe, ROWS - 1))
            turn_o(pe, it - 1, 2)
            turn_o(pe, it, 3)
            pe.wait_ge(s["oT_ev"], 2 * ROWS * PAIRS + 2)
            for it in range(4 * KD):
                m, n = it // 2 % KD, it % 2
                if it % 4 == 0:
                    chunk_here(pe, NPLAIN + it // 4)
                slot = chunk_at[NPLAIN + it // 4][0]
                if it == LN_STEP:
                    pe.wait_ge(s["conv_step"], NC * TAPS)
                    for h in range(2):
                        for c in range(NC):
                            mm = pe.matmul(ps[4 + h][:, :], ones, conv_u[:, c, 512 * h:512 * h + 512], start=(c == 0), stop=(c == NC - 1))
                        mm.then_inc(s["mu_done"], 1)
                if it >= 2:
                    pe.wait_ge(s["prod_ready"], it - 1)
                if it == 2 * KD:
                    pe.wait_ge(s["uT_ready"], 2 * NC)
                for b, kk, part, src in ((0, KD, "gate", hT), (1, NC, "out", attnT if it < 2 * KD else conv_u)):
                    for k in range(kk):
                        mm = pe.matmul(ps[2 * (it % 2) + b][:, :], gchunk(slot, part, m)[:, k, :], src[:, k, 512 * n:512 * n + 512],
                                       start=(k == 0), stop=(k == kk - 1))
                mm.then_inc(s["m_done"], 1)
                if it in (LN_STEP, LN_STEP + 1):
                    h = it - LN_STEP
                    for c in range(NC):
                        pe.wait_ge(s["csq_ready"], h * NC + c + 1)
                        mm = pe.matmul(ps[6 + h][:, :], ones, half[2 + c], start=(c == 0), stop=(c == NC - 1))
                    mm.then_inc(s["var_done"], 1)
            pe.wait_ge(s["wo_in"], 16)
            pe.wait_ge(s["merged_ready"], 2 * KD - 1)
            def shared_gu(i):
                if i < 2:
                    pe.wait_ge(s["x2_ready"], 2 * NT)
                else:
                    pe.wait_ge(s["shh_ready"], i - 1)
                for k in range(KD):
                    mm = pe.matmul(ps[i % 2][:, :], h2T[:, k, P * i:P * i + P], wshgu_sb[:, :, k, :], start=(k == 0), stop=(k == KD - 1))
                mm.then_inc(s["sh_done"], 1)

            for i in range(NT + 3):
                if i < NT:
                    if i == 1:
                        pe.wait_ge(s["merged_ready"], 2 * KD)
                    for n in range(2):
                        if i >= 2:
                            pe.wait_ge(s["x2_ready"], 2 * (i - 2) + n + 1)
                        for k in range(KD):
                            mm = pe.matmul(ps[2 * (i % 2) + n][:, :], merged[:, k, P * i:P * i + P], wo_sb[:, k, 512 * n:512 * n + 512],
                                           start=(k == 0), stop=(k == KD - 1))
                        mm.then_inc(s["xo_done"], 1)
                if 2 <= i < NT + 2:
                    j = i - 2
                    pe.wait_ge(s["h_ready"], NT + j + 1)
                    if j >= 1:
                        pe.wait_ge(s["h2T_evA"], j)
                        pe.wait_ge(s["h2T_evD"], j)
                    for k in range(KD):
                        mm = pe.transpose(ps[4 + k // 4][:, P * (k % 4):P * (k % 4) + P], hr[j % 2][:, k * P:(k + 1) * P], ident)
                    mm.then_inc(s["h2_T"], 1)
                if NT <= i < NT + 2:
                    shared_gu(i - NT)
                if i >= 3:
                    j = i - 3
                    if j == 0:
                        pe.wait_ge(s["misc_in"], 80)
                    else:
                        pe.wait_ge(s["scores_ready"], j)
                    pe.wait_ge(s["h2T_evA"], j + 1)
                    pe.wait_ge(s["h2T_evD"], j + 1)
                    for k in range(KD):
                        mm = pe.matmul(ps[6][:, EXP * j:EXP * j + EXP], h2T[:, k, P * j:P * j + P], wr_sb[:, k, :],
                                       start=(k == 0), stop=(k == KD - 1))
                    mm.then_inc(s["r_done"], 1)
            for i in range(NT + 1):
                if 2 <= i < NT:
                    shared_gu(i)
                if i == 3:
                    pe.wait_ge(s["sum_ready"], NT)
                    for t in range(NT):
                        pe.matmul(ps[4][:, EXP * t:EXP * t + EXP], tri, sel[:, EXP * t:EXP * t + EXP], start=True, stop=(t == 0))
                        if t:
                            pe.matmul(ps[4][:, EXP * t:EXP * t + EXP], ones, sel_sum[:, EXP * (t - 1):EXP * t], start=False, stop=True)
                    pe.matmul(ps[5][:, 0:EXP], ones, sel_sum[:, EXP * (NT - 1):EXP * NT], start=True, stop=True).then_inc(s["cum_done"], 1)
                if i == 4:
                    pe.wait_ge(s["tab_ready"], 1)
                    pe.transpose(ps[5][0:1, P:2 * P], r_eb, ident).then_inc(s["blk_done"], 1)
                if i == 5:
                    pe.wait_ge(s["row_parts"], 5)
                    pe.wait_ge(s["weight_parts"], 5 * NT)
                    slots(pe, 0, 0, 0)
                if i in (6, 7, 8):
                    pe.wait_ge(s["tab_ready"], 3)
                    slots(pe, i - 5, (i - 5) % 2, expert_of(pe, i - 5))
                if i >= 1:
                    j = i - 1
                    pe.wait_ge(s["shh_ready"], j + 1)
                    if j >= 1:
                        pe.wait_ge(s["shT_ev"], j)
                    for k in range(KF):
                        mm = pe.transpose(ps[7][:, P * k:P * k + P], hs2[j % 2][:, P * k:P * k + P], ident)
                    mm.then_inc(s["shT_done"], 1)
                    pe.wait_ge(s["shT_ev"], j + 1)
                    for n in range(2):
                        if j >= 1:
                            pe.wait_ge(s["acc_ready"], 2 * (j - 1) + n + 1)
                        else:
                            pe.wait_ge(s["x2_ready"], 2 * NT)
                        for k in range(KF):
                            mm = pe.matmul(ps[2 + n][:, :], hsT2[j % 2][:, P * k:P * k + P], wshd_sb[:, k, 512 * n:512 * n + 512],
                                           start=(k == 0), stop=(k == KF - 1))
                        mm.then_inc(s["shd_done"], 1)
            pe.sem_inc(s["gu_done"], 1)
            pe.sem_inc(s["hsT_done"], 1)
            nblk = pe.value_load(end_i[0:1, EXP - 1:EXP], min_val=0, max_val=MAXBLK)
            turn_x(pe, 0, 0)
            pe.wait_ge(s["acc_ready"], 2 * NT)
            turn_x(pe, 1, 1)
            gate_up(pe, 0, 0, 0)
            turn_h(pe, 0, 0)
            gate_up(pe, 1, 1, expert_of(pe, 1))

            def body(b, u):
                slots(pe, b + 4, u % 2, expert_of(pe, b + 4))
                turn_x(pe, b + 2, (u + 2) % 4)
                down(pe, b, u % 2, expert_of(pe, b))
                turn_h(pe, b + 1, (u + 1) % 2)
                gate_up(pe, b + 2, u % 2, expert_of(pe, b + 2))

            all_blocks(pe, nblk, body)

        @block.scalar
        def _(act):
            act.wait_ge(s["const_in"], 16)
            def rms(t):
                act.wait_ge(s[f"x{t}_in"], 16)
                if t >= 2:
                    act.wait_ge(s["h_T"], t - 1)
                rms_act(act, t, t, x_first[:, t, :])

            def sigmoid(it):
                act.wait_ge(s["ag_done"], it + 1)
                if it >= 2:
                    act.wait_ge(s["u_ready"], it - 1)
                act.activation(half[it % 2], ps[5 + 2 * (it % 2)][:, :], ACT.Sigmoid).then_inc(s["sig_ready"], 1)

            rms(0)
            for t in range(1, 6):
                rms(t)
                if t <= 4:
                    hT_act(act, t - 1)
            sigmoid(0)
            for t in (6, 7):
                hT_act(act, t - 2)
                rms(t)
            sigmoid(1)
            hT_act(act, 6)
            hT_act(act, 7)
            for it in range(2, 2 * NC):
                sigmoid(it)
            for i in range(2 * NT + 1):
                if i < 2 * NT:
                    act.wait_ge(s["qk_done"], i + 1)
                    if i >= 2:
                        act.wait_ge(s["ss_ready"], i - 1)
                    act.activation(half[4 + i % 2], ps[i % 2][:, :], ACT.Square).then_inc(s["sq_ready"], 1)
                    act.wait_ge(s["ss_ready"], i + 1)
                    if i >= 2:
                        act.wait_ge(s["qrstd_ready"], i - 1)
                    act.activation(st[:, 40 + 8 * (i % 2):48 + 8 * (i % 2)], st[:, 24 + 8 * (i % 2):32 + 8 * (i % 2)], ACT.Sqrt,
                                   bias=eps, scale=1.0 / HD).then_inc(s["qrms_ready"], 1)
                if i >= 1:
                    j = i - 1
                    act.wait_ge(s["qk_T"], j + 1)
                    if j == 0:
                        act.wait_ge(s["qg_ready"], 1)
                        act.wait_ge(s["small_in"], 16)
                    dst, g = (qT, st[:, 72:73]) if j < NT else (kT, sml[:, S_KG:S_KG + 1])
                    act.activation(dst[:, :, P * (j % NT):P * (j % NT) + P], ps[2 + j % 2][:, :].rearrange("p (a t) -> p a t", a=PAIRS),
                                   ACT.Copy, scale=g).then_inc(s["qk_ev"], 1)
            for t in range(NT):
                act.wait_ge(s["v_done"], t + 1)
                act.activation(v_rows[:, t, :], ps[4 + t % 2][:, :], ACT.Copy).then_inc(s["v_ev"], 1)
            act.sem_inc(s["p_ready"], 2)
            act.sem_inc(s["pT_ev"], 2)
            def row(r, first=False, last=False):
                for a in range(PAIRS):
                    it = r * PAIRS + a
                    act.wait_ge(s["negmax_ready"], it + 1)
                    act.wait_ge(s["pT_done"], it + 1)
                    act.wait_ge(s["o_ev"], it + 1)
                    act.activation(half[4 + a % 2], half[a], ACT.Exp, bias=st[:, 80 + a:81 + a],
                                   accum_out=st[:, 88 + a:89 + a]).then_inc(s["p_ready"], 1)
                    if a or not first:
                        copy_pT(act, it - 1, (a - 1) % PAIRS)

            all_rows(act, row)
            copy_pT(act, ROWS * PAIRS - 1, 3)
            def squares(n):
                if n:
                    act.wait_ge(s["var_done"], 1)
                for c in range(NC):
                    act.wait_ge(s["cen_ready"], n * NC + c + 1)
                    act.activation(half[2 + c], conv_u[:, c, 512 * n:512 * n + 512], ACT.Square).then_inc(s["csq_ready"], 1)

            def deviation(n):
                act.wait_ge(s["var_done"], n + 1)
                if n:
                    act.wait_ge(s["lrstd_ready"], 1)
                act.activation(half[6], ps[6 + n][:, :], ACT.Sqrt, bias=eps, scale=1.0 / D_CONV).then_inc(s["sd_ready"], 1)

            def conv_silu(n):
                for c in range(NC):
                    act.wait_ge(s["un_ready"], n * NC + c + 1)
                    act.activation(conv_u[:, c, 512 * n:512 * n + 512], conv_u[:, c, 512 * n:512 * n + 512], ACT.Silu,
                                   scale=sml[:, S_LG + c:S_LG + c + 1], bias=sml[:, S_LB + c:S_LB + c + 1]).then_inc(s["uT_ready"], 1)

            for it in range(4 * KD):
                if it == LN_STEP:
                    squares(0)
                if it == LN_STEP + 1:
                    deviation(0)
                    squares(1)
                if it == LN_STEP + 2:
                    deviation(1)
                if it in (LN_STEP + 3, LN_STEP + 4):
                    conv_silu(it - LN_STEP - 3)
                act.wait_ge(s["m_done"], it + 1)
                if it >= 2:
                    act.wait_ge(s["prod_ready"], it - 1)
                act.activation(half[it % 2], ps[2 * (it % 2)][:, :], ACT.Sigmoid).then_inc(s["gates_ready"], 1)
            for t in range(NT + 3):
                if t < NT:
                    act.wait_ge(s["x2_ready"], 2 * (t + 1))
                    if t >= 2:
                        act.wait_ge(s["h2_T"], t - 1)
                        act.wait_ge(s["h2_out"], 16 * (t - 1))
                    rms_act(act, NT + t, t, x2[:, t, :])
                if 1 <= t <= NT:
                    act.wait_ge(s["h_ready"], NT + t)
                    act.dma_start(h2_t[t - 1], hr[(t - 1) % 2]).then_inc(s["h2_out"], 16)
                if 2 <= t < NT + 2:
                    j = t - 2
                    act.wait_ge(s["h2_T"], j + 1)
                    act.activation(h2T[:, 0:4, P * j:P * j + P], ps[4][:, :].rearrange("p (k t) -> p k t", k=4), ACT.Copy).then_inc(s["h2T_evA"], 1)
                if t >= 3:
                    j = t - 3
                    act.wait_ge(s["r_done"], j + 1)
                    if j >= 2:
                        act.wait_ge(s["weight_ready"], j - 1)
                    act.activation(scores[j % 2], ps[6][:, EXP * j:EXP * j + EXP], ACT.Sigmoid).then_inc(s["scores_ready"], 1)
            for i in range(NT + 1):
                if i < NT:
                    act.wait_ge(s["sh_done"], i + 1)
                    if i >= 2:
                        act.wait_ge(s["shh_ready"], i - 1)
                    act.activation(silu2[i % 2], ps[i % 2][:, 0:F], ACT.Silu).then_inc(s["shs_ready"], 1)
                if i >= 1:
                    j = i - 1
                    act.wait_ge(s["shT_done"], j + 1)
                    if j >= 2:
                        act.wait_ge(s["shd_done"], 2 * (j - 1))
                    act.activation(hsT2[j % 2], ps[7][:, 0:F], ACT.Copy).then_inc(s["shT_ev"], 1)
                if i >= 2:
                    store_acc(act, i - 2)
                if i == NT - 1:
                    act.wait_ge(s["acc_first"], 16 * (NT // 2 + 1))
                    first_block(act, 0, 0, None, split_hi, range(PIECES))
            store_acc(act, NT - 1)
            act.wait_ge(s["tab_ready"], 3)
            nblk = act.value_load(end_i[0:1, EXP - 1:EXP], min_val=0, max_val=MAXBLK)
            act.sem_inc(s["hsT_ev"], 1)
            act.sem_inc(s["y_evA"], 1)
            copy_xT_act(act, 0, 0)
            act.wait_ge(s["acc_out"], 16 * NT // 2)
            e1 = expert_of(act, 1)
            first_block(act, 1, e1, 0, split_hi, range(PIECES))
            copy_xT_act(act, 1, 1)
            silu_act(act, 0, 0)
            copy_hT(act, 0, 0)
            first_block(act, 2, expert_of(act, 2), e1, split_hi, range(PIECES))

            def body(b, u):
                silu_act(act, b + 1, (u + 1) % 2)
                e, e_before = expert_of(act, b + 3), expert_of(act, b + 2)
                copy_xT_act(act, b + 2, u % 2)
                first_block(act, b + 3, e, e_before, split_hi, (0, 1))
                act.wait_ge(s["y_done"], b + 1)
                if not (isinstance(b, int) and b < 2):
                    act.wait_ge(s["y_out"], 16 * b - 16)
                act.activation(y_sb[u % 2][:, 0:512], ps[4][:, :], ACT.Copy).then_inc(s["y_evA"], 1)
                copy_hT(act, b + 1, (u + 1) % 2)
                first_block(act, b + 3, e, e_before, split_hi, (2, 3))

            all_blocks(act, nblk, body)

        @block.vector
        def _(dve):
            def norm(t):
                norm_rows(dve, t, t, x_first[:, t, :], t >= 2 and ("h_T", t - 1), hr[t % 2])

            def copy_hT_dve(j):
                dve.wait_ge(s["h_T"], j + 1)
                dve.tensor_copy(hT[:, 4:8, P * j:P * j + P], ps[2 * (j % 2) + 1][:, :].rearrange("p (k t) -> p k t", k=4)).then_inc(s["hT_evD"], 1)

            def glu(it):
                c, n = AG_STEPS[it]
                dve.wait_ge(s["sig_ready"], it + 1)
                dve.tensor_tensor(conv_in[:, c, PAD + 512 * n:PAD + 512 * n + 512], ps[4 + 2 * (it % 2)][:, :],
                                  half[it % 2], ALU.mult).then_inc(s["u_ready"], 1)

            norm(0)
            for t in range(1, 6):
                norm(t)
                if t <= 4:
                    copy_hT_dve(t - 1)
            glu(0)
            for t in (6, 7):
                copy_hT_dve(t - 2)
                norm(t)
            glu(1)
            copy_hT_dve(6)
            copy_hT_dve(7)
            for it in range(2, 2 * NC):
                glu(it)
            dve.wait_ge(s["small_in"], 16)
            dve.tensor_scalar(st[:, 72:73], sml[:, S_QG:S_QG + 1], HD ** -0.5, None, ALU.mult).then_inc(s["qg_ready"], 1)
            dve.tensor_copy(iota_b[:, :], iota).then_inc(s["iota_ready"], 1)
            dve.wait_ge(s["padded"], 2 * NC)
            dve.wait_ge(s["u_ready"], 2 * NC)
            dve.wait_ge(s["bias_ready"], 1)
            for i in range(3 * NT):
                if i < 2 * NT:
                    par = i % 2
                    ss, rms, rs = (st[:, o + 8 * par:o + 8 * par + 8] for o in (24, 40, 56))
                    dve.wait_ge(s["sq_ready"], i + 1)
                    dve.tensor_reduce(ss, half[4 + par].rearrange("p (h d) -> p h d", h=HEADS), AX, ALU.add).then_inc(s["ss_ready"], 1)
                for n in range(tap_start(i), tap_start(i + 1)):
                    tap(dve, n)
                if i < 2 * NT:
                    dve.wait_ge(s["qrms_ready"], i + 1)
                    dve.reciprocal(rs, rms).then_inc(s["qrstd_ready"], 1)
                    dve.wait_ge(s["qrstd_ready"], i + 1)
                    if i >= 2:
                        dve.wait_ge(s["qk_T"], i - 1)
                    dve.tensor_tensor(half[2 + par].rearrange("p (h d) -> p h d", h=HEADS), ps[par][:, :].rearrange("p (h d) -> p h d", h=HEADS),
                                      rs.unsqueeze(2).to_broadcast([P, HEADS, HD]), ALU.mult).then_inc(s["qn_ready"], 1)
            dve.sem_inc(s["o_ev"], 4)
            dve.sem_inc(s["oT_ev"], 2)
            for a in range(PAIRS):
                bias_max(dve, a, a, WIN_H - 1)
            def row(r, first=False, last=False):
                if isinstance(r, int):
                    d0 = None if last else window(r + 1) - r + (WIN_H - 2)
                else:
                    d0 = dve.snap((window(r + 1) - r + (WIN_H - 2)).with_bounds(min_val=0, max_val=WIN_H - 1))
                for a in range(PAIRS):
                    it = r * PAIRS + a
                    if not last:
                        dve.wait_ge(s["p_ready"], it + 3)
                        bias_max(dve, it + PAIRS, a, d0)
                    out_rows(dve, it, a)
                    if a or not first:
                        out_cols(dve, it - 1, (a - 1) % PAIRS, r if a else r - 1)

            all_rows(dve, row)
            out_cols(dve, ROWS * PAIRS - 1, 3, ROWS - 1)
            def center(n):
                dve.wait_ge(s["mu_done"], n + 1)
                for c in range(NC):
                    u = conv_u[:, c, 512 * n:512 * n + 512]
                    dve.scalar_tensor_tensor(out=u, in0=ps[4 + n][:, :], scalar=-1.0 / D_CONV, in1=u, op0=ALU.mult, op1=ALU.add).then_inc(s["cen_ready"], 1)

            def divide(n):
                dve.wait_ge(s["sd_ready"], n + 1)
                if n:
                    dve.wait_ge(s["un_ready"], NC)
                dve.reciprocal(half[7], half[6]).then_inc(s["lrstd_ready"], 1)
                dve.wait_ge(s["lrstd_ready"], n + 1)
                dve.wait_ge(s["cen_ready"], 2 * NC)
                for c in range(NC):
                    u = conv_u[:, c, 512 * n:512 * n + 512]
                    dve.tensor_tensor(u, u, half[7], ALU.mult).then_inc(s["un_ready"], 1)

            for it in range(4 * KD):
                m, n = it // 2 % KD, it % 2
                dst = merged[:, m, 512 * n:512 * n + 512]
                if it == LN_STEP:
                    center(0)
                    center(1)
                dve.wait_ge(s["gates_ready"], it + 1)
                if it < 2 * KD:
                    dve.tensor_tensor(dst, ps[2 * (it % 2) + 1][:, :], half[it % 2], ALU.mult).then_inc(s["prod_ready"], 1)
                    for j in range(tap_start(3 * NT + it), tap_start(3 * NT + it + 1)):
                        tap(dve, j)
                    if it in (LN_STEP, LN_STEP + 1):
                        divide(it - LN_STEP)
                else:
                    dve.tensor_tensor(half[4 + it % 2], ps[2 * (it % 2) + 1][:, :], half[it % 2], ALU.mult).then_inc(s["prod_ready"], 1)
                    dve.wait_ge(s["prod_ready"], it + 1)
                    dve.tensor_tensor(dst, dst, half[4 + it % 2], ALU.add).then_inc(s["merged_ready"], 1)
            dve.memset(blk_i[:, :], 0).then_inc(s["rt_step"], 1)
            dve.memset(r_gs[:, GROUPS:12], NEG).then_inc(s["rt_step"], 1)
            dve.memset(r_rep[:, 4:8], NEG).then_inc(s["rt_step"], 1)
            count = [3]

            def step(ins):
                count[0] += 1
                ins.then_inc(s["rt_step"], 1)
                dve.wait_ge(s["rt_step"], count[0])

            dve.wait_ge(s["rt_step"], 3)
            for i in range(NT + 2):
                if i < NT:
                    dve.wait_ge(s[f"x_in{i % 2}"], 16 * (i // 2 + 1))
                    for n in range(2):
                        dve.wait_ge(s["xo_done"], 2 * i + n + 1)
                        dve.tensor_tensor(x2[:, i, 512 * n:512 * n + 512], ps[2 * (i % 2) + n][:, :], xr[i % 2][:, 512 * n:512 * n + 512], ALU.add
                                          ).then_inc(s["x2_ready"], 1)
                if 1 <= i <= NT:
                    j = i - 1
                    dve.wait_ge(s["x2_ready"], 2 * (j + 1))
                    norm_rows(dve, NT + j, j, x2[:, j, :], None, hr[j % 2].rearrange("p (k q) -> p q k", k=KD))
                if i >= 2:
                    j = i - 2
                    dve.wait_ge(s["h2_T"], j + 1)
                    dve.tensor_copy(h2T[:, 4:8, P * j:P * j + P], ps[5][:, :].rearrange("p (k t) -> p k t", k=4)).then_inc(s["h2T_evD"], 1)
                if 3 <= i <= NT:
                    if i == 3:
                        dve.wait_ge(s["misc_in"], 80)
                    route(dve, step, i - 3)
            def tables():
                dve.wait_ge(s["cum_done"], 1)
                step(dve.tensor_scalar(r_nb_i, ps[5][:, 0:EXP], float(P - 1), None, ALU.add))
                step(dve.tensor_scalar(r_nb_i, r_nb_i, 7, None, ALU.logical_shift_right))
                step(dve.tensor_scalar(r_nb, r_nb_i, 1.0, None, ALU.max))
                step(dve.tensor_tensor_scan(r_end, ones[:, 0:EXP], r_nb, 0.0, ALU.mult, ALU.add))
                step(dve.tensor_scalar(r_le, r_end, cst[:, C_PID:C_PID + 1], None, ALU.is_le))
                step(dve.tensor_reduce(r_eb, r_le, AX, ALU.add))
                dve.tensor_scalar(r_eb, r_eb, float(EXP - 1), None, ALU.min).then_inc(s["tab_ready"], 1)
                dve.tensor_copy(end_i[:, :], r_end).then_inc(s["tab_ready"], 1)
                step(dve.tensor_tensor(r_start, r_end, r_nb, ALU.subtract))
                step(dve.tensor_scalar(r_start, r_start, float(P), 1.0, ALU.mult, ALU.add))
                key3 = slot_key.rearrange("p (t e) -> p t e", t=NT)
                step(dve.tensor_tensor(key3, ps[4][:, :].rearrange("p (t e) -> p t e", t=NT), r_start.unsqueeze(1).to_broadcast([P, NT, EXP]), ALU.add))
                step(dve.tensor_tensor(slot_key, slot_key, sel, ALU.mult))
                step(dve.tensor_scalar(slot_key, slot_key, -1.0, None, ALU.add))

            def block_table():
                dve.wait_ge(s["blk_done"], 1)
                dve.tensor_copy(blk_i[0:1, 0:MAXBLK], ps[5][0:1, P:P + MAXBLK]).then_inc(s["tab_ready"], 1)
                dve.wait_ge(s["tab_ready"], 3)

            for t in range(NT + 1):
                if t < NT:
                    dve.wait_ge(s["shs_ready"], t + 1)
                    if t >= 2:
                        dve.wait_ge(s["shT_done"], t - 1)
                    dve.tensor_tensor(hs2[t % 2].rearrange("p (k q) -> p q k", k=KF), ps[t % 2][:, F:2 * F].rearrange("p (q k) -> p q k", k=KF),
                                      silu2[t % 2].rearrange("p (q k) -> p q k", k=KF), ALU.mult).then_inc(s["shh_ready"], 1)
                if t < 2:
                    route(dve, step, NT - 2 + t)
                if t == 3:
                    tables()
                if t == 4:
                    block_table()
                    dve.wait_ge(s["iota_ready"], 1)
                    one_hot(dve, 0, 0)
                    one_hot(dve, 1, 1)
                if t == NT:
                    dve.wait_ge(s["sh_done"], NT)
                    first_block(dve, 0, 0, None, split_lo, range(PIECES))
                if t >= 5:
                    slot_rows(dve, t - 5, t - 5)
                    if t < NT:
                        one_hot(dve, t - 3, (t - 3) % 2)
                if t >= 1:
                    j = t - 1
                    for n in range(2):
                        dve.wait_ge(s["shd_done"], 2 * j + n + 1)
                        dve.tensor_tensor(x2[:, j, 512 * n:512 * n + 512], ps[2 + n][:, :], x2[:, j, 512 * n:512 * n + 512], ALU.add
                                          ).then_inc(s["acc_ready"], 1)
            nblk = dve.value_load(end_i[0:1, EXP - 1:EXP], min_val=0, max_val=MAXBLK)
            dve.sem_inc(s["hs_ready"], 1)
            dve.sem_inc(s["y_evD"], 1)
            copy_xT_dve(dve, 0, 0)
            e1 = expert_of(dve, 1)
            first_block(dve, 1, e1, 0, split_lo, range(PIECES))
            copy_xT_dve(dve, 1, 1)
            weigh(dve, 0, 0)
            first_block(dve, 2, expert_of(dve, 2), e1, split_lo, range(PIECES))

            def body(b, u):
                weigh(dve, b + 1, (u + 1) % 4)
                slot_rows(dve, b + 4, u)
                copy_xT_dve(dve, b + 2, u % 2)
                one_hot(dve, b + 5, (u + 1) % 2)
                e, e_before = expert_of(dve, b + 3), expert_of(dve, b + 2)
                dve.wait_ge(s["y_done"], b + 1)
                if not (isinstance(b, int) and b < 2):
                    dve.wait_ge(s["y_out"], 16 * b - 16)
                dve.tensor_copy(y_sb[u % 2][:, 512:1024], ps[5][:, :]).then_inc(s["y_evD"], 1)
                first_block(dve, b + 3, e, e_before, split_lo, range(PIECES))

            all_blocks(dve, nblk, body)


def _constants():
    p = np.arange(P)
    c = np.zeros((P, C_END), np.float32)
    c[:, C_ID:C_ID + P] = np.eye(P)
    c[:, C_TRI:C_TRI + P] = p[:, None] < p[None, :]
    c[:, C_ONE:C_ONE + P] = 1.0
    c[:, C_IOTA:C_IOTA + P] = p[None, :]
    q = p % GRID_W
    start = np.clip(q - WIN_W // 2, 0, GRID_W - WIN_W)
    col = np.arange(GRID_W)[None, :]
    c[:, C_MASK:C_MASK + GRID_W] = (col >= start[:, None]) & (col < start[:, None] + WIN_W)
    t = np.arange(NT)[None, :]
    c[:, C_ROW:C_ROW + NT] = P * t + p[:, None] - BIG
    c[:, C_EMPTY] = T + p
    c[:, C_EPS] = EPS
    c[:, C_PID] = p
    c[:, C_BASE:C_BASE + MAXBLK + 8] = P * np.arange(MAXBLK + 8)[None, :]
    return c


def kernel(x, norm_mix_g, w_in, q_norm_g, k_norm_g, rpb, conv_dw_w, conv_dw_b, conv_ln_g, conv_ln_b, w_conv_out,
           w_attn_out, w_o, norm_ffn_g, w_router, router_bias, w_exp_gate, w_exp_up, w_exp_down, w_sh_gate, w_sh_up, w_sh_down):
    import concourse.bacc as bacc
    from concourse.bass_utils import run_bass_kernel_spmd

    def chan(v):
        return np.asarray(v).reshape(NC, P, -1).transpose(1, 0, 2).reshape(P, -1)

    small = np.concatenate([chan(np.asarray(conv_dw_w)[0, :, 0, :].T), chan(conv_dw_b[0]), chan(conv_ln_g[0]), chan(conv_ln_b[0]),
                            np.tile(np.asarray(q_norm_g)[0], 2)[:, None], np.tile(np.asarray(k_norm_g)[0], 2)[:, None]], axis=1)
    rpb_rev = np.pad(np.asarray(rpb)[0, :, :, ::-1].reshape(-1), RPB_PAD)
    arrays = {
        "x": np.asarray(x)[0], "w_in": np.asarray(w_in)[0], "w_conv_out": np.asarray(w_conv_out)[0],
        "w_attn_out": np.asarray(w_attn_out)[0], "w_o": np.asarray(w_o)[0], "w_router": np.asarray(w_router)[0],
        "w_gate": np.asarray(w_exp_gate)[0], "w_up": np.asarray(w_exp_up)[0], "w_down": np.asarray(w_exp_down)[0],
        "w_sh_gate": np.asarray(w_sh_gate)[0], "w_sh_up": np.asarray(w_sh_up)[0], "w_sh_down": np.asarray(w_sh_down)[0],
        "mix_g": np.asarray(norm_mix_g)[0], "ffn_g": np.asarray(norm_ffn_g)[0], "router_bias": np.asarray(router_bias)[0],
        "rpb_rev": rpb_rev, "small": small, "consts": _constants(),
    }
    arrays = {k: np.ascontiguousarray(v) for k, v in arrays.items()}
    nc = bacc.Bacc("TRN2", target_bir_lowering=False, num_devices=1)
    args = [nc.dram_tensor(k, v.shape, mybir.dt.from_np(v.dtype), kind="ExternalInput").ap() for k, v in arrays.items()]
    out = nc.dram_tensor("out", (T + P, D), F32, kind="ExternalOutput").ap()
    build(nc, *args, out)
    r = run_bass_kernel_spmd(nc, [arrays], core_ids=[0])
    return r.results[0]["out"][:T].reshape(1, T, D)
```
